# Optimizing a Trainium2 kernel written in Bass

```python
import jax, jax.numpy as jnp
from jax import lax
import numpy as np

D_MODEL = 1024
BATCH = 1
SEQ = 256
DEPTH = 1
DEC_BATCH = 1
DEC_SEQ = 2048
PAST_LEN = 512

GRID_W = 64
H_RET = 4
HD_RET = 128
W_RET = H_RET * HD_RET
H_ML = 4
HD_ML = 128
W_ML = H_ML * HD_ML
MIX_W = W_RET + W_ML
N_DIR = 2
IN_COLS = 4 * W_RET + 4 * W_ML + 2 * N_DIR * H_ML
D_FF = 4 * D_MODEL
CHUNK = 128
CONV_W = 3
EPS = 1e-6
ROPE_BASE = 10000.0
F32 = jnp.float32

kernel_name = 'bidir_retention_mlstm_hybrid_dit_step'

def rms_norm(x, g):
    xf = x.astype(F32)
    y = xf * lax.rsqrt(jnp.mean(xf * xf, -1, keepdims=True) + EPS)
    return (y * g.astype(F32)).astype(x.dtype)

def group_norm(h, g):
    hf = h.astype(F32)
    mu = jnp.mean(hf, -1, keepdims=True)
    var = jnp.mean(jnp.square(hf - mu), -1, keepdims=True)
    y = (hf - mu) * lax.rsqrt(var + EPS)
    B, T, H, D = h.shape
    return y.reshape(B, T, H * D) * g.astype(F32)

def axial_rope(x):
    T, D = x.shape[1], x.shape[-1]
    rows = T // GRID_W
    row = jnp.repeat(jnp.arange(rows), GRID_W).astype(F32)
    col = jnp.tile(jnp.arange(GRID_W), rows).astype(F32)
    nf = D // 4
    inv = ROPE_BASE ** (-jnp.arange(nf, dtype=F32) / nf)
    ang = jnp.concatenate([row[:, None] * inv, col[:, None] * inv], -1)
    cos = jnp.cos(ang)[None, :, None, :]
    sin = jnp.sin(ang)[None, :, None, :]
    xf = x.astype(F32)
    x1, x2 = xf[..., :D // 2], xf[..., D // 2:]
    return jnp.concatenate([x1 * cos - x2 * sin, x1 * sin + x2 * cos], -1)

def centred_conv(x, w):
    pad = CONV_W // 2
    T = x.shape[1]
    xp = jnp.pad(x, ((0, 0), (pad, pad), (0, 0)))
    out = xp[:, 0:T] * w[0]
    for j in range(1, CONV_W):
        out = out + xp[:, j:j + T] * w[j]
    return out

def to_chunks(a):
    B, H, T = a.shape[:3]
    n = T // CHUNK
    a = a.reshape((B, H, n, CHUNK) + a.shape[3:])
    return jnp.moveaxis(a, 2, 0)

def from_chunks(a):
    n, B, H, L, D = a.shape
    return jnp.moveaxis(a, 0, 2).reshape(B, H, n * L, D)

def retention_scan(q, k, v, log_gamma, s0):
    idx = jnp.arange(CHUNK, dtype=F32)
    lg = log_gamma.astype(F32)[:, None]
    diff = idx[:, None] - idx[None, :]
    mask = diff >= 0
    intra = jnp.where(mask, jnp.exp(lg[:, :, None] * jnp.where(mask, diff, 0.0)), 0.0)
    inter = jnp.exp(lg * (idx + 1.0))
    to_end = jnp.exp(lg * (CHUNK - 1.0 - idx))
    chunk_decay = jnp.exp(lg[:, 0] * CHUNK)

    def step(s, xs):
        qi, ki, vi = xs
        sc = jnp.einsum('bhtd,bhsd->bhts', qi, ki) * intra
        o = jnp.einsum('bhts,bhse->bhte', sc, vi) + jnp.einsum('bhtd,bhde->bhte', qi, s) * inter[..., None]
        s_new = s * chunk_decay[:, None, None] + jnp.einsum('bhsd,bhse->bhde', ki * to_end[..., None], vi)
        return s_new, o

    s_fin, oc = lax.scan(step, s0.astype(F32), (to_chunks(q), to_chunks(k), to_chunks(v)))
    return from_chunks(oc), s_fin

def mlstm_scan(q, k, v, log_i, log_f, C0, n0, m0):
    causal = jnp.tril(jnp.ones((CHUNK, CHUNK), bool))

    def step(carry, xs):
        C, nv, m = carry
        qi, ki, vi, li, lf = xs
        b = jnp.cumsum(lf, -1)
        log_inter = b + m[..., None]
        log_intra = jnp.where(causal, b[..., :, None] - b[..., None, :] + li[..., None, :], -jnp.inf)
        m_t = jnp.maximum(log_inter, jnp.max(log_intra, -1))
        w_inter = jnp.exp(log_inter - m_t)
        w_intra = jnp.exp(log_intra - m_t[..., None])
        sc = jnp.einsum('bhtd,bhsd->bhts', qi, ki) * w_intra
        num = jnp.einsum('bhts,bhse->bhte', sc, vi) + jnp.einsum('bhtd,bhde->bhte', qi, C) * w_inter[..., None]
        den = jnp.sum(sc, -1) + jnp.einsum('bhtd,bhd->bht', qi, nv) * w_inter
        h = num / jnp.maximum(jnp.abs(den), jnp.exp(-m_t))[..., None]
        b_end = b[..., -1]
        log_w_end = b_end[..., None] - b + li
        m_new = jnp.maximum(b_end + m, jnp.max(log_w_end, -1))
        decay = jnp.exp(b_end + m - m_new)
        w_end = jnp.exp(log_w_end - m_new[..., None])
        C_new = C * decay[..., None, None] + jnp.einsum('bhs,bhsd,bhse->bhde', w_end, ki, vi)
        n_new = nv * decay[..., None] + jnp.einsum('bhs,bhsd->bhd', w_end, ki)
        return (C_new, n_new, m_new), h

    xs = (to_chunks(q), to_chunks(k), to_chunks(v), to_chunks(log_i), to_chunks(log_f))
    (C_f, n_f, m_f), hc = lax.scan(step, (C0.astype(F32), n0.astype(F32), m0.astype(F32)), xs)
    return from_chunks(hc), C_f, n_f, m_f

def flip_t(a):
    return jnp.flip(a, axis=2)

def mixer(h, init, latent, w_in, conv_w, ret_decay_logit, mlstm_gate_bias, ret_gn_g, mlstm_gn_g, w_out):
    B, T, _ = h.shape
    s_ret0, C0, n0, m0 = init
    proj = h @ w_in
    cuts = [W_RET, 2 * W_RET, 3 * W_RET, 4 * W_RET, 4 * W_RET + 2 * W_ML, 4 * W_RET + 3 * W_ML, 4 * W_RET + 4 * W_ML]
    rq, rk, rv, rg, mqk, mv, mo, mgate = jnp.split(proj, cuts, axis=-1)

    rq = rq.reshape(B, T, H_RET, HD_RET)
    rk = rk.reshape(B, T, H_RET, HD_RET) * (HD_RET ** -0.5)
    if latent:
        rq, rk = axial_rope(rq), axial_rope(rk)
    q = jnp.transpose(rq.astype(F32), (0, 2, 1, 3))
    k = jnp.transpose(rk.astype(F32), (0, 2, 1, 3))
    v = jnp.transpose(rv.reshape(B, T, H_RET, HD_RET).astype(F32), (0, 2, 1, 3))
    log_gamma = jax.nn.log_sigmoid(ret_decay_logit.astype(F32))
    o_f, s_f = retention_scan(q, k, v, log_gamma[0], s_ret0[:, 0])
    o_b, s_b = retention_scan(flip_t(q), flip_t(k), flip_t(v), log_gamma[1], s_ret0[:, 1])
    o_ret = o_f + flip_t(o_b)
    ret_y = group_norm(jnp.transpose(o_ret, (0, 2, 1, 3)), ret_gn_g) * jax.nn.silu(rg.astype(F32))

    mqk = jax.nn.silu(centred_conv(mqk, conv_w))
    mq, mk = jnp.split(mqk, 2, axis=-1)
    q = jnp.transpose(mq.reshape(B, T, H_ML, HD_ML).astype(F32), (0, 2, 1, 3))
    k = jnp.transpose(mk.reshape(B, T, H_ML, HD_ML).astype(F32), (0, 2, 1, 3)) * (HD_ML ** -0.5)
    v = jnp.transpose(mv.reshape(B, T, H_ML, HD_ML).astype(F32), (0, 2, 1, 3))
    gates = mgate.astype(F32).reshape(B, T, N_DIR, 2, H_ML) + mlstm_gate_bias.astype(F32)
    gates = jnp.transpose(gates, (2, 3, 0, 4, 1))
    log_i = gates[:, 0]
    log_f = jax.nn.log_sigmoid(gates[:, 1])
    h_f, C_f, n_f, m_f = mlstm_scan(q, k, v, log_i[0], log_f[0], C0[:, 0], n0[:, 0], m0[:, 0])
    h_b, C_b, n_b, m_b = mlstm_scan(flip_t(q), flip_t(k), flip_t(v), flip_t(log_i[1]), flip_t(log_f[1]),
                                    C0[:, 1], n0[:, 1], m0[:, 1])
    h_ml = h_f + flip_t(h_b)
    ml_y = group_norm(jnp.transpose(h_ml, (0, 2, 1, 3)), mlstm_gn_g) * jax.nn.sigmoid(mo.astype(F32))

    out = jnp.concatenate([ret_y, ml_y], -1).astype(h.dtype) @ w_out
    new_state = (jnp.stack([s_f, s_b], 1), jnp.stack([C_f, C_b], 1),
                 jnp.stack([n_f, n_b], 1), jnp.stack([m_f, m_b], 1))
    return out, new_state

def layer(x, cond, init, latent, w_ada, b_ada, norm1_g, norm2_g, w_in, conv_w, ret_decay_logit,
          mlstm_gate_bias, ret_gn_g, mlstm_gn_g, w_out, w_ff1, w_ff2):
    mod = (jax.nn.silu(cond) @ w_ada + b_ada)[:, None, :]
    sh1, sc1, g1, sh2, sc2, g2 = jnp.split(mod, 6, axis=-1)
    h = rms_norm(x, norm1_g) * (1 + sc1) + sh1
    a, st = mixer(h, init, latent, w_in, conv_w, ret_decay_logit, mlstm_gate_bias, ret_gn_g, mlstm_gn_g, w_out)
    x = x + g1 * a
    h = rms_norm(x, norm2_g) * (1 + sc2) + sh2
    f = jnp.square(jax.nn.relu(h @ w_ff1)) @ w_ff2
    x = x + g2 * f
    return x, st

def setup_inputs(seed: int = 0) -> dict:
    key = jax.random.key(seed)
    ks = jax.random.split(key, 26)

    def nrm(k, shape, s):
        return jax.random.normal(k, shape, F32) * s

    hidx = jnp.arange(H_RET, dtype=F32)
    gam = 1.0 - 2.0 ** (-5.0 - hidx)
    base_logit = jnp.log(gam) - jnp.log1p(-gam)
    f_bias = jnp.linspace(3.0, 6.0, H_ML, dtype=F32)
    i_b = nrm(ks[16], (DEPTH, N_DIR, 1, H_ML), 0.1)
    f_b = f_bias + nrm(ks[17], (DEPTH, N_DIR, 1, H_ML), 0.1)
    return {
        'x_prompt': nrm(ks[0], (BATCH, SEQ, D_MODEL), 1.0),
        'x_sample': nrm(ks[1], (DEC_BATCH, DEC_SEQ, D_MODEL), 1.0),
        'state_ret': nrm(ks[2], (DEC_BATCH, DEPTH, N_DIR, H_RET, HD_RET, HD_RET), 0.5),
        'state_mlstm_C': nrm(ks[3], (DEC_BATCH, DEPTH, N_DIR, H_ML, HD_ML, HD_ML), 0.5),
        'state_mlstm_n': nrm(ks[4], (DEC_BATCH, DEPTH, N_DIR, H_ML, HD_ML), 0.5),
        'state_mlstm_m': nrm(ks[5], (DEC_BATCH, DEPTH, N_DIR, H_ML), 0.5),
        'c': nrm(ks[6], (DEC_BATCH, D_MODEL), 1.0),
        'c_ctx': nrm(ks[7], (D_MODEL,), 1.0),
        'w_ada': nrm(ks[8], (DEPTH, D_MODEL, 6 * D_MODEL), 0.5 * D_MODEL ** -0.5),
        'b_ada': nrm(ks[9], (DEPTH, 6 * D_MODEL), 0.1),
        'norm1_g': 1.0 + nrm(ks[10], (DEPTH, D_MODEL), 0.05),
        'norm2_g': 1.0 + nrm(ks[11], (DEPTH, D_MODEL), 0.05),
        'w_in': nrm(ks[12], (DEPTH, D_MODEL, IN_COLS), D_MODEL ** -0.5),
        'conv_w': nrm(ks[13], (DEPTH, CONV_W, 2 * W_ML), CONV_W ** -0.5),
        'ret_decay_logit': base_logit + nrm(ks[14], (DEPTH, N_DIR, H_RET), 0.1),
        'mlstm_gate_bias': jnp.concatenate([i_b, f_b], axis=2),
        'ret_gn_g': 1.0 + nrm(ks[18], (DEPTH, W_RET), 0.05),
        'mlstm_gn_g': 1.0 + nrm(ks[19], (DEPTH, W_ML), 0.05),
        'w_out': nrm(ks[20], (DEPTH, MIX_W, D_MODEL), MIX_W ** -0.5),
        'w_ff1': nrm(ks[21], (DEPTH, D_MODEL, D_FF), D_MODEL ** -0.5),
        'w_ff2': nrm(ks[22], (DEPTH, D_FF, D_MODEL), D_FF ** -0.5),
        'final_g': 1.0 + nrm(ks[23], (D_MODEL,), 0.05),
    }

def reference(x_prompt, x_sample, state_ret, state_mlstm_C, state_mlstm_n, state_mlstm_m, c, c_ctx,
              w_ada, b_ada, norm1_g, norm2_g, w_in, conv_w, ret_decay_logit, mlstm_gate_bias,
              ret_gn_g, mlstm_gn_g, w_out, w_ff1, w_ff2, final_g):
    Bp = x_prompt.shape[0]
    ctx_cond = jnp.broadcast_to(c_ctx, (Bp, D_MODEL))
    zero_init = (jnp.zeros((Bp, N_DIR, H_RET, HD_RET, HD_RET), F32),
                 jnp.zeros((Bp, N_DIR, H_ML, HD_ML, HD_ML), F32),
                 jnp.zeros((Bp, N_DIR, H_ML, HD_ML), F32),
                 jnp.zeros((Bp, N_DIR, H_ML), F32))
    xp, xs = x_prompt, x_sample
    new_ret, new_C, new_n, new_m = [], [], [], []
    for l in range(DEPTH):
        lw = (w_ada[l], b_ada[l], norm1_g[l], norm2_g[l], w_in[l], conv_w[l], ret_decay_logit[l],
              mlstm_gate_bias[l], ret_gn_g[l], mlstm_gn_g[l], w_out[l], w_ff1[l], w_ff2[l])
        xp, st = layer(xp, ctx_cond, zero_init, False, *lw)
        new_ret.append(st[0]); new_C.append(st[1]); new_n.append(st[2]); new_m.append(st[3])
        cache = (state_ret[:, l], state_mlstm_C[:, l], state_mlstm_n[:, l], state_mlstm_m[:, l])
        xs, _ = layer(xs, c, cache, True, *lw)
    y_prompt = rms_norm(xp, final_g)
    y_sample = rms_norm(xs, final_g)
    return (y_prompt, y_sample, jnp.stack(new_ret, 1), jnp.stack(new_C, 1), jnp.stack(new_n, 1), jnp.stack(new_m, 1))


_drawn_inputs = setup_inputs


def setup_inputs(seed=0):
    import zlib

    import numpy as np

    out = dict(_drawn_inputs(seed))
    spreads = {}
    factors = {'state_ret': 4.597,
     'state_mlstm_C': 4.732,
     'state_mlstm_n': 8.0,
     'state_mlstm_m': 8.0,
     'ret_gn_g': 8.0,
     'mlstm_gn_g': 8.0,
     'norm2_g': 4.447}
    for name, (base, spread) in spreads.items():
        noise = np.random.default_rng([zlib.crc32(name.encode()), seed]).standard_normal(out[name].shape)
        drawn = base * np.exp(spread * noise) if base else spread * noise
        out[name] = __import__('jax').numpy.asarray(drawn.astype(out[name].dtype))
    for name, factor in factors.items():
        out[name] = (out[name] * factor).astype(out[name].dtype)
    return out
```

```python
from contextlib import ExitStack

import concourse.bass as bass
from concourse import mybir

ALU = mybir.AluOpType
ACT = mybir.ActivationFunctionType
F32 = mybir.dt.float32
AX_X = mybir.AxisListType.X

P = 128
D = 1024
KT = D // P
HEADS = 4
HD = 128
W = HEADS * HD
AUG = HD + 1
CTX = 256
LAT = 2048
CTX_TILES = CTX // P
TILES = (CTX + LAT) // P
PAIRS = TILES // 2
TOKENS = CTX + LAT
FF = 4 * D
FF_CHUNKS = FF // P
BLK = 512
MOD = 6 * D
EPS = 1e-6
KSCALE = HD ** -0.5
STATE = W + HEADS * AUG
U, EN, WE, MX, WI = range(5)
ROWS = 8
FAR = 1e30


def over_tiles(engine, body):
    for j in range(2):
        body(0, j, 0)
    with engine.Fori(1, PAIRS) as pair:
        for j in range(2):
            body(pair, j, 1)


def build(nc, a, out):
    with ExitStack() as ctx:
        def dram(name, shape):
            return nc.dram_tensor(name, shape, F32).ap()

        s = {
            "mod": dram("mod_rows", [2, MOD]),
            "qkv": dram("qkv_rows", [TOKENS, 4 * W]),
            "mqk": dram("mqk_rows", [TOKENS + 4, 2 * W]),
            "mqk2": dram("conv_rows", [TOKENS, 2 * W]),
            "gate": dram("gate_rows_out", [TOKENS, D]),
            "rows": dram("scalar_rows", [5 * ROWS, TOKENS]),
            "mdec": dram("backward_decays", [TILES, HEADS]),
            "bst": dram("backward_states", [TILES, P, STATE]),
            "y": dram("mixed_rows", [TOKENS, D]),
            "x1": dram("residual_rows", [TOKENS, D]),
            "h2T": dram("mlp_in", [P, KT, TOKENS]),
        }
        ident = ctx.enter_context(nc.sbuf_tensor("ident", [P, P], F32))
        with ExitStack() as c2:
            def sb(name, shape):
                return c2.enter_context(nc.sbuf_tensor(name, shape, F32))

            keep = {
                "ident": ident,
                "grows": sb("grows", [P, TOKENS]),
                "mret": sb("mret", [P, HEADS, P]),
                "qdec": sb("qdec", [P, 2, HEADS, P]),
                "kdec": sb("kdec", [P, 8]),
                "cdec": sb("cdec", [P, 8]),
            }
            modulation(nc, a, s, keep)
            projection(nc, a, s, keep)
            gate_rows(nc, a, s, keep, out)
            backward_scan(nc, a, s, keep, out)
            forward_scan(nc, a, s, keep, out)
        keep = {"ident": ident}
        output(nc, a, s, keep)
        mlp(nc, a, s, keep, out)


class Scope:

    def __init__(self, nc, ctx, name):
        self.nc, self.ctx, self.name, self.sems = nc, ctx, name, []
        ctx.callback(self.close)

    def sb(self, name, shape):
        return self.ctx.enter_context(self.nc.sbuf_tensor(f"{self.name}_{name}", shape, F32))

    def ps(self, name, shape):
        return self.ctx.enter_context(self.nc.psum_tensor(f"{self.name}_{name}", shape, F32))

    def sem(self, name):
        self.sems.append(self.nc.alloc_semaphore(name=f"{self.name}_{name}"))
        return self.sems[-1]

    def close(self):
        self.nc.clear_and_free_semaphores(self.sems)
        self.nc.all_engine_barrier()


def modulation(nc, a, s, keep):
    NB = MOD // BLK
    RING = 4
    with ExitStack() as ctx:
        m = Scope(nc, ctx, "mod")
        cond = m.sb("cond", [P, 2, KT])
        sig = m.sb("sig", [P, 2, KT])
        act_c = m.sb("act", [P, 2, KT])
        w = m.sb("w", [P, RING, KT, BLK])
        bias = m.sb("bias", [2, RING, BLK])
        row = m.sb("row", [2, 2, BLK])
        acc = m.ps("acc", [P, 2, BLK])
        cond_loaded, sig_done, silu_done = m.sem("cond_loaded"), m.sem("sig_done"), m.sem("silu_done")
        w_loaded = [m.sem(f"w_loaded{j}") for j in range(RING)]
        product, row_ready = m.sem("product"), m.sem("row_ready")
        row_stored = [m.sem(f"row_stored{j}") for j in range(2)]
        ident_loaded = m.sem("ident_loaded")
        w_ada = a["w_ada"][0].rearrange("(p k) n -> p k n", k=KT)
        block = ctx.enter_context(nc.Block())

        def over_blocks(engine, body):
            for j in range(RING):
                body(0, j)
            with engine.Fori(1, NB // RING) as r:
                for j in range(RING):
                    body(r, j)

        @block.sync
        def _(sp):
            sp.dma_start(cond[:, 0, :], a["c_ctx"].rearrange("(p k) -> p k", k=KT)).then_inc(cond_loaded, 16)
            sp.dma_start(cond[:, 1, :], a["c"][0].rearrange("(p k) -> p k", k=KT)).then_inc(cond_loaded, 16)
            sp.dma_start(keep["ident"][:, :], a["ident"]).then_inc(ident_loaded, 16)

            def load(r, j):
                n = r * RING + j
                if not (isinstance(r, int) and r == 0):
                    sp.wait_ge(row_ready, n - RING + 1)
                sp.dma_start(w[:, j, :, :], w_ada[:, :, bass.ts(n, BLK)]).then_inc(w_loaded[j], 16)
                sp.dma_start(bias[:, j, :], a["b_ada"][0:1, bass.ts(n, BLK)].to_broadcast([2, BLK])
                             ).then_inc(w_loaded[j], 16)

            over_blocks(sp, load)
            sp.wait_ge(ident_loaded, 16)

        @block.scalar
        def _(act):
            act.wait_ge(cond_loaded, 32)
            act.activation(sig[:, :, :], cond[:, :, :], ACT.Sigmoid).then_inc(sig_done, 1)

        @block.tensor
        def _(pe):
            pe.wait_ge(silu_done, 1)

            def multiply(r, j):
                n = r * RING + j
                pe.wait_ge(w_loaded[j], 32 * (r + 1))
                if not (isinstance(r, int) and n < 2):
                    pe.wait_ge(row_ready, n - 1)
                for k in range(KT):
                    last = pe.matmul(acc[0:2, j % 2, :], act_c[:, :, k], w[:, j, k, :], start=(k == 0), stop=(k == KT - 1))
                last.then_inc(product, 1)

            over_blocks(pe, multiply)

        @block.vector
        def _(dve):
            dve.wait_ge(sig_done, 1)
            dve.tensor_tensor(act_c[:, :, :], cond[:, :, :], sig[:, :, :], ALU.mult).then_inc(silu_done, 1)

            def add_bias(r, j):
                n = r * RING + j
                dve.wait_ge(product, n + 1)
                if not (isinstance(r, int) and n < 2):
                    dve.wait_ge(row_stored[j % 2], 16 * (2 * r + j // 2))
                dve.tensor_tensor(row[:, j % 2, :], acc[0:2, j % 2, :], bias[:, j, :], ALU.add).then_inc(row_ready, 1)

            over_blocks(dve, add_bias)

        @block.gpsimd
        def _(pool):
            def store(r, j):
                n = r * RING + j
                pool.wait_ge(row_ready, n + 1)
                pool.dma_start(s["mod"][:, bass.ts(n, BLK)], row[:, j % 2, :]).then_inc(row_stored[j % 2], 16)

            over_blocks(pool, store)
            for j in range(2):
                pool.wait_ge(row_stored[j], 16 * NB // 2)


def load_modulation(sp, s, a, shift, scale, shift_at, scale_at, seq, loaded):
    sp.dma_start(shift[:, :], s["mod"][seq:seq + 1, shift_at * D:(shift_at + 1) * D].to_broadcast([P, D])
                 ).then_inc(loaded, 16)
    sp.dma_start(scale[:, :], s["mod"][seq:seq + 1, scale_at * D:(scale_at + 1) * D].to_broadcast([P, D])
                 ).then_inc(loaded, 16)


def projection(nc, a, s, keep):
    NB = 8
    ident = keep["ident"]
    with ExitStack() as ctx:
        m = Scope(nc, ctx, "proj")
        w = m.sb("w", [P, KT, NB * BLK])
        wg16 = m.sb("wg16", [P, KT, 16])
        wg = m.sb("wg", [P, KT, P])
        gbias = m.sb("gbias", [P, 1])
        x = m.sb("x", [P, 2, D])
        hT = m.sb("hT", [P, 2, KT, P])
        stage = m.sb("stage", [P, 4, BLK])
        pre = m.sb("pre", [P, 2, BLK])
        sig = m.sb("sig", [P, BLK])
        gnorm = m.sb("gnorm", [P, D])
        shift = m.sb("shift", [P, D])
        scale = m.sb("scale", [P, D])
        rope = m.sb("rope", [P, 2, 2, HD // 2])
        turn = m.sb("turn", [P, 2, HEADS, HD // 2])
        junk = m.sb("junk", [P, D])
        ssq = m.sb("ssq", [P, 2])
        mean = m.sb("mean", [P, 2])
        rstd = m.sb("rstd", [P, 2])
        power = m.sb("power", [P, 1])
        zrow = m.sb("zrow", [4, 2 * W])
        acc = m.ps("acc", [P, 4, BLK])
        tps = m.ps("tps", [P, KT, P])
        gps = m.ps("gps", [P, BLK])

        w_loaded = [m.sem(f"w_loaded{n}") for n in range(NB)]
        wg_loaded, gb_loaded = m.sem("wg_loaded"), m.sem("gb_loaded")
        gb_zero, wg_zero, wg_ready = m.sem("gb_zero"), m.sem("wg_zero"), m.sem("wg_ready")
        mod_loaded, gnorm_loaded = m.sem("mod_loaded"), m.sem("gnorm_loaded")
        scale_ready = m.sem("scale_ready")
        x_loaded = [m.sem(f"x_loaded{j}") for j in range(2)]
        ssq_ready, mean_ready, rstd_ready = m.sem("ssq_ready"), m.sem("mean_ready"), m.sem("rstd_ready")
        scaled, h_ready = m.sem("scaled"), m.sem("h_ready")
        transposed, hT_ready = m.sem("transposed"), m.sem("hT_ready")
        product, gate_product = m.sem("product"), m.sem("gate_product")
        act_read, gate_read, grow_ready = m.sem("act_read"), m.sem("gate_read"), m.sem("grow_ready")
        turned = m.sem("turned")
        part_done = m.sem("part_done")
        staged = [m.sem(f"staged{n}") for n in range(4)]
        stored = [m.sem(f"stored{n}") for n in range(4)]
        zero_ready, zero_stored = m.sem("zero_ready"), m.sem("zero_stored")
        w_in = a["w_in"][0].rearrange("(k p) n -> p k n", p=P)
        power_ready = m.sem("power_ready")
        block = ctx.enter_context(nc.Block())

        def first(pair):
            return isinstance(pair, int)

        @block.sync
        def _(sp):
            def load(pair, j, seq):
                t = 2 * pair + j
                if seq == 1:
                    sp.wait_ge(transposed, t - 1)
                src = a["x_sample"][0, bass.ts(t - CTX_TILES, P), :] if seq else a["x_prompt"][0, bass.ts(t, P), :]
                sp.dma_start(x[:, j, :], src).then_inc(x_loaded[j], 16)
                if seq:
                    sp.wait_ge(staged[1], t - 1)
                    sp.dma_start(rope[:, j, :, :], a["rope"][bass.ts(t - CTX_TILES, P), :, :]).then_inc(x_loaded[j], 16)

            for j in range(2):
                load(0, j, 0)
            load_modulation(sp, s, a, shift, scale, 0, 1, 0, mod_loaded)
            sp.dma_start(junk[:, :], a["norm1_g"].to_broadcast([P, D])).then_inc(mod_loaded, 16)
            sp.dma_start(wg16[:, :, :], w_in[:, :, NB * BLK:NB * BLK + 16]).then_inc(wg_loaded, 16)
            for n in range(NB):
                sp.dma_start(w[:, :, n * BLK:(n + 1) * BLK], w_in[:, :, n * BLK:(n + 1) * BLK]).then_inc(w_loaded[n], 16)
                if n == 2:
                    sp.dma_start(gnorm[:, 0:W], a["ret_gn_g"].to_broadcast([P, W])).then_inc(gnorm_loaded, 16)
                    sp.dma_start(gnorm[:, W:D], a["mlstm_gn_g"].to_broadcast([P, W])).then_inc(gnorm_loaded, 16)
            sp.wait_ge(h_ready, CTX_TILES)
            load_modulation(sp, s, a, shift, scale, 0, 1, 1, mod_loaded)
            sp.wait_ge(ssq_ready, CTX_TILES)
            sp.dma_start(junk[:, :], a["norm1_g"].to_broadcast([P, D])).then_inc(mod_loaded, 16)

            with sp.Fori(1, PAIRS) as pair:
                for j in range(2):
                    load(pair, j, 1)

        @block.scalar
        def _(act):
            def evacuate(pair, j, seq):
                t = 2 * pair + j
                act.wait_ge(x_loaded[j], 16 if seq == 0 else 16 + 32 * pair)
                act.wait_ge(scale_ready, seq + 1)
                if not first(pair) or t > 0:
                    act.wait_ge(ssq_ready, t)
                if seq or t >= 2:
                    act.wait_ge(mean_ready, t - 1)
                act.activation(junk[:, :], x[:, j, :], ACT.Square, accum_out=ssq[:, j:j + 1]).then_inc(ssq_ready, 1)
                for half in range(2):
                    act.wait_ge(transposed, t + 1)
                    if seq:
                        act.wait_ge(gate_product, t - 1)
                    act.activation(hT[:, j, 4 * half:4 * half + 4, :], tps[:, 4 * half:4 * half + 4, :], ACT.Copy
                                   ).then_inc(hT_ready, 1)
                for n in range(NB):
                    act.wait_ge(product, NB * t + n + 1)
                    slot = n % 4
                    if n in (0, 1):
                        act.wait_ge(staged[n], t)
                        act.activation(pre[:, n, :], acc[:, n, :], ACT.Copy, scale=(1.0, KSCALE)[n]).then_inc(act_read, 1)
                    elif n in (3, 7):
                        act.wait_ge(staged[3], 2 * t + n // 4)
                        act.activation(sig[:, :], acc[:, 3, :], ACT.Sigmoid).then_inc(act_read, 1)
                    else:
                        act.wait_ge(stored[slot], 16 * (2 * t + n // 4))
                        act.activation(stage[:, slot, :], acc[:, slot, :], ACT.Copy).then_inc(act_read, 1)
                act.wait_ge(gate_product, t + 1)
                act.activation(keep["grows"][:, bass.ts(t, P)], gps[:, 0:P], ACT.Identity, bias=gbias[:, 0:1]
                               ).then_inc(grow_ready, 1)

            act.wait_ge(gb_loaded, 64)
            over_tiles(act, evacuate)

        @block.tensor
        def _(pe):
            def multiply(pair, j, seq):
                t = 2 * pair + j
                pe.wait_ge(h_ready, t + 1)
                if not (first(pair) and t == 0):
                    pe.wait_ge(hT_ready, 2 * t)
                for k in range(KT):
                    last = pe.transpose(tps[:, k, :], x[:, j, k * P:(k + 1) * P], ident[:, :])
                last.then_inc(transposed, 1)
                pe.wait_ge(hT_ready, 2 * t + 2)
                for n in range(NB):
                    if seq == 0:
                        pe.wait_ge(w_loaded[n], 16)
                    if not (first(pair) and t == 0 and n < 4):
                        pe.wait_ge(act_read, NB * t + n - 3)
                        if n == 7:
                            pe.wait_ge(gate_read, t + 1)
                    for k in range(KT):
                        last = pe.matmul(acc[:, n % 4, :], hT[:, j, k, :], w[:, k, n * BLK:(n + 1) * BLK],
                                         start=(k == 0), stop=(k == KT - 1))
                    last.then_inc(product, 1)
                pe.wait_ge(wg_ready, 4)
                if not (first(pair) and t == 0):
                    pe.wait_ge(grow_ready, t)
                for k in range(KT):
                    last = pe.matmul(gps[:, 0:P], wg[:, k, :], hT[:, j, k, :], start=(k == 0), stop=(k == KT - 1))
                last.then_inc(gate_product, 1)

            over_tiles(pe, multiply)

        @block.vector
        def _(dve):
            dve.memset(wg[:, :, :], 0.0).then_inc(wg_zero, 1)
            dve.wait_ge(wg_zero, 1)
            dve.wait_ge(wg_loaded, 16)
            for d in range(2):
                for f in range(2):
                    at = 64 * f + 32 * d
                    dve.tensor_copy(wg[:, :, at:at + 4], wg16[:, :, 8 * d + 4 * f:8 * d + 4 * f + 4]).then_inc(wg_ready, 1)

            def make_scale(seq):
                dve.wait_ge(mod_loaded, 48 * (seq + 1))
                dve.scalar_tensor_tensor(out=scale[:, :], in0=scale[:, :], scalar=1.0, in1=junk[:, :],
                                         op0=ALU.add, op1=ALU.mult).then_inc(scale_ready, 1)

            def normalise(pair, j, seq):
                t = 2 * pair + j
                dve.wait_ge(ssq_ready, t + 1)
                dve.tensor_scalar(mean[:, j:j + 1], ssq[:, j:j + 1], 1.0 / D, EPS, ALU.mult, ALU.add).then_inc(mean_ready, 1)
                dve.wait_ge(rstd_ready, t + 1)
                dve.wait_ge(scale_ready, seq + 1)
                dve.scalar_tensor_tensor(out=x[:, j, :], in0=x[:, j, :], scalar=rstd[:, j:j + 1], in1=scale[:, :],
                                         op0=ALU.mult, op1=ALU.mult).then_inc(scaled, 1)
                dve.wait_ge(scaled, t + 1)
                dve.tensor_tensor(x[:, j, :], x[:, j, :], shift[:, :], ALU.add).then_inc(h_ready, 1)

            def finish(pair, j, seq):
                t = 2 * pair + j
                for n in range(NB):
                    slot = n % 4
                    if n in (0, 1) and not seq:
                        dve.wait_ge(act_read, NB * t + n + 1)
                        dve.wait_ge(stored[slot], 32 * t)
                        dve.tensor_copy(stage[:, n, :], pre[:, n, :]).then_inc(staged[n], 1)
                    elif n in (0, 1):
                        dve.wait_ge(act_read, NB * t + n + 1)
                        dve.wait_ge(stored[slot], 32 * t)
                        v = pre[:, n, :].rearrange("p (h b e) -> p h b e", h=HEADS, b=2)
                        o = stage[:, n, :].rearrange("p (h b e) -> p h b e", h=HEADS, b=2)
                        cos = rope[:, j, 0:1, :].to_broadcast([P, HEADS, HD // 2])
                        sin = rope[:, j, 1:2, :].to_broadcast([P, HEADS, HD // 2])
                        at = 4 * (2 * (t - CTX_TILES) + n)
                        for b in range(2):
                            one, two = (cos, sin) if b == 0 else (sin, cos)
                            if b == 0:
                                dve.wait_ge(staged[1 - n], t + n)
                            dve.tensor_tensor(turn[:, 0, :, :], v[:, :, 0, :], one, ALU.mult).then_inc(turned, 1)
                            dve.tensor_tensor(turn[:, 1, :, :], v[:, :, 1, :], two, ALU.mult).then_inc(turned, 1)
                            dve.wait_ge(turned, at + 2 * b + 2)
                            done = dve.tensor_tensor(o[:, :, b, :], turn[:, 0, :, :], turn[:, 1, :, :],
                                                     ALU.subtract if b == 0 else ALU.add)
                            if b == 0:
                                done.then_inc(part_done, 1)
                                dve.wait_ge(part_done, 2 * (t - CTX_TILES) + n + 1)
                            else:
                                done.then_inc(staged[slot], 1)
                    elif n in (3, 7):
                        dve.wait_ge(act_read, NB * t + n + 1)
                        if n == 3 and seq == 0:
                            dve.wait_ge(gnorm_loaded, 32)
                        half = gnorm[:, 0:W] if n == 3 else gnorm[:, W:D]
                        dve.wait_ge(stored[3], 16 * (2 * t + n // 4))
                        if n == 3:
                            dve.tensor_tensor(stage[:, 3, :], acc[:, 3, :], sig[:, :], ALU.mult).then_inc(gate_read, 1)
                            dve.wait_ge(gate_read, t + 1)
                            dve.tensor_tensor(stage[:, 3, :], stage[:, 3, :], half, ALU.mult).then_inc(staged[3], 1)
                        else:
                            dve.tensor_tensor(stage[:, 3, :], sig[:, :], half, ALU.mult).then_inc(staged[3], 1)

            make_scale(0)
            for j in range(2):
                normalise(0, j, 0)
                finish(0, j, 0)
            make_scale(1)
            with dve.Fori(1, PAIRS) as pair:
                for j in range(2):
                    normalise(pair, j, 1)
                    finish(pair, j, 1)

        @block.gpsimd
        def _(pool):
            pool.memset(power[:, :], -0.5).then_inc(power_ready, 1)
            pool.wait_ge(power_ready, 1)
            pool.memset(gbias[:, :], 0.0).then_inc(gb_zero, 1)
            pool.memset(zrow[:, :], 0.0).then_inc(zero_ready, 1)
            pool.wait_ge(gb_zero, 1)
            for d in range(2):
                for f in range(2):
                    at = 64 * f + 32 * d
                    pool.dma_start(gbias[at:at + 4, :], a["mlstm_gate_bias"][0, d, f, :].rearrange("(h o) -> h o", o=1)
                                   ).then_inc(gb_loaded, 16)
            pool.wait_ge(zero_ready, 1)
            pool.dma_start(s["mqk"][0:1, :], zrow[0:1, :]).then_inc(zero_stored, 16)
            pool.dma_start(s["mqk"][CTX + 1:CTX + 3, :], zrow[1:3, :]).then_inc(zero_stored, 16)
            pool.dma_start(s["mqk"][TOKENS + 3:TOKENS + 4, :], zrow[3:4, :]).then_inc(zero_stored, 16)

            def store(pair, j, seq):
                t = 2 * pair + j
                pool.wait_ge(mean_ready, t + 1)
                pool.tensor_tensor(rstd[:, j:j + 1], mean[:, j:j + 1], power[:, 0:1], ALU.pow).then_inc(rstd_ready, 1)
                for n in range(NB):
                    slot = n % 4
                    rows = bass.ts(t, P)
                    if n < 3:
                        dst = s["qkv"][rows, n * W:(n + 1) * W]
                    elif n == 6:
                        dst = s["qkv"][rows, 3 * W:4 * W]
                    elif n in (3, 7):
                        dst = s["gate"][rows, (n // 4) * W:(n // 4 + 1) * W]
                    else:
                        dst = s["mqk"][bass.ds(t * P + 1 + 2 * seq, P), (n - 4) * W:(n - 3) * W]
                    if slot == 3:
                        pool.wait_ge(staged[3], 2 * t + n // 4 + 1)
                    elif n < 2:
                        pool.wait_ge(staged[n], t + 1)
                    else:
                        pool.wait_ge(act_read, NB * t + n + 1)
                    pool.dma_start(dst, stage[:, slot, :]).then_inc(stored[slot], 16)

            over_tiles(pool, store)
            pool.wait_ge(zero_stored, 48)
            for slot in range(4):
                pool.wait_ge(stored[slot], 32 * TILES)


def gate_rows(nc, a, s, keep, out):
    G = 64
    grows = keep["grows"]
    with ExitStack() as ctx:
        m = Scope(nc, ctx, "gates")
        absf = m.sb("absf", [G, TOKENS])
        logf = m.sb("logf", [G, TILES, P])
        logi = m.sb("logi", [G, TILES, P])
        ping = m.sb("ping", [G, TILES, P])
        pong = m.sb("pong", [G, TILES, P])
        cum_b = m.sb("cum_b", [G, TILES, P])
        u = m.sb("u", [G, TILES, P])
        final = m.sb("final", [G, 4, TILES, P])
        ends = m.sb("ends", [G, 2, TILES])
        m_in = m.sb("m_in", [G, TILES + 1])
        m_ctx = m.sb("m_ctx", [G, 1])
        m_chunk = m.sb("m_chunk", [G, TILES])
        logit = m.sb("logit", [P, 8])
        decay_abs = m.sb("decay_abs", [P, 8])
        decay_min = m.sb("decay_min", [P, 8])
        shapes = m.sb("shapes", [P, 6, P])
        cols = m.sb("cols", [P, 2])
        tables = m.sb("tables", [P, 2, HEADS, P])
        loaded, m_zero, m_loaded = m.sem("loaded"), m.sem("m_zero"), m.sem("m_loaded")
        act_step, dve_step = m.sem("act_step"), m.sem("dve_step")
        stored = m.sem("stored")
        block = ctx.enter_context(nc.Block())
        F0, B0 = slice(0, 32), slice(32, 64)
        DV_LG = 2
        DV_LOGF = 5
        DV_CUM = DV_LOGF + 2 * 7
        DV_U = DV_CUM + 2
        DV_MAX = DV_U + 2 * 7
        DV_MPREV = DV_MAX + 4 + TILES + 2
        DV_FINAL = DV_MPREV + 4


        @block.sync
        def _(sp):
            sp.dma_start(logit[:, :], a["ret_decay_logit"].rearrange("o d h -> o (d h)").to_broadcast([P, 8])
                         ).then_inc(loaded, 16)
            sp.dma_start(shapes[:, :, :], a["shapes"]).then_inc(loaded, 16)
            sp.dma_start(cols[:, :], a["cols"]).then_inc(loaded, 16)
            sp.wait_ge(m_zero, 1)
            for d in range(2):
                sp.dma_start(m_in[32 * d:32 * d + 4, CTX_TILES:CTX_TILES + 1],
                             a["state_mlstm_m"][0, 0, d, :].rearrange("(h o) -> h o", o=1)).then_inc(m_loaded, 16)

        @block.scalar
        def _(act):
            fr = grows[64:128, :]
            act.activation(absf[:, :], fr, ACT.Abs).then_inc(act_step, 1)
            act.wait_ge(act_step, 1)
            act.activation(absf[:, :], absf[:, :], ACT.Exp, scale=-1.0).then_inc(act_step, 1)
            act.wait_ge(act_step, 2)
            act.activation(absf[:, :], absf[:, :], ACT.Ln, bias=1.0).then_inc(act_step, 1)
            act.wait_ge(loaded, 48)
            act.activation(decay_abs[:, :], logit[:, :], ACT.Abs).then_inc(act_step, 1)
            act.wait_ge(act_step, 4)
            act.activation(decay_abs[:, :], decay_abs[:, :], ACT.Exp, scale=-1.0).then_inc(act_step, 1)
            act.wait_ge(act_step, 5)
            act.activation(decay_abs[:, :], decay_abs[:, :], ACT.Ln, bias=1.0).then_inc(act_step, 1)
            lg = decay_min
            act.wait_ge(dve_step, DV_LG)
            for d in range(2):
                for h in range(HEADS):
                    g = lg[:, 4 * d + h:4 * d + h + 1]
                    act.activation(tables[:, d, h, :], shapes[:, d, :], ACT.Exp, scale=g).then_inc(act_step, 1)
                    act.activation(keep["qdec"][:, d, h, :], shapes[:, 4 + d, :], ACT.Exp, scale=g).then_inc(act_step, 1)
                    act.activation(keep["kdec"][:, 4 * d + h:4 * d + h + 1], cols[:, d:d + 1], ACT.Exp, scale=g
                                   ).then_inc(act_step, 1)
            act.activation(keep["cdec"][:, :], lg[:, :], ACT.Exp, scale=float(P)).then_inc(act_step, 1)
            act.wait_ge(dve_step, DV_FINAL)
            act.activation(final[:, 3, :, :], final[:, 3, :, :], ACT.Exp).then_inc(act_step, 1)
            act.activation(final[:, 1, :, :], final[:, 1, :, :], ACT.Exp, scale=-1.0).then_inc(act_step, 1)
            act.activation(final[:, 2, :, :], final[:, 2, :, :], ACT.Exp).then_inc(act_step, 1)

        @block.vector
        def _(dve):
            n = [0]

            def step(ins):
                ins.then_inc(dve_step, 1)
                n[0] += 1
                dve.wait_ge(dve_step, n[0])

            dve.wait_ge(act_step, 6)
            step(dve.tensor_scalar(decay_min[:, :], logit[:, :], 0.0, None, ALU.min))
            step(dve.tensor_tensor(decay_min[:, :], decay_min[:, :], decay_abs[:, :], ALU.subtract))
            assert n[0] == DV_LG
            fview = grows[64:128, :].rearrange("p (c t) -> p c t", t=P)
            iview = grows[0:64, :].rearrange("p (c t) -> p c t", t=P)
            lview = absf[:, :].rearrange("p (c t) -> p c t", t=P)
            step(dve.tensor_scalar(ping[:, :, :], fview, 0.0, None, ALU.min))
            step(dve.tensor_tensor(logf[F0, :, :], ping[F0, :, :], lview[F0, :, :], ALU.subtract))
            step(dve.tensor_tensor(logf[B0, :, ::-1], ping[B0, :, :], lview[B0, :, :], ALU.subtract))
            assert n[0] == DV_LOGF

            def scan(src, bufs, dst, op):
                cur = src
                for k in range(7):
                    reach = 1 << k
                    nxt = dst if k == 6 else bufs[k % 2]
                    step(dve.tensor_copy(nxt[:, :, 0:reach], cur[:, :, 0:reach]))
                    step(dve.tensor_tensor(nxt[:, :, reach:P], cur[:, :, reach:P], cur[:, :, 0:P - reach], op))
                    cur = nxt

            scan(logf, (ping, pong), cum_b, ALU.add)
            assert n[0] == DV_CUM
            dve.tensor_copy(logi[F0, :, :], iview[F0, :, :])
            step(dve.tensor_copy(logi[B0, :, ::-1], iview[B0, :, :]))
            step(dve.tensor_tensor(u[:, :, :], logi[:, :, :], cum_b[:, :, :], ALU.subtract))
            assert n[0] == DV_U
            top = final[:, 0, :, :]
            scan(u, (ping, pong), logf, ALU.max)
            assert n[0] == DV_MAX
            for e, src in enumerate((cum_b, logf)):
                step(dve.tensor_copy(ends[F0, e, :], src[F0, :, P - 1]))
                dve.tensor_copy(ends[B0, e, 0:CTX_TILES], src[B0, CTX_TILES - 1::-1, P - 1])
                step(dve.tensor_copy(ends[B0, e, CTX_TILES:TILES], src[B0, TILES - 1:CTX_TILES - 1:-1, P - 1]))
            dve.wait_ge(m_loaded, 32)
            for r in range(TILES):
                dst = m_ctx[:, 0:1] if r == CTX_TILES - 1 else m_in[:, r + 1:r + 2]
                step(dve.scalar_tensor_tensor(out=dst, in0=m_in[:, r:r + 1], scalar=ends[:, 1, r:r + 1],
                                              in1=ends[:, 0, r:r + 1], op0=ALU.max, op1=ALU.add))
            dve.tensor_copy(m_chunk[F0, :], m_in[F0, 0:TILES])
            step(dve.tensor_copy(m_chunk[B0, 0:CTX_TILES], m_in[B0, CTX_TILES - 1::-1]))
            step(dve.tensor_copy(m_chunk[B0, CTX_TILES:TILES], m_in[B0, TILES - 1:CTX_TILES - 1:-1]))
            assert n[0] == DV_MPREV
            mc = m_chunk[:, :].rearrange("p (c o) -> p c o", o=1).to_broadcast([G, TILES, P])
            step(dve.tensor_tensor(top, logf[:, :, :], mc, ALU.max))
            step(dve.tensor_tensor(final[:, 3, :, :], mc, top, ALU.subtract))
            step(dve.tensor_tensor(final[:, 1, :, :], cum_b[:, :, :], top, ALU.add))
            step(dve.tensor_tensor(final[:, 2, :, :], u[:, :, :], final[:, 0, :, P - 1:P].to_broadcast([G, TILES, P]),
                                   ALU.subtract))
            assert n[0] == DV_FINAL
            dve.wait_ge(act_step, 31)
            for d in range(2):
                step(dve.tensor_tensor(tables[:, d, :, :], tables[:, d, :, :],
                                       shapes[:, 2 + d:3 + d, :].to_broadcast([P, HEADS, P]), ALU.mult))
            step(dve.tensor_tensor(keep["mret"][:, :, :], tables[:, 0, :, :], tables[:, 1, :, :], ALU.add))
            dve.wait_ge(act_step, 34)
            for src, dst in ((u, ping), (final[:, 1, :, :], pong), (final[:, 2, :, :], cum_b),
                             (final[:, 0, :, :], logi), (final[:, 3, :, :], logf)):
                dve.tensor_copy(dst[F0, :, :], src[F0, :, :])
                step(dve.tensor_copy(dst[B0, :, ::-1], src[B0, :, :]))

        @block.gpsimd
        def _(pool):
            pool.memset(m_in[:, :], 0.0).then_inc(m_zero, 1)
            pool.wait_ge(dve_step, DV_FINAL + 3 + 5)
            for kind, src in ((U, ping), (EN, pong), (WE, cum_b), (MX, logi), (WI, logf)):
                for d in range(2):
                    at = kind * ROWS + 4 * d
                    pool.dma_start(s["rows"][at:at + 4, :], src[32 * d:32 * d + 4, :, :].rearrange("p c t -> p (c t)")
                                   ).then_inc(stored, 16)
            for d in range(2):
                pool.dma_start(out["m"][0, 0, d, :].rearrange("(h o) -> h o", o=1), m_ctx[32 * d:32 * d + 4, :]
                               ).then_inc(stored, 16)
            pool.dma_start(s["mdec"].rearrange("c (h o) -> h c o", o=1), logf[32:36, :, 0:1], allow_slow_non_contiguous=True
                           ).then_inc(stored, 16)
            pool.wait_ge(stored, 13 * 16)


def load_states(eng, a, state, d, loaded):
    eng.dma_start(state[:, 0:W].rearrange("p (h e) -> p h e", h=HEADS),
                  a["state_ret"][0, 0, d].rearrange("h p e -> p h e")).then_inc(loaded, 16)
    ml = state[:, W:STATE].rearrange("p (h e) -> p h e", h=HEADS)
    eng.dma_start(ml[:, :, 0:HD], a["state_mlstm_C"][0, 0, d].rearrange("h p e -> p h e")).then_inc(loaded, 16)
    eng.dma_start(ml[:, :, HD:AUG], a["state_mlstm_n"][0, 0, d].rearrange("h (p o) -> p h o", o=1),
                  allow_slow_non_contiguous=True).then_inc(loaded, 16)


def store_states(eng, out, state, d, stored):
    eng.dma_start(out["ret"][0, 0, d].rearrange("h p e -> p h e"),
                  state[:, 0:W].rearrange("p (h e) -> p h e", h=HEADS)).then_inc(stored, 16)
    ml = state[:, W:STATE].rearrange("p (h e) -> p h e", h=HEADS)
    eng.dma_start(out["C"][0, 0, d].rearrange("h p e -> p h e"), ml[:, :, 0:HD]).then_inc(stored, 16)
    eng.dma_start(out["n"][0, 0, d].rearrange("h (p o) -> p h o", o=1), ml[:, :, HD:AUG],
                  allow_slow_non_contiguous=True).then_inc(stored, 16)


def update_states(dve, old, new, kv_ret, kv_ml, cdec, mdec, done):
    for h in range(HEADS):
        dve.scalar_tensor_tensor(out=new[:, h * HD:(h + 1) * HD], in0=old[:, h * HD:(h + 1) * HD],
                                 scalar=cdec[:, h:h + 1], in1=kv_ret[:, h * HD:(h + 1) * HD], op0=ALU.mult, op1=ALU.add)
        at = slice(W + h * AUG, W + (h + 1) * AUG)
        last = dve.scalar_tensor_tensor(out=new[:, at], in0=old[:, at], scalar=mdec(h),
                                        in1=kv_ml(h), op0=ALU.mult, op1=ALU.add)
    last.then_inc(done, 1)


def backward_scan(nc, a, s, keep, out):
    ident = keep["ident"]
    with ExitStack() as ctx:
        m = Scope(nc, ctx, "bwd")
        convw = m.sb("convw", [P, 3, 2 * W])
        kv = m.sb("kv", [P, 2, 2, W])
        v1 = m.sb("v1", [P, 2, HEADS, AUG])
        xs = m.sb("xs", [P, 2, 3, 2 * W])
        werow = m.sb("werow", [HEADS, 2, P])
        mdec = m.sb("mdec", [P, 2, HEADS])
        sig = m.sb("sig", [P, 2, 2 * W])
        qk = m.sb("qk", [P, 2, 2 * W])
        kret = m.sb("kret", [P, 2, W])
        kml = m.sb("kml", [P, 2, W])
        state = m.sb("state", [P, 2, STATE])
        kvr_ps = m.ps("kvr", [P, 2, BLK])
        kvm_ps = m.ps("kvm", [P, 4, BLK])
        we_ps = m.ps("we", [P, 2, BLK])
        conv_loaded, ones_ready = m.sem("conv_loaded"), m.sem("ones_ready")
        loaded = [m.sem(f"loaded{j}") for j in range(2)]
        LOADS = 7
        side_taps, mid_tap, tap_sum, conv_sum = m.sem("side_taps"), m.sem("mid_tap"), m.sem("tap_sum"), m.sem("conv_sum")
        sig_ready, q_ready, k_ready = m.sem("sig_ready"), m.sem("q_ready"), m.sem("k_ready")
        kret_ready, we_ready, kml_ready = m.sem("kret_ready"), m.sem("we_ready"), m.sem("kml_ready")
        kv_done, updated = m.sem("kv_done"), m.sem("updated")
        zeroed, cached, ctx_stored = m.sem("zeroed"), m.sem("cached"), m.sem("ctx_stored")
        saved = [m.sem(f"saved{j}") for j in range(2)]
        qk_stored = [m.sem(f"qk_stored{j}") for j in range(2)]
        block = ctx.enter_context(nc.Block())

        def chunk(r, seq):
            return r * -1 + (TILES + CTX_TILES - 1 if seq else CTX_TILES - 1)

        def kvm(j, h):
            return kvm_ps[:, 2 * j + h // 2, (h % 2) * AUG:(h % 2 + 1) * AUG]

        @block.sync
        def _(sp):
            sp.dma_start(convw[:, :, :].rearrange("p j n -> p (j n)"),
                         a["conv_w"].rearrange("o j n -> o (j n)").to_broadcast([P, 6 * W])).then_inc(conv_loaded, 16)

            def load(pair, j, seq):
                r = 2 * pair + j
                c = chunk(r, seq)
                if seq:
                    sp.wait_ge(updated, r - 1)
                    sp.wait_ge(ctx_stored, 48)
                for i in range(3):
                    sp.dma_start(xs[:, j, i, :], s["mqk"][bass.ds(c * P + 2 * seq + i, P), :]).then_inc(loaded[j], 16)
                sp.dma_start(kv[:, j, :, :].rearrange("p a n -> p (a n)"), s["qkv"][bass.ts(c, P), W:3 * W]
                             ).then_inc(loaded[j], 16)
                sp.dma_start(v1[:, j, :, 0:HD], s["qkv"][bass.ts(c, P), 3 * W:4 * W].rearrange("p (h e) -> p h e", h=HEADS)
                             ).then_inc(loaded[j], 16)
                sp.dma_start(werow[:, j, :], s["rows"][WE * ROWS + 4:WE * ROWS + 8, bass.ts(c, P)]).then_inc(loaded[j], 16)
                sp.dma_start(mdec[:, j, :], s["mdec"][bass.ds(c, 1), :].to_broadcast([P, HEADS])).then_inc(loaded[j], 16)

            for j in range(2):
                load(0, j, 0)
            sp.wait_ge(updated, CTX_TILES)
            store_states(sp, out, state[:, 0, :], 1, ctx_stored)
            sp.wait_ge(ctx_stored, 48)
            sp.wait_ge(saved[0], 16)
            load_states(sp, a, state[:, 0, :], 1, cached)
            with sp.Fori(1, PAIRS) as pair:
                for j in range(2):
                    load(pair, j, 1)

        @block.scalar
        def _(act):
            def silu(pair, j, seq):
                r = 2 * pair + j
                act.wait_ge(conv_sum, r + 1)
                if seq:
                    act.wait_ge(q_ready, r - 1)
                act.activation(sig[:, j, :], xs[:, j, 1, :], ACT.Sigmoid).then_inc(sig_ready, 1)

            over_tiles(act, silu)

        @block.tensor
        def _(pe):
            def accumulate(pair, j, seq):
                r = 2 * pair + j
                pe.wait_ge(loaded[j], 16 * LOADS * (pair + 1))
                if seq:
                    pe.wait_ge(updated, r - 1)
                pe.wait_ge(kret_ready, r + 1)
                for h in range(HEADS):
                    pe.matmul(kvr_ps[:, j, h * HD:(h + 1) * HD], kret[:, j, h * HD:(h + 1) * HD],
                              kv[:, j, 1, h * HD:(h + 1) * HD], start=True, stop=True)
                pe.transpose(we_ps[:, j, 0:HEADS], werow[:, j, :], ident[0:HEADS, 0:HEADS]).then_inc(we_ready, 1)
                pe.wait_ge(kml_ready, r + 1)
                pe.wait_ge(ones_ready, 1)
                for h in range(HEADS):
                    last = pe.matmul(kvm(j, h), kml[:, j, h * HD:(h + 1) * HD], v1[:, j, h, :], start=True, stop=True)
                last.then_inc(kv_done, 1)

            over_tiles(pe, accumulate)

        @block.vector
        def _(dve):
            dve.memset(state[:, 0, :], 0.0).then_inc(zeroed, 1)
            dve.wait_ge(zeroed, 1)
            dve.wait_ge(conv_loaded, 16)

            def chunk_step(pair, j, seq):
                r = 2 * pair + j
                dve.wait_ge(loaded[j], 16 * LOADS * (pair + 1))
                dve.tensor_tensor(xs[:, j, 1, :], xs[:, j, 1, :], convw[:, 1, :], ALU.mult).then_inc(mid_tap, 1)
                dve.wait_ge(mid_tap, r + 1)
                dve.wait_ge(side_taps, 2 * r + 1)
                dve.tensor_tensor(xs[:, j, 1, :], xs[:, j, 0, :], xs[:, j, 1, :], ALU.add).then_inc(tap_sum, 1)
                dve.wait_ge(tap_sum, r + 1)
                dve.wait_ge(side_taps, 2 * r + 2)
                dve.tensor_tensor(xs[:, j, 1, :], xs[:, j, 1, :], xs[:, j, 2, :], ALU.add).then_inc(conv_sum, 1)
                dve.wait_ge(sig_ready, r + 1)
                dve.wait_ge(conv_sum, r + 1)
                dve.wait_ge(qk_stored[j], 16 * pair)
                dve.scalar_tensor_tensor(out=qk[:, j, W:2 * W], in0=xs[:, j, 1, W:2 * W], scalar=KSCALE,
                                         in1=sig[:, j, W:2 * W], op0=ALU.mult, op1=ALU.mult).then_inc(k_ready, 1)
                dve.wait_ge(we_ready, r + 1)
                dve.wait_ge(k_ready, r + 1)
                dve.tensor_tensor(kml[:, j, :].rearrange("p (h e) -> p h e", h=HEADS),
                                  qk[:, j, W:2 * W].rearrange("p (h e) -> p h e", h=HEADS),
                                  we_ps[:, j, 0:HEADS].rearrange("p (h o) -> p h o", o=1).to_broadcast([P, HEADS, HD]),
                                  ALU.mult).then_inc(kml_ready, 1)
                dve.tensor_tensor(qk[:, j, 0:W], xs[:, j, 1, 0:W], sig[:, j, 0:W], ALU.mult).then_inc(q_ready, 1)
                dve.wait_ge(kv_done, r + 1)
                if seq:
                    dve.wait_ge(cached, 48)
                    dve.wait_ge(updated, r)
                    dve.wait_ge(saved[1 - j], 16 * (pair + j))
                elif j == 1:
                    dve.wait_ge(updated, 1)
                    dve.wait_ge(saved[0], 16)
                update_states(dve, state[:, j, :], state[:, 1 - j, :], kvr_ps[:, j, :], lambda h: kvm(j, h),
                              keep["cdec"][:, 4:8], lambda h: mdec[:, j, h:h + 1], updated)

            over_tiles(dve, chunk_step)

        @block.gpsimd
        def _(pool):
            for j in range(2):
                last = pool.memset(v1[:, j, :, HD:AUG], 1.0)
            last.then_inc(ones_ready, 1)
            pool.wait_ge(conv_loaded, 16)

            def taps(pair, j, seq):
                r = 2 * pair + j
                pool.wait_ge(loaded[j], 16 * LOADS * (pair + 1))
                pool.tensor_tensor(xs[:, j, 0, :], xs[:, j, 0, :], convw[:, 0, :], ALU.mult).then_inc(side_taps, 1)
                pool.tensor_tensor(xs[:, j, 2, :], xs[:, j, 2, :], convw[:, 2, :], ALU.mult).then_inc(side_taps, 1)
                pool.tensor_tensor(kret[:, j, :].rearrange("p (h e) -> p h e", h=HEADS),
                                   kv[:, j, 0, :].rearrange("p (h e) -> p h e", h=HEADS),
                                   keep["kdec"][:, 4:8].rearrange("p (h o) -> p h o", o=1).to_broadcast([P, HEADS, HD]),
                                   ALU.mult).then_inc(kret_ready, 1)
                if seq:
                    pool.wait_ge(updated, r)
                    pool.wait_ge(cached, 48)
                else:
                    pool.wait_ge(zeroed, 1)
                    pool.wait_ge(updated, r)
                pool.dma_start(s["bst"][bass.ds(chunk(r, seq), 1), :, :].rearrange("c p n -> (c p) n"), state[:, j, :]
                               ).then_inc(saved[j], 16)
                pool.wait_ge(q_ready, r + 1)
                pool.wait_ge(conv_loaded, 16)
                pool.dma_start(s["mqk2"][bass.ts(chunk(r, seq), P), :], qk[:, j, :]).then_inc(qk_stored[j], 16)

            over_tiles(pool, taps)
            for j in range(2):
                pool.wait_ge(saved[j], 16 * PAIRS)
                pool.wait_ge(qk_stored[j], 16 * PAIRS)


def forward_scan(nc, a, s, keep, out):
    ident = keep["ident"]
    with ExitStack() as ctx:
        m = Scope(nc, ctx, "fwd")
        far = m.sb("far", [P, 2, P])
        qkv = m.sb("qkv", [P, 2, 3, W])
        v1 = m.sb("v1", [P, 2, HEADS, AUG])
        qk = m.sb("qk", [P, 2, 2 * W])
        gate = m.sb("gate", [P, 2, D])
        rows = m.sb("rows", [3 * ROWS, 2, P])
        wide = m.sb("wide", [P, 2, 2, ROWS, P])
        bst = m.sb("bst", [P, 2, STATE])
        state = m.sb("state", [P, 2, STATE])
        qT = m.sb("qT", [P, 2, HEADS, P])
        kT = m.sb("kT", [P, 2, HEADS, P])
        qd = m.sb("qd", [P, 2, 2, HEADS, P])
        cols = m.sb("cols", [P, 3, ROWS])
        wts = m.sb("wts", [P, 2, HEADS, P])
        aret = m.sb("aret", [P, HEADS, P])
        aml = m.sb("aml", [P, 2, HEADS, P])
        kret = m.sb("kret", [P, W])
        kml = m.sb("kml", [P, W])
        den = m.sb("den", [P, 8])
        den2 = m.sb("den2", [P, 8])
        o = m.sb("o", [P, 2 * HEADS, HD])
        hb = m.sb("hb", [P, HEADS, HD])
        mean = m.sb("mean", [P, 8])
        var = m.sb("var", [P, 8])
        rstd = m.sb("rstd", [P, 8])
        power = m.sb("power", [P, 8])
        y = m.sb("y", [P, 2, D])
        big = m.ps("big", [P, 4, BLK])
        sc = m.ps("sc", [P, 2, BLK])
        ret_ps = m.ps("ret", [P, BLK])
        misc = m.ps("misc", [P, BLK])
        COLS = slice(0, 3 * ROWS)
        KV3 = slice(3 * ROWS, 3 * ROWS + AUG)

        far_loaded, ones_ready = m.sem("far_loaded"), m.sem("ones_ready")
        loaded = [m.sem(f"loaded{j}") for j in range(2)]
        LOADS = 8
        transposed, cols_T = m.sem("transposed"), m.sem("cols_T")
        cols_ready, plain_ready, decayed_ready = m.sem("cols_ready"), m.sem("plain_ready"), m.sem("decayed_ready")
        scores, arg_ready, wts_ready = m.sem("scores"), m.sem("arg_ready"), m.sem("wts_ready")
        aret_ready, aml_ready = m.sem("aret_ready"), m.sem("aml_ready")
        kret_ready, kml_ready = m.sem("kret_ready"), m.sem("kml_ready")
        mixed, kv_done, updated = m.sem("mixed"), m.sem("kv_done"), m.sem("updated")
        oret_ready, den_step, h_part = m.sem("oret_ready"), m.sem("den_step"), m.sem("h_part")
        o_ready, norm_step, centred = m.sem("o_ready"), m.sem("norm_step"), m.sem("centred")
        squared, normed, y_ready = m.sem("squared"), m.sem("normed"), m.sem("y_ready")
        y_stored = [m.sem(f"y_stored{j}") for j in range(2)]
        zeroed, cached, ctx_stored = m.sem("zeroed"), m.sem("cached"), m.sem("ctx_stored")
        power_ready = m.sem("power_ready")
        block = ctx.enter_context(nc.Block())

        def retq(d, h):
            return qd[:, 0, d, h, :]

        def mlq(d, h):
            return qd[:, 1, d, h, :]

        def kvm(h):
            return sc[:, 1, h * AUG:(h + 1) * AUG] if h < 3 else misc[:, KV3]

        def num(d, h):
            return big[:, 2 * d + h // 2, (h % 2) * AUG:(h % 2 + 1) * AUG]

        def head_sum(d):
            return big[:, 2 * d:2 * d + 2, 0:2 * AUG].rearrange("p b (g e) -> p b g e", g=2)[:, :, :, 0:HD]

        @block.sync
        def _(sp):
            sp.dma_start(far[:, :, :], a["far"]).then_inc(far_loaded, 16)

            def load(pair, j, seq):
                c = 2 * pair + j
                if seq:
                    sp.wait_ge(updated, c - 1)
                    sp.wait_ge(y_ready, c - 1)
                r = bass.ts(c, P)
                inc = (loaded[j], 16)
                sp.dma_start(rows[:, j, :], s["rows"][0:3 * ROWS, r]).then_inc(*inc)
                sp.dma_start(qkv[:, j, :, :].rearrange("p a n -> p (a n)"), s["qkv"][r, 0:3 * W]).then_inc(*inc)
                sp.dma_start(qk[:, j, :], s["mqk2"][r, :]).then_inc(*inc)
                for kind in (MX, WI):
                    sp.dma_start(wide[:, j, kind - MX, :, :], s["rows"][kind * ROWS:(kind + 1) * ROWS, r]
                                 .rearrange("(o k) t -> o k t", o=1).to_broadcast([P, ROWS, P])).then_inc(*inc)
                sp.dma_start(v1[:, j, :, 0:HD], s["qkv"][r, 3 * W:4 * W].rearrange("p (h e) -> p h e", h=HEADS)).then_inc(*inc)
                sp.dma_start(bst[:, j, :], s["bst"][bass.ds(c, 1), :, :].rearrange("c p n -> (c p) n")).then_inc(*inc)
                sp.dma_start(gate[:, j, :], s["gate"][r, :]).then_inc(*inc)

            for j in range(2):
                load(0, j, 0)
            sp.wait_ge(updated, CTX_TILES)
            store_states(sp, out, state[:, 0, :], 0, ctx_stored)
            sp.wait_ge(ctx_stored, 48)
            load_states(sp, a, state[:, 0, :], 0, cached)
            with sp.Fori(1, PAIRS) as pair:
                for j in range(2):
                    load(pair, j, 1)

        @block.scalar
        def _(act):
            def chunk_step(pair, j, seq):
                c = 2 * pair + j
                act.wait_ge(transposed, c + 1)
                act.wait_ge(scores, c)
                for i in range(2):
                    act.activation(qT[:, i, :, :], big[:, 2 * i, :].rearrange("p (h t) -> p h t", h=HEADS), ACT.Copy)
                    last = act.activation(kT[:, i, :, :], big[:, 2 * i + 1, :].rearrange("p (h t) -> p h t", h=HEADS), ACT.Copy)
                last.then_inc(plain_ready, 1)
                act.wait_ge(arg_ready, c + 1)
                act.activation(wts[:, :, :, :], wts[:, :, :, :], ACT.Exp, scale=-1.0).then_inc(wts_ready, 1)
                act.wait_ge(mixed, c + 1)
                if not (isinstance(pair, int) and c == 0):
                    act.wait_ge(y_ready, c)
                act.activation(o[:, 0:HEADS, :], ret_ps[:, :].rearrange("p (h e) -> p h e", h=HEADS), ACT.Copy
                               ).then_inc(oret_ready, 1)
                act.wait_ge(centred, c + 1)
                act.wait_ge(y_stored[j], 16 * pair)
                act.activation(y[:, j, :], o[:, :, :].rearrange("p h e -> p (h e)"), ACT.Square).then_inc(squared, 1)

            over_tiles(act, chunk_step)

        @block.tensor
        def _(pe):
            def chunk_step(pair, j, seq):
                c = 2 * pair + j
                pe.wait_ge(loaded[j], 16 * LOADS * (pair + 1))
                pe.wait_ge(o_ready, c)
                pe.wait_ge(updated, c)
                for i, src in enumerate((qkv[:, j, 0, :], qkv[:, j, 1, :], qk[:, j, 0:W], qk[:, j, W:2 * W])):
                    for h in range(HEADS):
                        last = pe.transpose(big[:, i, h * P:(h + 1) * P], src[:, h * HD:(h + 1) * HD], ident[:, :])
                    if i == 0:
                        pe.transpose(misc[:, COLS], rows[:, j, :], ident[0:3 * ROWS, 0:3 * ROWS]).then_inc(cols_T, 1)
                last.then_inc(transposed, 1)
                pe.wait_ge(plain_ready, c + 1)
                for i in range(2):
                    for h in range(HEADS):
                        last = pe.matmul(sc[:, i, h * P:(h + 1) * P], kT[:, i, h, :], qT[:, i, h, :], start=True, stop=True)
                last.then_inc(scores, 1)
                pe.wait_ge(aret_ready, c + 1)
                pe.wait_ge(decayed_ready, 2 * c + 2)
                if seq:
                    pe.wait_ge(cached, 48)
                pe.wait_ge(oret_ready, c)
                for h in range(HEADS):
                    at = slice(h * HD, (h + 1) * HD)
                    pe.matmul(ret_ps[:, at], aret[:, h, :], qkv[:, j, 2, at], start=True, stop=False)
                    pe.matmul(ret_ps[:, at], retq(0, h), state[:, j, at], start=False, stop=False)
                    pe.matmul(ret_ps[:, at], retq(1, h), bst[:, j, at], start=False, stop=True)
                pe.wait_ge(aml_ready, c + 1)
                pe.wait_ge(ones_ready, 1)
                for d in range(2):
                    for h in range(HEADS):
                        at = slice(W + h * AUG, W + (h + 1) * AUG)
                        pe.matmul(num(d, h), aml[:, d, h, :], v1[:, j, h, :], start=True, stop=False)
                        last = pe.matmul(num(d, h), mlq(d, h), (state if d == 0 else bst)[:, j, at],
                                         start=False, stop=True)
                last.then_inc(mixed, 1)
                pe.wait_ge(kret_ready, c + 1)
                pe.wait_ge(kml_ready, c + 1)
                for h in range(HEADS):
                    at = slice(h * HD, (h + 1) * HD)
                    pe.matmul(sc[:, 0, at], kret[:, at], qkv[:, j, 2, at], start=True, stop=True)
                for h in range(HEADS):
                    last = pe.matmul(kvm(h), kml[:, h * HD:(h + 1) * HD], v1[:, j, h, :], start=True, stop=True)
                last.then_inc(kv_done, 1)

            over_tiles(pe, chunk_step)

        @block.vector
        def _(dve):
            dve.memset(state[:, 0, :], 0.0).then_inc(zeroed, 1)
            dve.wait_ge(zeroed, 1)
            dve.wait_ge(far_loaded, 16)

            def chunk_step(pair, j, seq):
                c = 2 * pair + j
                dve.wait_ge(loaded[j], 16 * LOADS * (pair + 1))
                dve.wait_ge(cols_T, c + 1)
                dve.wait_ge(kml_ready, c)
                dve.tensor_copy(cols[:, :, :].rearrange("p k r -> p (k r)"), misc[:, COLS]).then_inc(cols_ready, 1)
                dve.wait_ge(cols_ready, c + 1)
                for d in range(2):
                    for h in range(HEADS):
                        last = dve.scalar_tensor_tensor(out=wts[:, d, h, :], in0=wide[:, j, 0, 4 * d + h, :],
                                                        scalar=cols[:, U, 4 * d + h:4 * d + h + 1], in1=far[:, d, :],
                                                        op0=ALU.subtract, op1=ALU.add)
                last.then_inc(arg_ready, 1)
                dve.wait_ge(plain_ready, c + 1)
                dve.wait_ge(mixed, c)
                for d in range(2):
                    q = big[:, 0, :].rearrange("p (h t) -> p h t", h=HEADS)
                    dve.tensor_tensor(qd[:, 0, d, :, :], q, keep["qdec"][:, d, :, :], ALU.mult)
                    q = big[:, 2, :].rearrange("p (h t) -> p h t", h=HEADS)
                    dve.tensor_tensor(qd[:, 1, d, :, :], q, wide[:, j, 1, 4 * d:4 * d + 4, :], ALU.mult).then_inc(decayed_ready, 1)
                dve.wait_ge(scores, c + 1)
                dve.tensor_tensor(aret[:, :, :], sc[:, 0, :].rearrange("p (h t) -> p h t", h=HEADS), keep["mret"][:, :, :],
                                  ALU.mult).then_inc(aret_ready, 1)
                dve.wait_ge(wts_ready, c + 1)
                for d in range(2):
                    last = dve.tensor_tensor(aml[:, d, :, :], sc[:, 1, :].rearrange("p (h t) -> p h t", h=HEADS),
                                             wts[:, d, :, :], ALU.mult)
                last.then_inc(aml_ready, 1)
                dve.wait_ge(mixed, c + 1)
                dv = big[:, :, 0:2 * AUG].rearrange("p b (g e) -> p b g e", g=2)[:, :, :, HD]
                dve.tensor_copy(den[:, :].rearrange("p (b g) -> p b g", g=2), dv).then_inc(den_step, 1)
                dve.wait_ge(den_step, 4 * c + 1)
                dve.scalar_tensor_tensor(out=den2[:, :], in0=den[:, :], scalar=-1.0, in1=den[:, :], op0=ALU.mult, op1=ALU.max
                                         ).then_inc(den_step, 1)
                dve.wait_ge(den_step, 4 * c + 2)
                dve.tensor_tensor(den[:, :], den2[:, :], cols[:, EN, :], ALU.max).then_inc(den_step, 1)
                dve.wait_ge(den_step, 4 * c + 3)
                dve.reciprocal(den2[:, :], den[:, :]).then_inc(den_step, 1)
                dve.wait_ge(den_step, 4 * c + 4)
                dve.wait_ge(y_ready, c)
                for d, dst in ((0, o[:, HEADS:2 * HEADS, :]), (1, hb[:, :, :])):
                    last = dve.tensor_tensor(dst.rearrange("p (b g) e -> p b g e", g=2), head_sum(d),
                                             den2[:, 4 * d:4 * d + 4].rearrange("p (b g o) -> p b g o", g=2, o=1)
                                             .to_broadcast([P, 2, 2, HD]), ALU.mult)
                last.then_inc(h_part, 1)
                dve.wait_ge(h_part, c + 1)
                dve.tensor_tensor(o[:, HEADS:2 * HEADS, :], o[:, HEADS:2 * HEADS, :], hb[:, :, :], ALU.add).then_inc(o_ready, 1)
                dve.wait_ge(kv_done, c + 1)
                if seq:
                    dve.wait_ge(cached, 48)
                dve.wait_ge(updated, c)
                update_states(dve, state[:, j, :], state[:, 1 - j, :], sc[:, 0, :], kvm, keep["cdec"][:, 0:4],
                              lambda h: wide[:, j, 1, h, P - 1:P], updated)
                dve.wait_ge(oret_ready, c + 1)
                dve.wait_ge(o_ready, c + 1)
                dve.tensor_reduce(mean[:, :], o[:, :, :], AX_X, ALU.add).then_inc(norm_step, 1)
                dve.wait_ge(norm_step, 5 * c + 1)
                dve.tensor_scalar(mean[:, :], mean[:, :], 1.0 / HD, None, ALU.mult).then_inc(norm_step, 1)
                dve.wait_ge(norm_step, 5 * c + 2)
                wide_mean = mean[:, :].rearrange("p (h o) -> p h o", o=1).to_broadcast([P, 2 * HEADS, HD])
                dve.tensor_tensor(o[:, :, :], o[:, :, :], wide_mean, ALU.subtract).then_inc(centred, 1)
                dve.wait_ge(squared, c + 1)
                dve.wait_ge(centred, c + 1)
                dve.tensor_reduce(var[:, :], y[:, j, :].rearrange("p (h e) -> p h e", e=HD), AX_X, ALU.add).then_inc(norm_step, 1)
                dve.wait_ge(norm_step, 5 * c + 3)
                dve.tensor_scalar(var[:, :], var[:, :], 1.0 / HD, EPS, ALU.mult, ALU.add).then_inc(norm_step, 1)
                dve.wait_ge(norm_step, 5 * c + 5)
                wide_std = rstd[:, :].rearrange("p (h o) -> p h o", o=1).to_broadcast([P, 2 * HEADS, HD])
                dve.tensor_tensor(y[:, j, :].rearrange("p (h e) -> p h e", e=HD), o[:, :, :], wide_std, ALU.mult).then_inc(normed, 1)
                dve.wait_ge(normed, c + 1)
                dve.tensor_tensor(y[:, j, :], y[:, j, :], gate[:, j, :], ALU.mult).then_inc(y_ready, 1)

            over_tiles(dve, chunk_step)

        @block.gpsimd
        def _(pool):
            for j in range(2):
                last = pool.memset(v1[:, j, :, HD:AUG], 1.0)
            last.then_inc(ones_ready, 1)
            pool.memset(power[:, :], -0.5).then_inc(power_ready, 1)
            pool.wait_ge(power_ready, 1)

            def chunk_step(pair, j, seq):
                c = 2 * pair + j
                pool.wait_ge(loaded[j], 16 * LOADS * (pair + 1))
                pool.wait_ge(kv_done, c)
                pool.tensor_tensor(kret[:, :].rearrange("p (h e) -> p h e", h=HEADS),
                                   qkv[:, j, 1, :].rearrange("p (h e) -> p h e", h=HEADS),
                                   keep["kdec"][:, 0:4].rearrange("p (h o) -> p h o", o=1).to_broadcast([P, HEADS, HD]),
                                   ALU.mult).then_inc(kret_ready, 1)
                pool.wait_ge(cols_ready, c + 1)
                pool.tensor_tensor(kml[:, :].rearrange("p (h e) -> p h e", h=HEADS),
                                   qk[:, j, W:2 * W].rearrange("p (h e) -> p h e", h=HEADS),
                                   cols[:, WE, 0:4].rearrange("p (h o) -> p h o", o=1).to_broadcast([P, HEADS, HD]),
                                   ALU.mult).then_inc(kml_ready, 1)
                pool.wait_ge(norm_step, 5 * c + 4)
                pool.tensor_tensor(rstd[:, :], var[:, :], power[:, :], ALU.pow).then_inc(norm_step, 1)
                pool.wait_ge(y_ready, c + 1)
                pool.dma_start(s["y"][bass.ts(c, P), :], y[:, j, :]).then_inc(y_stored[j], 16)

            over_tiles(pool, chunk_step)
            for j in range(2):
                pool.wait_ge(y_stored[j], 16 * PAIRS)


def output(nc, a, s, keep):
    ident = keep["ident"]
    with ExitStack() as ctx:
        m = Scope(nc, ctx, "out")
        w = m.sb("w", [P, KT, D])
        y = m.sb("y", [P, 2, D])
        x = m.sb("x", [P, 2, D])
        yT = m.sb("yT", [P, 2, KT, P])
        x1 = m.sb("x1", [P, 2, D])
        h = m.sb("h", [P, 2, D])
        hT = m.sb("hT", [P, 2, KT, P])
        g1 = m.sb("g1", [P, 2, D])
        shift = m.sb("shift", [P, 2, D])
        scale = m.sb("scale", [P, 2, D])
        gain = m.sb("gain", [P, D])
        junk = m.sb("junk", [P, D])
        ssq = m.sb("ssq", [P, 2])
        rstd = m.sb("rstd", [P, 2])
        mean = m.sb("mean", [P, 2])
        power = m.sb("power", [P, 1])
        yT_ps = m.ps("yT_ps", [P, KT, P])
        hT_ps = m.ps("hT_ps", [P, KT, P])
        acc = m.ps("acc", [P, 2, 2, BLK])
        w_loaded, mod_loaded, scale_ready = m.sem("w_loaded"), m.sem("mod_loaded"), m.sem("scale_ready")
        loaded = [m.sem(f"loaded{j}") for j in range(2)]
        y_T, yT_ready, product = m.sem("y_T"), m.sem("yT_ready"), m.sem("product")
        gated, x1_ready, ssq_ready = m.sem("gated"), m.sem("x1_ready"), m.sem("ssq_ready")
        rstd_step, scaled, h_ready = m.sem("rstd_step"), m.sem("scaled"), m.sem("h_ready")
        h_T, hT_ready = m.sem("h_T"), m.sem("hT_ready")
        x1_stored = [m.sem(f"x1_stored{j}") for j in range(2)]
        hT_stored = [m.sem(f"hT_stored{j}") for j in range(2)]
        power_ready = m.sem("power_ready")
        block = ctx.enter_context(nc.Block())

        @block.sync
        def _(sp):
            def load(pair, j, seq):
                t = 2 * pair + j
                if seq:
                    sp.wait_ge(x1_ready, t - 1)
                sp.dma_start(y[:, j, :], s["y"][bass.ts(t, P), :]).then_inc(loaded[j], 16)
                src = a["x_sample"][0, bass.ts(t - CTX_TILES, P), :] if seq else a["x_prompt"][0, bass.ts(t, P), :]
                sp.dma_start(x[:, j, :], src).then_inc(loaded[j], 16)

            for j in range(2):
                load(0, j, 0)
            w_out = a["w_out"][0].rearrange("(k p) n -> p k n", p=P)
            for n in range(2):
                sp.dma_start(w[:, :, n * BLK:(n + 1) * BLK], w_out[:, :, n * BLK:(n + 1) * BLK]).then_inc(w_loaded, 16)
            for seq in range(2):
                for dst, at in ((g1, 2), (shift, 3), (scale, 4)):
                    sp.dma_start(dst[:, seq, :], s["mod"][seq:seq + 1, at * D:(at + 1) * D].to_broadcast([P, D])
                                 ).then_inc(mod_loaded, 16)
            sp.dma_start(gain[:, :], a["norm2_g"].to_broadcast([P, D])).then_inc(mod_loaded, 16)
            with sp.Fori(1, PAIRS) as pair:
                for j in range(2):
                    load(pair, j, 1)

        @block.scalar
        def _(act):
            def tile_step(pair, j, seq):
                t = 2 * pair + j
                act.wait_ge(y_T, t + 1)
                if seq:
                    act.wait_ge(product, t - 1)
                act.activation(yT[:, j, :, :], yT_ps[:, :, :], ACT.Copy).then_inc(yT_ready, 1)
                act.wait_ge(x1_ready, t + 1)
                act.wait_ge(ssq_ready, t)
                if seq:
                    act.wait_ge(rstd_step, 2 * (t - 1))
                act.activation(junk[:, :], x1[:, j, :], ACT.Square, accum_out=ssq[:, j:j + 1]).then_inc(ssq_ready, 1)
                act.wait_ge(h_T, t + 1)
                act.wait_ge(hT_stored[j], 16 * pair)
                act.activation(hT[:, j, :, :], hT_ps[:, :, :], ACT.Copy).then_inc(hT_ready, 1)

            over_tiles(act, tile_step)

        @block.tensor
        def _(pe):
            pe.wait_ge(w_loaded, 32)

            def tile_step(pair, j, seq):
                t = 2 * pair + j
                pe.wait_ge(loaded[j], 32 * (pair + 1))
                pe.wait_ge(yT_ready, t)
                for k in range(KT):
                    last = pe.transpose(yT_ps[:, k, :], y[:, j, k * P:(k + 1) * P], ident[:, :])
                last.then_inc(y_T, 1)
                pe.wait_ge(yT_ready, t + 1)
                if seq:
                    pe.wait_ge(gated, t - 1)
                for n in range(2):
                    for k in range(KT):
                        last = pe.matmul(acc[:, j, n, :], yT[:, j, k, :], w[:, k, n * BLK:(n + 1) * BLK],
                                         start=(k == 0), stop=(k == KT - 1))
                last.then_inc(product, 1)
                pe.wait_ge(h_ready, t + 1)
                pe.wait_ge(hT_ready, t)
                for k in range(KT):
                    last = pe.transpose(hT_ps[:, k, :], h[:, j, k * P:(k + 1) * P], ident[:, :])
                last.then_inc(h_T, 1)

            over_tiles(pe, tile_step)

        @block.vector
        def _(dve):
            dve.wait_ge(mod_loaded, 7 * 16)
            for seq in range(2):
                dve.scalar_tensor_tensor(out=scale[:, seq, :], in0=scale[:, seq, :], scalar=1.0, in1=gain[:, :],
                                         op0=ALU.add, op1=ALU.mult).then_inc(scale_ready, 1)
            dve.wait_ge(scale_ready, 2)

            def tile_step(pair, j, seq):
                t = 2 * pair + j
                dve.wait_ge(product, t + 1)
                dve.wait_ge(x1_stored[j], 16 * pair)
                if seq:
                    dve.wait_ge(h_ready, t - 1)
                dve.tensor_tensor(x1[:, j, :], acc[:, j, :, :].rearrange("p n c -> p (n c)"), g1[:, seq, :], ALU.mult
                                  ).then_inc(gated, 1)
                dve.wait_ge(gated, t + 1)
                dve.wait_ge(loaded[j], 32 * (pair + 1))
                dve.tensor_tensor(x1[:, j, :], x1[:, j, :], x[:, j, :], ALU.add).then_inc(x1_ready, 1)
                dve.wait_ge(ssq_ready, t + 1)
                dve.tensor_scalar(mean[:, j:j + 1], ssq[:, j:j + 1], 1.0 / D, EPS, ALU.mult, ALU.add).then_inc(rstd_step, 1)
                dve.wait_ge(rstd_step, 2 * t + 2)
                if seq:
                    dve.wait_ge(h_T, t - 1)
                dve.scalar_tensor_tensor(out=h[:, j, :], in0=x1[:, j, :], scalar=rstd[:, j:j + 1], in1=scale[:, seq, :],
                                         op0=ALU.mult, op1=ALU.mult).then_inc(scaled, 1)
                dve.wait_ge(scaled, t + 1)
                dve.tensor_tensor(h[:, j, :], h[:, j, :], shift[:, seq, :], ALU.add).then_inc(h_ready, 1)

            over_tiles(dve, tile_step)

        @block.gpsimd
        def _(pool):
            pool.memset(power[:, :], -0.5).then_inc(power_ready, 1)
            pool.wait_ge(power_ready, 1)

            def store(pair, j, seq):
                t = 2 * pair + j
                pool.wait_ge(x1_ready, t + 1)
                pool.dma_start(s["x1"][bass.ts(t, P), :], x1[:, j, :]).then_inc(x1_stored[j], 16)
                pool.wait_ge(rstd_step, 2 * t + 1)
                pool.tensor_tensor(rstd[:, j:j + 1], mean[:, j:j + 1], power[:, 0:1], ALU.pow).then_inc(rstd_step, 1)
                pool.wait_ge(hT_ready, t + 1)
                pool.dma_start(s["h2T"][:, :, bass.ts(t, P)], hT[:, j, :, :]).then_inc(hT_stored[j], 16)

            over_tiles(pool, store)
            for j in range(2):
                pool.wait_ge(x1_stored[j], 16 * PAIRS)
                pool.wait_ge(hT_stored[j], 16 * PAIRS)


def mlp(nc, a, s, keep, out):
    BLOCKS = [(at, min(BLK, TOKENS - at)) for at in range(0, TOKENS, BLK)]
    NBL = len(BLOCKS)
    with ExitStack() as ctx:
        m = Scope(nc, ctx, "mlp")
        hT = m.sb("hT", [P, KT, TOKENS])
        total = m.sb("total", [P, TILES, D])
        w1 = m.sb("w1", [P, 2, KT, P])
        w2 = m.sb("w2", [P, 2, D])
        fT = m.sb("fT", [P, 2, TOKENS])
        up = m.ps("up", [P, 2, BLK])
        down = m.ps("down", [P, 4, BLK])
        hT_loaded = [m.sem(f"hT_loaded{i}") for i in range(NBL)]
        w_loaded = [m.sem(f"w_loaded{j}") for j in range(2)]
        total_zero = m.sem("total_zero")
        up_done, relu_done, squared = m.sem("up_done"), m.sem("relu_done"), m.sem("squared")
        down_done, added = m.sem("down_done"), m.sem("added")
        w_ff1 = a["w_ff1"][0].rearrange("(k p) f -> p k f", p=P)
        w_ff2 = a["w_ff2"][0]
        matmuls = ctx.enter_context(ExitStack())
        block = matmuls.enter_context(nc.Block())

        def bank(j, i):
            return (NBL * j + i) % 2

        def over_chunks(engine, body):
            for j in range(2):
                body(0, j)
            with engine.Fori(1, FF_CHUNKS // 2) as pair:
                for j in range(2):
                    body(pair, j)

        @block.sync
        def _(sp):
            def load(pair, j):
                f = 2 * pair + j
                if not isinstance(pair, int):
                    sp.wait_ge(down_done, 2 * TILES * (f - 1))
                sp.dma_start(w1[:, j, :, :], w_ff1[:, :, bass.ts(f, P)]).then_inc(w_loaded[j], 16)
                sp.dma_start(w2[:, j, :], w_ff2[bass.ts(f, P), :]).then_inc(w_loaded[j], 16)

            load(0, 0)
            for i, (at, size) in enumerate(BLOCKS):
                sp.dma_start(hT[:, :, at:at + size], s["h2T"][:, :, at:at + size]).then_inc(hT_loaded[i], 16)
            load(0, 1)
            with sp.Fori(1, FF_CHUNKS // 2) as pair:
                for j in range(2):
                    load(pair, j)

        @block.scalar
        def _(act):
            def activate(pair, j):
                f = 2 * pair + j
                for i, (at, size) in enumerate(BLOCKS):
                    q = NBL * f + i
                    act.wait_ge(up_done, q + 1)
                    if not isinstance(pair, int) and i == 0:
                        act.wait_ge(down_done, 2 * TILES * (f - 1))
                    act.activation(fT[:, j, at:at + size], up[:, bank(j, i), 0:size], ACT.Relu
                                   ).then_inc(relu_done, 1)
                    act.wait_ge(relu_done, q + 1)
                    act.activation(fT[:, j, at:at + size], fT[:, j, at:at + size], ACT.Square).then_inc(squared, 1)

            over_chunks(act, activate)

        @block.tensor
        def _(pe):
            def multiply(pair, j):
                f = 2 * pair + j
                pe.wait_ge(w_loaded[j], 32 * (pair + 1))
                for i, (at, size) in enumerate(BLOCKS):
                    q = NBL * f + i
                    if isinstance(pair, int) and j == 0:
                        pe.wait_ge(hT_loaded[i], 16)
                    if not (isinstance(pair, int) and q < 2):
                        pe.wait_ge(relu_done, q - 1)
                    for k in range(KT):
                        last = pe.matmul(up[:, bank(j, i), 0:size], w1[:, j, k, :], hT[:, k, at:at + size],
                                         start=(k == 0), stop=(k == KT - 1))
                    last.then_inc(up_done, 1)
                for t in range(TILES):
                    if t * P % BLK == 0:
                        pe.wait_ge(squared, NBL * f + t * P // BLK + 1)
                    for n in range(2):
                        q = 2 * TILES * f + 2 * t + n
                        if not (isinstance(pair, int) and q < 4):
                            pe.wait_ge(added, q - 3)
                        pe.matmul(down[:, (2 * t + n) % 4, :], fT[:, j, t * P:(t + 1) * P], w2[:, j, n * BLK:(n + 1) * BLK],
                                  start=True, stop=True).then_inc(down_done, 1)

            over_chunks(pe, multiply)

        @block.vector
        def _(dve):
            dve.wait_ge(total_zero, 1)

            def add(pair, j):
                f = 2 * pair + j
                for t in range(TILES):
                    for n in range(2):
                        q = 2 * TILES * f + 2 * t + n
                        dst = total[:, t, n * BLK:(n + 1) * BLK]
                        dve.wait_ge(down_done, q + 1)
                        if not (isinstance(pair, int) and f == 0):
                            dve.wait_ge(added, q - 2 * TILES + 1)
                        dve.tensor_tensor(dst, dst, down[:, (2 * t + n) % 4, :], ALU.add).then_inc(added, 1)

            over_chunks(dve, add)

        @block.gpsimd
        def _(pool):
            pool.memset(total[:, :, :], 0.0).then_inc(total_zero, 1)

        matmuls.close()
        final = ctx.enter_context(nc.Block())
        flat = hT[:, :, :].rearrange("p k t -> p (k t)")
        x1 = flat[:, 0:2 * D].rearrange("p (j n) -> p j n", j=2)
        g2 = flat[:, 2 * D:4 * D].rearrange("p (j n) -> p j n", j=2)
        gain = flat[:, 4 * D:5 * D]
        junk = flat[:, 5 * D:6 * D]
        ssq = flat[:, 6 * D:6 * D + 2]
        rstd = flat[:, 6 * D + 2:6 * D + 4]
        mean = flat[:, 6 * D + 4:6 * D + 6]
        power = flat[:, 6 * D + 6:6 * D + 7]
        power_ready = m.sem("power_ready")
        mod_loaded, gated, x2_ready, ssq_ready = m.sem("mod_loaded"), m.sem("gated"), m.sem("x2_ready"), m.sem("ssq_ready")
        rstd_step, y_ready = m.sem("rstd_step"), m.sem("y_ready")
        x1_loaded = [m.sem(f"x1_loaded{j}") for j in range(2)]
        y_stored = [m.sem(f"y_stored{j}") for j in range(2)]

        @final.sync
        def _(sp):
            for seq in range(2):
                sp.dma_start(g2[:, seq, :], s["mod"][seq:seq + 1, 5 * D:6 * D].to_broadcast([P, D])).then_inc(mod_loaded, 16)
            sp.dma_start(gain, a["final_g"].rearrange("(o n) -> o n", o=1).to_broadcast([P, D])).then_inc(mod_loaded, 16)

            def load(pair, j, seq):
                t = 2 * pair + j
                if seq:
                    sp.wait_ge(y_stored[j], 16 * pair)
                sp.dma_start(x1[:, j, :], s["x1"][bass.ts(t, P), :]).then_inc(x1_loaded[j], 16)

            over_tiles(sp, load)

        @final.scalar
        def _(act):
            def square(pair, j, seq):
                t = 2 * pair + j
                act.wait_ge(x2_ready, t + 1)
                act.wait_ge(ssq_ready, t)
                if seq:
                    act.wait_ge(rstd_step, 2 * (t - 1))
                act.activation(junk, x1[:, j, :], ACT.Square, accum_out=ssq[:, j:j + 1]).then_inc(ssq_ready, 1)

            over_tiles(act, square)

        @final.vector
        def _(dve):
            dve.wait_ge(mod_loaded, 48)

            def tile_step(pair, j, seq):
                t = 2 * pair + j
                f = total[:, bass.ds(t, 1), :].rearrange("p o n -> p (o n)")
                dve.tensor_tensor(f, f, g2[:, seq, :], ALU.mult).then_inc(gated, 1)
                dve.wait_ge(gated, t + 1)
                dve.wait_ge(x1_loaded[j], 16 * (pair + 1))
                dve.tensor_tensor(x1[:, j, :], x1[:, j, :], f, ALU.add).then_inc(x2_ready, 1)
                dve.wait_ge(ssq_ready, t + 1)
                dve.tensor_scalar(mean[:, j:j + 1], ssq[:, j:j + 1], 1.0 / D, EPS, ALU.mult, ALU.add).then_inc(rstd_step, 1)
                dve.wait_ge(rstd_step, 2 * t + 2)
                dve.wait_ge(x2_ready, t + 1)
                dve.scalar_tensor_tensor(out=x1[:, j, :], in0=x1[:, j, :], scalar=rstd[:, j:j + 1], in1=gain,
                                         op0=ALU.mult, op1=ALU.mult).then_inc(y_ready, 1)

            over_tiles(dve, tile_step)

        @final.gpsimd
        def _(pool):
            pool.memset(power[:, :], -0.5).then_inc(power_ready, 1)
            pool.wait_ge(power_ready, 1)

            def store(pair, j, seq):
                t = 2 * pair + j
                pool.wait_ge(rstd_step, 2 * t + 1)
                pool.tensor_tensor(rstd[:, j:j + 1], mean[:, j:j + 1], power[:, 0:1], ALU.pow).then_inc(rstd_step, 1)
                pool.wait_ge(y_ready, t + 1)
                dst = out["y_s"][0, bass.ts(t - CTX_TILES, P), :] if seq else out["y_p"][0, bass.ts(t, P), :]
                pool.dma_start(dst, x1[:, j, :]).then_inc(y_stored[j], 16)

            over_tiles(pool, store)
            for j in range(2):
                pool.wait_ge(y_stored[j], 16 * PAIRS)


_INS = ["x_prompt", "x_sample", "state_ret", "state_mlstm_C", "state_mlstm_n", "state_mlstm_m", "c", "c_ctx", "w_ada",
        "b_ada", "norm1_g", "norm2_g", "w_in", "conv_w", "ret_decay_logit", "mlstm_gate_bias", "ret_gn_g", "mlstm_gn_g",
        "w_out", "w_ff1", "w_ff2", "final_g"]
_OUTS = [("y_p", (1, 256, 1024)), ("y_s", (1, 2048, 1024)), ("ret", (1, 1, 2, 4, 128, 128)), ("C", (1, 1, 2, 4, 128, 128)),
         ("n", (1, 1, 2, 4, 128)), ("m", (1, 1, 2, 4))]


def shape_constants():
    import numpy as np
    i = np.arange(128, dtype=np.float32)
    s, t = i[:, None], i[None, :]
    zero = np.zeros((128, 128), np.float32)
    shapes = np.stack([np.maximum(t - s, 0), np.maximum(s - t, 0), (t >= s).astype(np.float32),
                       (t <= s).astype(np.float32), zero + t + 1, zero + 128 - t], 1).astype(np.float32)
    far = np.stack([np.where(t >= s, 0, 1e30), np.where(t <= s, 0, 1e30)], 1).astype(np.float32)
    rows = np.arange(2048, dtype=np.float32) // 64
    grid_cols = np.arange(2048, dtype=np.float32) % 64
    inv = (10000.0 ** (-np.arange(32, dtype=np.float64) / 32)).astype(np.float32)
    ang = np.concatenate([rows[:, None] * inv, grid_cols[:, None] * inv], -1).astype(np.float64)
    rope = np.stack([np.cos(ang), np.sin(ang)], 1).astype(np.float32)
    return {"ident": np.eye(128, dtype=np.float32), "shapes": shapes, "far": far,
            "cols": np.stack([127 - i, i], 1).astype(np.float32), "rope": rope}


def kernel(**inputs):
    import numpy as np
    import concourse.bacc as bacc
    from concourse import mybir as mb
    from concourse.bass_utils import run_bass_kernel_spmd as run

    nc = bacc.Bacc("TRN2", target_bir_lowering=False, num_devices=1)
    arrays, args = {}, {}
    given = {name: np.ascontiguousarray(inputs[name]) for name in _INS}
    for name, value in {**given, **shape_constants()}.items():
        arrays[f"in_{name}"] = value
        args[name] = nc.dram_tensor(f"in_{name}", value.shape, mb.dt.from_np(value.dtype), kind="ExternalInput").ap()
    outs = {name: nc.dram_tensor(f"out_{name}", shape, mb.dt.float32, kind="ExternalOutput").ap() for name, shape in _OUTS}
    build(nc, args, outs)
    r = run(nc, [arrays], core_ids=[0])
    return tuple(r.results[0][f"out_{name}"] for name, _ in _OUTS)
```

```python
from contextlib import ExitStack

import concourse.bass as bass
from concourse import mybir

ALU = mybir.AluOpType
ACT = mybir.ActivationFunctionType
F32 = mybir.dt.float32
F32R = mybir.dt.float32r
AX_X = mybir.AxisListType.X

P = 128
D = 1024
KT = D // P
HEADS = 4
HD = 128
W = HEADS * HD
AUG = HD + 1
CTX = 256
LAT = 2048
CTX_TILES = CTX // P
TILES = (CTX + LAT) // P
PAIRS = TILES // 2
TOKENS = CTX + LAT
FF = 4 * D
FF_CHUNKS = FF // P
BLK = 512
MOD = 6 * D
EPS = 1e-6
KSCALE = HD ** -0.5
STATE = W + HEADS * AUG
U, EN, WE, MX, WI = range(5)
ROWS = 8
FAR = 1e30


def over_tiles(engine, body):
    for j in range(2):
        body(0, j, 0)
    with engine.Fori(1, PAIRS) as pair:
        for j in range(2):
            body(pair, j, 1)


def over_steps(engine, stages):
    def step(t, pair, j):
        for lag, stage in stages:
            if isinstance(t, int):
                if 0 <= t - lag < TILES:
                    stage(t - lag, (t - lag) // 2, (t - lag) % 2)
            else:
                stage(t - lag, pair - (lag - j + 1) // 2, (j - lag) % 2)

    for t in range(4):
        step(t, None, None)
    with engine.Fori(2, PAIRS) as pair:
        for j in range(2):
            step(2 * pair + j, pair, j)
    for t in range(TILES, TILES + 2):
        step(t, None, None)


def seq_of(t):
    return 0 if isinstance(t, int) and t < CTX_TILES else 1


def reuses(t):
    return not isinstance(t, int) or t >= 2


def build(nc, a, out):
    with ExitStack() as ctx:
        def dram(name, shape):
            return nc.dram_tensor(name, shape, F32).ap()

        s = {
            "mod": dram("mod_rows", [2, MOD]),
            "qkv": dram("qkv_rows", [TOKENS, 4 * W]),
            "mqk": dram("mqk_rows", [TOKENS + 4, 2 * W]),
            "mqk2": dram("conv_rows", [TOKENS, 2 * W]),
            "gate": dram("gate_rows_out", [TOKENS, D]),
            "rows": dram("scalar_rows", [5 * ROWS, TOKENS]),
            "mdec": dram("backward_decays", [TILES, HEADS]),
            "bst": dram("backward_states", [TILES, P, STATE]),
            "y": dram("mixed_rows", [TOKENS, D]),
            "x1": dram("residual_rows", [TOKENS, D]),
            "h2T": dram("mlp_in", [P, 2, KT, TOKENS]),
        }
        ident = ctx.enter_context(nc.sbuf_tensor("ident", [P, P], F32))
        with ExitStack() as c2:
            def sb(name, shape):
                return c2.enter_context(nc.sbuf_tensor(name, shape, F32))

            keep = {
                "ident": ident,
                "grows": sb("grows", [P, TOKENS]),
                "mret": sb("mret", [P, HEADS, P]),
                "qdec": sb("qdec", [P, 2, HEADS, P]),
                "kdec": sb("kdec", [P, 8]),
                "cdec": sb("cdec", [P, 8]),
            }
            modulation(nc, a, s, keep)
            projection(nc, a, s, keep)
            gate_rows(nc, a, s, keep, out)
            backward_scan(nc, a, s, keep, out)
            forward_scan(nc, a, s, keep, out)
        keep = {"ident": ident}
        output(nc, a, s, keep)
        mlp(nc, a, s, keep, out)


class Scope:

    def __init__(self, nc, ctx, name):
        self.nc, self.ctx, self.name, self.sems = nc, ctx, name, []
        ctx.callback(self.close)

    def sb(self, name, shape, dtype=F32):
        return self.ctx.enter_context(self.nc.sbuf_tensor(f"{self.name}_{name}", shape, dtype))

    def ps(self, name, shape):
        return self.ctx.enter_context(self.nc.psum_tensor(f"{self.name}_{name}", shape, F32))

    def sem(self, name):
        self.sems.append(self.nc.alloc_semaphore(name=f"{self.name}_{name}"))
        return self.sems[-1]

    def close(self):
        self.nc.clear_and_free_semaphores(self.sems)
        self.nc.all_engine_barrier()


def product(pe, acc, n, left, right):
    for k in range(n):
        pe.matmul(acc, left(1, k), right(0, k), start=(k == 0), stop=False)
        pe.matmul(acc, left(0, k), right(1, k), start=False, stop=False)
        last = pe.matmul(acc, left(0, k), right(0, k), start=False, stop=(k == n - 1))
    return last


def modulation(nc, a, s, keep):
    NB = MOD // BLK
    RING = 4
    with ExitStack() as ctx:
        m = Scope(nc, ctx, "mod")
        cond = m.sb("cond", [P, 2, KT])
        sig = m.sb("sig", [P, 2, KT])
        act_c = m.sb("act", [P, 2, KT])
        w = m.sb("w", [P, RING, KT, BLK])
        bias = m.sb("bias", [2, RING, BLK])
        row = m.sb("row", [2, 2, BLK])
        acc = m.ps("acc", [P, 2, BLK])
        cond_loaded, sig_done, silu_done = m.sem("cond_loaded"), m.sem("sig_done"), m.sem("silu_done")
        w_loaded = [m.sem(f"w_loaded{j}") for j in range(RING)]
        product, row_ready = m.sem("product"), m.sem("row_ready")
        row_stored = [m.sem(f"row_stored{j}") for j in range(2)]
        ident_loaded = m.sem("ident_loaded")
        w_ada = a["w_ada"][0].rearrange("(p k) n -> p k n", k=KT)
        block = ctx.enter_context(nc.Block())

        def over_blocks(engine, body):
            for j in range(RING):
                body(0, j)
            with engine.Fori(1, NB // RING) as r:
                for j in range(RING):
                    body(r, j)

        @block.sync
        def _(sp):
            sp.dma_start(cond[:, 0, :], a["c_ctx"].rearrange("(p k) -> p k", k=KT)).then_inc(cond_loaded, 16)
            sp.dma_start(cond[:, 1, :], a["c"][0].rearrange("(p k) -> p k", k=KT)).then_inc(cond_loaded, 16)
            sp.dma_start(keep["ident"][:, :], a["ident"]).then_inc(ident_loaded, 16)

            def load(r, j):
                n = r * RING + j
                if not (isinstance(r, int) and r == 0):
                    sp.wait_ge(row_ready, n - RING + 1)
                sp.dma_start(w[:, j, :, :], w_ada[:, :, bass.ts(n, BLK)]).then_inc(w_loaded[j], 16)
                sp.dma_start(bias[:, j, :], a["b_ada"][0:1, bass.ts(n, BLK)].to_broadcast([2, BLK])
                             ).then_inc(w_loaded[j], 16)

            over_blocks(sp, load)
            sp.wait_ge(ident_loaded, 16)

        @block.scalar
        def _(act):
            act.wait_ge(cond_loaded, 32)
            act.activation(sig[:, :, :], cond[:, :, :], ACT.Sigmoid).then_inc(sig_done, 1)

        @block.tensor
        def _(pe):
            pe.wait_ge(silu_done, 1)

            def multiply(r, j):
                n = r * RING + j
                pe.wait_ge(w_loaded[j], 32 * (r + 1))
                if not (isinstance(r, int) and n < 2):
                    pe.wait_ge(row_ready, n - 1)
                for k in range(KT):
                    last = pe.matmul(acc[0:2, j % 2, :], act_c[:, :, k], w[:, j, k, :], start=(k == 0), stop=(k == KT - 1))
                last.then_inc(product, 1)

            over_blocks(pe, multiply)

        @block.vector
        def _(dve):
            dve.wait_ge(sig_done, 1)
            dve.tensor_tensor(act_c[:, :, :], cond[:, :, :], sig[:, :, :], ALU.mult).then_inc(silu_done, 1)

            def add_bias(r, j):
                n = r * RING + j
                dve.wait_ge(product, n + 1)
                if not (isinstance(r, int) and n < 2):
                    dve.wait_ge(row_stored[j % 2], 16 * (2 * r + j // 2))
                dve.tensor_tensor(row[:, j % 2, :], acc[0:2, j % 2, :], bias[:, j, :], ALU.add).then_inc(row_ready, 1)

            over_blocks(dve, add_bias)

        @block.gpsimd
        def _(pool):
            def store(r, j):
                n = r * RING + j
                pool.wait_ge(row_ready, n + 1)
                pool.dma_start(s["mod"][:, bass.ts(n, BLK)], row[:, j % 2, :]).then_inc(row_stored[j % 2], 16)

            over_blocks(pool, store)
            for j in range(2):
                pool.wait_ge(row_stored[j], 16 * NB // 2)


def load_modulation(sp, s, a, shift, scale, shift_at, scale_at, seq, loaded):
    sp.dma_start(shift[:, :], s["mod"][seq:seq + 1, shift_at * D:(shift_at + 1) * D].to_broadcast([P, D])
                 ).then_inc(loaded, 16)
    sp.dma_start(scale[:, :], s["mod"][seq:seq + 1, scale_at * D:(scale_at + 1) * D].to_broadcast([P, D])
                 ).then_inc(loaded, 16)


def projection(nc, a, s, keep):
    ident = keep["ident"]
    HALF = TILES // 2
    TRIPLES = HALF // 3
    RV, RQ, RK, MQ, MK, RG, MO, MV = range(8)
    COLUMN = {RQ: 0, RK: 1, RV: 2, RG: 3, MQ: 4, MK: 5, MV: 6, MO: 7}
    BLOCKS = range(8)
    ON_DVE = [RQ, RK, RG, MO]
    PIECES = 4
    PK = KT // PIECES
    with ExitStack() as ctx:
        m = Scope(nc, ctx, "proj")
        hT = m.sb("hT", [P, 2, HALF, KT, P], F32R)
        w = m.sb("w", [P, 2, 2, KT, BLK], F32R)
        raw = m.sb("raw", [P, 2, PK, BLK])
        wg16 = m.sb("wg16", [P, KT, 16])
        wg = m.sb("wg", [P, 2, KT, P], F32R)
        gbias = m.sb("gbias", [P, 1])
        x = m.sb("x", [P, 2, D])
        stage = m.sb("stage", [P, 3, BLK])
        pre = m.sb("pre", [P, 3, BLK])
        gnorm = m.sb("gnorm", [P, D])
        shift = m.sb("shift", [P, D])
        scale = m.sb("scale", [P, D])
        rope = m.sb("rope", [P, HALF, 2, HD // 2])
        turn = m.sb("turn", [P, 2, HEADS, HD // 2])
        ssq = m.sb("ssq", [P, 2])
        mean = m.sb("mean", [P, 2])
        rstd = m.sb("rstd", [P, 2])
        power = m.sb("power", [P, 1])
        acc = m.ps("acc", [P, 3, BLK])
        tps = m.ps("tps", [P, KT, P])
        gps = m.ps("gps", [P, BLK])
        junk = m.ps("junk", [P, D])

        wg_loaded, gb_loaded = m.sem("wg_loaded"), m.sem("gb_loaded")
        gb_zero, wg_zero, wg_hi, wg_ready = m.sem("gb_zero"), m.sem("wg_zero"), m.sem("wg_hi"), m.sem("wg_ready")
        raw_loaded = [m.sem(f"raw_loaded{i}") for i in range(2)]
        w_hi, w_lo = m.sem("w_hi"), m.sem("w_lo")
        mod_loaded, gnorm_loaded, rope_loaded = m.sem("mod_loaded"), m.sem("gnorm_loaded"), m.sem("rope_loaded")
        scale_ready, power_ready = m.sem("scale_ready"), m.sem("power_ready")
        x_loaded = [m.sem(f"x_loaded{j}") for j in range(2)]
        ssq_ready, mean_ready, rstd_ready = m.sem("ssq_ready"), m.sem("mean_ready"), m.sem("rstd_ready")
        scaled, h_ready = m.sem("scaled"), m.sem("h_ready")
        transposed, hT_hi, hT_lo = m.sem("transposed"), m.sem("hT_hi"), m.sem("hT_lo")
        done, gate_done, grow_ready = m.sem("done"), m.sem("gate_done"), m.sem("grow_ready")
        acc_read, turned, part_done, gated = m.sem("acc_read"), m.sem("turned"), m.sem("part_done"), m.sem("gated")
        staged = m.sem("staged")
        stored = [m.sem(f"stored{i}") for i in range(3)]
        zero_stored = m.sem("zero_stored")
        w_in = a["w_in"][0].rearrange("(k p) n -> p k n", p=P)
        block = ctx.enter_context(nc.Block())

        def nth(half, b, t):
            return half * (len(BLOCKS) - 1) * HALF + HALF * b + t

        def nth_staged(half, b, t):
            return half * (len(ON_DVE) - 1) * HALF + HALF * ON_DVE.index(b) + t

        def slot_uses(half, b, triple):
            return half * (len(BLOCKS) - 1) * TRIPLES + TRIPLES * b + triple

        def over_triples(engine, half, body):
            if half == 0:
                for i in range(3):
                    body(i, i, 0)
            with engine.Fori(TRIPLES * half + (1 - half), TRIPLES * (half + 1)) as triple:
                for i in range(3):
                    body(3 * triple + i, i, triple)

        @block.sync
        def _(sp):
            def load_x(t):
                if t >= 2:
                    sp.wait_ge(transposed, t - 1)
                src = a["x_prompt"][0, t * P:(t + 1) * P, :] if t < CTX_TILES else \
                    a["x_sample"][0, (t - CTX_TILES) * P:(t - CTX_TILES + 1) * P, :]
                sp.dma_start(x[:, t % 2, :], src).then_inc(x_loaded[t % 2], 16)

            def load_mod(seq):
                if seq:
                    sp.wait_ge(h_ready, CTX_TILES)
                load_modulation(sp, s, a, shift, scale, 0, 1, seq, mod_loaded)

            def store(half, b, t, i):
                q = nth(half, b, t)
                if b in ON_DVE:
                    sp.wait_ge(staged, nth_staged(half, b, t) + 1)
                else:
                    sp.wait_ge(acc_read, q + 1)
                rows = bass.ts(t, P)
                if b in (RQ, RK, RV):
                    dst = s["qkv"][rows, COLUMN[b] * W:(COLUMN[b] + 1) * W]
                elif b == MV:
                    dst = s["qkv"][rows, 3 * W:4 * W]
                elif b in (RG, MO):
                    dst = s["gate"][rows, (b == MO) * W:((b == MO) + 1) * W]
                else:
                    context = isinstance(t, int) and t < CTX_TILES
                    dst = s["mqk"][bass.ds(t * P + (1 if context else 3), P), (b - MQ) * W:(b - MQ + 1) * W]
                sp.dma_start(dst, stage[:, i, :]).then_inc(stored[i], 16)

            load_x(0)
            load_mod(0)
            sp.dma_start(gnorm[:, :], a["norm1_g"].to_broadcast([P, D])).then_inc(gnorm_loaded, 16)
            load_x(1)
            sp.dma_start(wg16[:, :, :], w_in[:, :, len(BLOCKS) * BLK:len(BLOCKS) * BLK + 16]).then_inc(wg_loaded, 16)
            sp.dma_start(rope[:, CTX_TILES:HALF, :, :], a["rope"][0:(HALF - CTX_TILES) * P].rearrange("(t p) a e -> p t a e", p=P)
                         ).then_inc(rope_loaded, 16)
            for half in range(2):
                for t in range(half * HALF, (half + 1) * HALF):
                    if t == CTX_TILES:
                        load_mod(1)
                    if t not in (0, 1, HALF, HALF + 1):
                        load_x(t)
                    if t - half * HALF >= 2:
                        store(half, RV, t - 2, (t - 2) % 3)
                for t in range((half + 1) * HALF - 2, (half + 1) * HALF):
                    store(half, RV, t, t % 3)
                if half == 0:
                    sp.wait_ge(scale_ready, 2)
                    sp.dma_start(gnorm[:, 0:W], a["ret_gn_g"].to_broadcast([P, W])).then_inc(gnorm_loaded, 16)
                    sp.dma_start(gnorm[:, W:D], a["mlstm_gn_g"].to_broadcast([P, W])).then_inc(gnorm_loaded, 16)
                else:
                    sp.wait_ge(staged, nth_staged(0, RK, HALF - 1) + 1)
                    sp.dma_start(rope[:, :, :, :], a["rope"][(HALF - CTX_TILES) * P:].rearrange("(t p) a e -> p t a e", p=P)
                                 ).then_inc(rope_loaded, 16)
                for b in BLOCKS[1:]:
                    if half == 0 and b == BLOCKS[-1]:
                        load_x(HALF)
                        load_x(HALF + 1)
                    over_triples(sp, half, lambda t, i, triple: store(half, b, t, i))
            for i in range(3):
                sp.wait_ge(stored[i], 16 * TILES * len(BLOCKS) // 3)

        @block.scalar
        def _(act):
            def square(t):
                act.wait_ge(x_loaded[t % 2], 16 * (t // 2 + 1))
                if t:
                    act.wait_ge(ssq_ready, t)
                if t >= 2:
                    act.wait_ge(mean_ready, t - 1)
                act.activation(junk[:, :], x[:, t % 2, :], ACT.Square, accum_out=ssq[:, t % 2:t % 2 + 1]).then_inc(ssq_ready, 1)

            def evacuate(half, b, t, i, triple):
                q = nth(half, b, t)
                act.wait_ge(done, q + 1)
                if b in ON_DVE:
                    z = nth_staged(half, b, t)
                    if not (isinstance(z, int) and z < 3):
                        act.wait_ge(staged, z - 2)
                    if b == RG:
                        act.wait_ge(stored[i], 16 * slot_uses(half, b, triple))
                        act.activation(stage[:, i, :], acc[:, i, :], ACT.Copy)
                    f = ACT.Copy if b in (RQ, RK) else ACT.Sigmoid
                    act.activation(pre[:, i, :], acc[:, i, :], f, scale=KSCALE if b == RK else 1.0).then_inc(acc_read, 1)
                else:
                    act.wait_ge(stored[i], 16 * slot_uses(half, b, triple))
                    act.activation(stage[:, i, :], acc[:, i, :], ACT.Copy).then_inc(acc_read, 1)

            def gate_rows_out(half):
                act.wait_ge(gb_loaded, 64)
                for g in range(TRIPLES):
                    n = half * TRIPLES + g
                    act.wait_ge(gate_done, n + 1)
                    act.activation(keep["grows"][:, n * 3 * P:(n + 1) * 3 * P], gps[:, 0:3 * P], ACT.Identity,
                                   bias=gbias[:, 0:1]).then_inc(grow_ready, 1)

            for half in range(2):
                first, end = half * HALF, (half + 1) * HALF
                if half == 0:
                    square(first)
                for t in range(first, end):
                    if t + 1 < end:
                        square(t + 1)
                    act.wait_ge(transposed, t + 1)
                    if half:
                        act.wait_ge(done, nth(0, MV, t - HALF) + 1)
                    act.activation(hT[:, 0, t - first, :, :], tps[:, :, :], ACT.Copy).then_inc(hT_hi, 1)
                    if t > first:
                        evacuate(half, RV, t - 1, (t - 1) % 3, (t - 1) // 3)
                evacuate(half, RV, end - 1, (end - 1) % 3, (end - 1) // 3)
                for b in BLOCKS[1:]:
                    if half == 0 and b == BLOCKS[-1]:
                        square(HALF)
                    over_triples(act, half, lambda t, i, triple: evacuate(half, b, t, i, triple))
                    if b == RQ:
                        gate_rows_out(half)

        @block.tensor
        def _(pe):
            def transpose(t):
                pe.wait_ge(h_ready, t + 1)
                if t:
                    pe.wait_ge(hT_lo, t)
                for k in range(KT):
                    last = pe.transpose(tps[:, k, :], x[:, t % 2, k * P:(k + 1) * P], ident[:, :])
                last.then_inc(transposed, 1)

            def multiply(half, b, t, j):
                q = nth(half, b, t)
                if half or b is not RV or t >= 3:
                    pe.wait_ge(acc_read, q - 2)
                last = product(pe, acc[:, t % 3, :], KT, lambda part, k: hT[:, part, t % HALF, k, :],
                               lambda part, k: w[:, j, part, k, :])
                last.then_inc(done, 1)

            for half in range(2):
                tiles = range(half * HALF, (half + 1) * HALF)
                transpose(tiles[0])
                for t in tiles:
                    if t + 1 in tiles:
                        transpose(t + 1)
                    pe.wait_ge(hT_lo, t + 1)
                    if t == tiles[0]:
                        pe.wait_ge(w_lo, PIECES * (half * len(BLOCKS) + 1))
                    multiply(half, 0, t, 0)
                pe.wait_ge(w_lo, PIECES * (half * len(BLOCKS) + 2))
                for t in tiles:
                    multiply(half, 1, t, 1)
                pe.wait_ge(wg_ready, 1)
                for g in range(TRIPLES):
                    n = half * TRIPLES + g
                    if n:
                        pe.wait_ge(grow_ready, n)
                    last = product(pe, gps[:, 0:3 * P].rearrange("p (t c) -> p t c", t=3), KT, lambda part, k: wg[:, part, k, :],
                                   lambda part, k: hT[:, part, 3 * g:3 * g + 3, k, :])
                    last.then_inc(gate_done, 1)
                with pe.Fori(1, len(BLOCKS) // 2) as pair:
                    for j in range(2):
                        pe.wait_ge(w_lo, PIECES * (half * len(BLOCKS) + 2 * pair + j + 1))
                        for t in tiles:
                            multiply(half, 2 * pair + j, t, j)

        @block.vector
        def _(dve):
            dve.memset(wg[:, :, :, :].bitcast(F32), 0.0).then_inc(wg_zero, 1)
            dve.wait_ge(wg_zero, 1)
            dve.wait_ge(wg_loaded, 16)
            for d in range(2):
                for f in range(2):
                    at, src = 64 * f + 32 * d, wg16[:, :, 8 * d + 4 * f:8 * d + 4 * f + 4]
                    dve.tensor_copy(wg[:, 0, :, at:at + 4], src).then_inc(wg_hi, 1)
                    dve.wait_ge(wg_hi, 2 * d + f + 1)
                    last = dve.tensor_tensor(wg[:, 1, :, at:at + 4], src, wg[:, 0, :, at:at + 4].bitcast(F32), ALU.subtract)
            last.then_inc(wg_ready, 1)

            def normalise(t):
                j = t % 2
                seq = int(t >= CTX_TILES)
                if t in (0, CTX_TILES):
                    dve.wait_ge(mod_loaded, 32 * (seq + 1))
                    dve.wait_ge(gnorm_loaded, 16)
                    dve.scalar_tensor_tensor(out=scale[:, :], in0=scale[:, :], scalar=1.0, in1=gnorm[:, :],
                                             op0=ALU.add, op1=ALU.mult).then_inc(scale_ready, 1)
                    dve.wait_ge(scale_ready, seq + 1)
                dve.wait_ge(ssq_ready, t + 1)
                dve.tensor_scalar(mean[:, j:j + 1], ssq[:, j:j + 1], 1.0 / D, EPS, ALU.mult, ALU.add).then_inc(mean_ready, 1)
                dve.wait_ge(rstd_ready, t + 1)
                dve.scalar_tensor_tensor(out=x[:, j, :], in0=x[:, j, :], scalar=rstd[:, j:j + 1], in1=scale[:, :],
                                         op0=ALU.mult, op1=ALU.mult).then_inc(scaled, 1)
                dve.wait_ge(scaled, t + 1)
                dve.tensor_tensor(x[:, j, :], x[:, j, :], shift[:, :], ALU.add).then_inc(h_ready, 1)

            def finish(half, b, t, i, triple):
                q, z = nth(half, b, t), nth_staged(half, b, t)
                dve.wait_ge(acc_read, q + 1)
                if b != RG:
                    dve.wait_ge(stored[i], 16 * slot_uses(half, b, triple))
                if b in (RQ, RK) and isinstance(t, int) and t < CTX_TILES:
                    dve.tensor_copy(stage[:, i, :], pre[:, i, :]).then_inc(staged, 1)
                elif b in (RQ, RK):
                    v = pre[:, i, :].rearrange("p (h b e) -> p h b e", h=HEADS, b=2)
                    o = stage[:, i, :].rearrange("p (h b e) -> p h b e", h=HEADS, b=2)
                    row = rope[:, bass.ds(t - half * HALF, 1), :, :].rearrange("p o a e -> p (o a) e")
                    cos = row[:, 0:1, :].to_broadcast([P, HEADS, HD // 2])
                    sin = row[:, 1:2, :].to_broadcast([P, HEADS, HD // 2])
                    latents = HALF - CTX_TILES
                    r = (b == RK) * latents + (t - CTX_TILES) if half == 0 else 2 * latents + (b == RK) * HALF + (t - HALF)
                    dve.wait_ge(staged, z)
                    for side in range(2):
                        one, two = (cos, sin) if side == 0 else (sin, cos)
                        dve.tensor_tensor(turn[:, 0, :, :], v[:, :, 0, :], one, ALU.mult)
                        dve.tensor_tensor(turn[:, 1, :, :], v[:, :, 1, :], two, ALU.mult).then_inc(turned, 1)
                        dve.wait_ge(turned, r * 2 + side + 1)
                        last = dve.tensor_tensor(o[:, :, side, :], turn[:, 0, :, :], turn[:, 1, :, :],
                                                 ALU.subtract if side == 0 else ALU.add)
                        if side == 0:
                            last.then_inc(part_done, 1)
                            dve.wait_ge(part_done, r + 1)
                        else:
                            last.then_inc(staged, 1)
                elif b == RG:
                    dve.tensor_tensor(stage[:, i, :], stage[:, i, :], pre[:, i, :], ALU.mult).then_inc(gated, 1)
                    dve.wait_ge(gated, t + 1)
                    dve.tensor_tensor(stage[:, i, :], stage[:, i, :], gnorm[:, 0:W], ALU.mult).then_inc(staged, 1)
                else:
                    dve.tensor_tensor(stage[:, i, :], pre[:, i, :], gnorm[:, W:D], ALU.mult).then_inc(staged, 1)

            for half in range(2):
                first, end = half * HALF, (half + 1) * HALF
                if half == 0:
                    normalise(first)
                for t in range(first, end):
                    if t + 1 < end:
                        normalise(t + 1)
                    dve.wait_ge(hT_hi, t + 1)
                    if t == HALF - 1:
                        dve.wait_ge(zero_stored, 48)
                    dve.tensor_tensor(hT[:, 1, t - first, :, :], tps[:, :, :], hT[:, 0, t - first, :, :].bitcast(F32),
                                      ALU.subtract).then_inc(hT_lo, 1)
                dve.wait_ge(rope_loaded, 16 * (half + 1))
                for b in ON_DVE:
                    if half == 0 and b == RG:
                        dve.wait_ge(gnorm_loaded, 48)
                    over_triples(dve, half, lambda t, i, triple: finish(half, b, t, i, triple))
                if half == 0:
                    normalise(HALF)

        @block.gpsimd
        def _(pool):
            pool.memset(power[:, :], -0.5).then_inc(power_ready, 1)
            pool.memset(gbias[:, :], 0.0).then_inc(gb_zero, 1)
            pool.memset(hT[0:4, 1, HALF - 1, :, :].bitcast(F32), 0.0).then_inc(gb_zero, 1)
            pool.wait_ge(power_ready, 1)

            def weights(half, b, between=()):
                g = half * len(BLOCKS) + b
                if g >= 2:
                    pool.wait_ge(done, HALF * (g - 1))
                col = COLUMN[b] * BLK
                for c in range(PIECES):
                    n = PIECES * g + c
                    if n >= 2:
                        pool.wait_ge(w_lo, n - 1)
                    pool.dma_start(raw[:, c % 2, :, :], w_in[:, PK * c:PK * (c + 1), col:col + BLK]).then_inc(raw_loaded[c % 2], 16)
                    if c:
                        split(g, c - 1)
                    if c < len(between):
                        root(between[c])
                split(g, PIECES - 1)

            def split(g, c):
                n = PIECES * g + c
                pool.wait_ge(raw_loaded[c % 2], 16 * (n // 2 + 1))
                k = slice(PK * c, PK * (c + 1))
                pool.tensor_copy(w[:, g % 2, 0, k, :], raw[:, c % 2, :, :]).then_inc(w_hi, 1)
                pool.wait_ge(w_hi, n + 1)
                pool.tensor_tensor(w[:, g % 2, 1, k, :], raw[:, c % 2, :, :], w[:, g % 2, 0, k, :].bitcast(F32), ALU.subtract
                                   ).then_inc(w_lo, 1)

            def root(t):
                j = t % 2
                pool.wait_ge(mean_ready, t + 1)
                pool.tensor_tensor(rstd[:, j:j + 1], mean[:, j:j + 1], power[:, 0:1], ALU.pow).then_inc(rstd_ready, 1)

            weights(0, 0)
            root(0)
            pool.wait_ge(gb_zero, 2)
            for d in range(2):
                for f in range(2):
                    at = 64 * f + 32 * d
                    pool.dma_start(gbias[at:at + 4, :],
                                   a["mlstm_gate_bias"][0, d, f, :].rearrange("(h o) -> h o", o=1)).then_inc(gb_loaded, 16)
            zero = hT[0:4, 1, HALF - 1, :, :].bitcast(F32).rearrange("p k n -> p (k n)")
            pool.dma_start(s["mqk"][0:1, :], zero[0:1, :]).then_inc(zero_stored, 16)
            pool.dma_start(s["mqk"][CTX + 1:CTX + 3, :], zero[1:3, :]).then_inc(zero_stored, 16)
            pool.dma_start(s["mqk"][TOKENS + 3:TOKENS + 4, :], zero[3:4, :]).then_inc(zero_stored, 16)
            pool.wait_ge(zero_stored, 48)
            for half in range(2):
                tiles = range(half * HALF, (half + 1) * HALF)
                weights(half, 1, tiles[1:1 + PIECES])
                for t in tiles[1 + PIECES:]:
                    root(t)
                for b in BLOCKS[2:]:
                    weights(half, b)
                if half == 0:
                    root(HALF)
                    weights(1, 0)


def gate_rows(nc, a, s, keep, out):
    G = 64
    grows = keep["grows"]
    with ExitStack() as ctx:
        m = Scope(nc, ctx, "gates")
        absf = m.sb("absf", [G, TOKENS])
        logf = m.sb("logf", [G, TILES, P])
        logi = m.sb("logi", [G, TILES, P])
        ping = m.sb("ping", [G, TILES, P])
        pong = m.sb("pong", [G, TILES, P])
        cum_b = m.sb("cum_b", [G, TILES, P])
        u = m.sb("u", [G, TILES, P])
        final = m.sb("final", [G, 4, TILES, P])
        ends = m.sb("ends", [G, 2, TILES])
        m_in = m.sb("m_in", [G, TILES + 1])
        m_ctx = m.sb("m_ctx", [G, 1])
        m_chunk = m.sb("m_chunk", [G, TILES])
        logit = m.sb("logit", [P, 8])
        decay_abs = m.sb("decay_abs", [P, 8])
        decay_min = m.sb("decay_min", [P, 8])
        shapes = m.sb("shapes", [P, 6, P])
        cols = m.sb("cols", [P, 2])
        tables = m.sb("tables", [P, 2, HEADS, P])
        loaded, m_zero, m_loaded = m.sem("loaded"), m.sem("m_zero"), m.sem("m_loaded")
        act_step, dve_step = m.sem("act_step"), m.sem("dve_step")
        stored = m.sem("stored")
        block = ctx.enter_context(nc.Block())
        F0, B0 = slice(0, 32), slice(32, 64)
        DV_LG = 2
        DV_LOGF = 5
        DV_CUM = DV_LOGF + 2 * 7
        DV_U = DV_CUM + 2
        DV_MAX = DV_U + 2 * 7
        DV_MPREV = DV_MAX + 4 + TILES + 2
        DV_FINAL = DV_MPREV + 4


        @block.sync
        def _(sp):
            sp.dma_start(logit[:, :], a["ret_decay_logit"].rearrange("o d h -> o (d h)").to_broadcast([P, 8])
                         ).then_inc(loaded, 16)
            sp.dma_start(shapes[:, :, :], a["shapes"]).then_inc(loaded, 16)
            sp.dma_start(cols[:, :], a["cols"]).then_inc(loaded, 16)
            sp.wait_ge(m_zero, 1)
            for d in range(2):
                sp.dma_start(m_in[32 * d:32 * d + 4, CTX_TILES:CTX_TILES + 1],
                             a["state_mlstm_m"][0, 0, d, :].rearrange("(h o) -> h o", o=1)).then_inc(m_loaded, 16)

        @block.scalar
        def _(act):
            fr = grows[64:128, :]
            act.activation(absf[:, :], fr, ACT.Abs).then_inc(act_step, 1)
            act.wait_ge(act_step, 1)
            act.activation(absf[:, :], absf[:, :], ACT.Exp, scale=-1.0).then_inc(act_step, 1)
            act.wait_ge(act_step, 2)
            act.activation(absf[:, :], absf[:, :], ACT.Ln, bias=1.0).then_inc(act_step, 1)
            act.wait_ge(loaded, 48)
            act.activation(decay_abs[:, :], logit[:, :], ACT.Abs).then_inc(act_step, 1)
            act.wait_ge(act_step, 4)
            act.activation(decay_abs[:, :], decay_abs[:, :], ACT.Exp, scale=-1.0).then_inc(act_step, 1)
            act.wait_ge(act_step, 5)
            act.activation(decay_abs[:, :], decay_abs[:, :], ACT.Ln, bias=1.0).then_inc(act_step, 1)
            lg = decay_min
            act.wait_ge(dve_step, DV_LG)
            for d in range(2):
                for h in range(HEADS):
                    g = lg[:, 4 * d + h:4 * d + h + 1]
                    act.activation(tables[:, d, h, :], shapes[:, d, :], ACT.Exp, scale=g).then_inc(act_step, 1)
                    act.activation(keep["qdec"][:, d, h, :], shapes[:, 4 + d, :], ACT.Exp, scale=g).then_inc(act_step, 1)
                    act.activation(keep["kdec"][:, 4 * d + h:4 * d + h + 1], cols[:, d:d + 1], ACT.Exp, scale=g
                                   ).then_inc(act_step, 1)
            act.activation(keep["cdec"][:, :], lg[:, :], ACT.Exp, scale=float(P)).then_inc(act_step, 1)
            act.wait_ge(dve_step, DV_FINAL)
            act.activation(final[:, 3, :, :], final[:, 3, :, :], ACT.Exp).then_inc(act_step, 1)
            act.activation(final[:, 1, :, :], final[:, 1, :, :], ACT.Exp, scale=-1.0).then_inc(act_step, 1)
            act.activation(final[:, 2, :, :], final[:, 2, :, :], ACT.Exp).then_inc(act_step, 1)

        @block.vector
        def _(dve):
            n = [0]

            def step(ins):
                ins.then_inc(dve_step, 1)
                n[0] += 1
                dve.wait_ge(dve_step, n[0])

            dve.wait_ge(act_step, 6)
            step(dve.tensor_scalar(decay_min[:, :], logit[:, :], 0.0, None, ALU.min))
            step(dve.tensor_tensor(decay_min[:, :], decay_min[:, :], decay_abs[:, :], ALU.subtract))
            assert n[0] == DV_LG
            fview = grows[64:128, :].rearrange("p (c t) -> p c t", t=P)
            iview = grows[0:64, :].rearrange("p (c t) -> p c t", t=P)
            lview = absf[:, :].rearrange("p (c t) -> p c t", t=P)
            step(dve.tensor_scalar(ping[:, :, :], fview, 0.0, None, ALU.min))
            step(dve.tensor_tensor(logf[F0, :, :], ping[F0, :, :], lview[F0, :, :], ALU.subtract))
            step(dve.tensor_tensor(logf[B0, :, ::-1], ping[B0, :, :], lview[B0, :, :], ALU.subtract))
            assert n[0] == DV_LOGF

            def scan(src, bufs, dst, op):
                cur = src
                for k in range(7):
                    reach = 1 << k
                    nxt = dst if k == 6 else bufs[k % 2]
                    step(dve.tensor_copy(nxt[:, :, 0:reach], cur[:, :, 0:reach]))
                    step(dve.tensor_tensor(nxt[:, :, reach:P], cur[:, :, reach:P], cur[:, :, 0:P - reach], op))
                    cur = nxt

            scan(logf, (ping, pong), cum_b, ALU.add)
            assert n[0] == DV_CUM
            dve.tensor_copy(logi[F0, :, :], iview[F0, :, :])
            step(dve.tensor_copy(logi[B0, :, ::-1], iview[B0, :, :]))
            step(dve.tensor_tensor(u[:, :, :], logi[:, :, :], cum_b[:, :, :], ALU.subtract))
            assert n[0] == DV_U
            top = final[:, 0, :, :]
            scan(u, (ping, pong), logf, ALU.max)
            assert n[0] == DV_MAX
            for e, src in enumerate((cum_b, logf)):
                step(dve.tensor_copy(ends[F0, e, :], src[F0, :, P - 1]))
                dve.tensor_copy(ends[B0, e, 0:CTX_TILES], src[B0, CTX_TILES - 1::-1, P - 1])
                step(dve.tensor_copy(ends[B0, e, CTX_TILES:TILES], src[B0, TILES - 1:CTX_TILES - 1:-1, P - 1]))
            dve.wait_ge(m_loaded, 32)
            for r in range(TILES):
                dst = m_ctx[:, 0:1] if r == CTX_TILES - 1 else m_in[:, r + 1:r + 2]
                step(dve.scalar_tensor_tensor(out=dst, in0=m_in[:, r:r + 1], scalar=ends[:, 1, r:r + 1],
                                              in1=ends[:, 0, r:r + 1], op0=ALU.max, op1=ALU.add))
            dve.tensor_copy(m_chunk[F0, :], m_in[F0, 0:TILES])
            step(dve.tensor_copy(m_chunk[B0, 0:CTX_TILES], m_in[B0, CTX_TILES - 1::-1]))
            step(dve.tensor_copy(m_chunk[B0, CTX_TILES:TILES], m_in[B0, TILES - 1:CTX_TILES - 1:-1]))
            assert n[0] == DV_MPREV
            mc = m_chunk[:, :].rearrange("p (c o) -> p c o", o=1).to_broadcast([G, TILES, P])
            step(dve.tensor_tensor(top, logf[:, :, :], mc, ALU.max))
            step(dve.tensor_tensor(final[:, 3, :, :], mc, top, ALU.subtract))
            step(dve.tensor_tensor(final[:, 1, :, :], cum_b[:, :, :], top, ALU.add))
            step(dve.tensor_tensor(final[:, 2, :, :], u[:, :, :], final[:, 0, :, P - 1:P].to_broadcast([G, TILES, P]),
                                   ALU.subtract))
            assert n[0] == DV_FINAL
            dve.wait_ge(act_step, 31)
            for d in range(2):
                step(dve.tensor_tensor(tables[:, d, :, :], tables[:, d, :, :],
                                       shapes[:, 2 + d:3 + d, :].to_broadcast([P, HEADS, P]), ALU.mult))
            step(dve.tensor_tensor(keep["mret"][:, :, :], tables[:, 0, :, :], tables[:, 1, :, :], ALU.add))
            dve.wait_ge(act_step, 34)
            for src, dst in ((u, ping), (final[:, 1, :, :], pong), (final[:, 2, :, :], cum_b),
                             (final[:, 0, :, :], logi), (final[:, 3, :, :], logf)):
                dve.tensor_copy(dst[F0, :, :], src[F0, :, :])
                step(dve.tensor_copy(dst[B0, :, ::-1], src[B0, :, :]))

        @block.gpsimd
        def _(pool):
            pool.memset(m_in[:, :], 0.0).then_inc(m_zero, 1)
            pool.wait_ge(dve_step, DV_FINAL + 3 + 5)
            for kind, src in ((U, ping), (EN, pong), (WE, cum_b), (MX, logi), (WI, logf)):
                for d in range(2):
                    at = kind * ROWS + 4 * d
                    pool.dma_start(s["rows"][at:at + 4, :], src[32 * d:32 * d + 4, :, :].rearrange("p c t -> p (c t)")
                                   ).then_inc(stored, 16)
            for d in range(2):
                pool.dma_start(out["m"][0, 0, d, :].rearrange("(h o) -> h o", o=1), m_ctx[32 * d:32 * d + 4, :]
                               ).then_inc(stored, 16)
            pool.dma_start(s["mdec"].rearrange("c (h o) -> h c o", o=1), logf[32:36, :, 0:1], allow_slow_non_contiguous=True
                           ).then_inc(stored, 16)
            pool.wait_ge(stored, 13 * 16)


def load_states(eng, a, state, d, loaded):
    eng.dma_start(state[:, 0:W].rearrange("p (h e) -> p h e", h=HEADS),
                  a["state_ret"][0, 0, d].rearrange("h p e -> p h e")).then_inc(loaded, 16)
    ml = state[:, W:STATE].rearrange("p (h e) -> p h e", h=HEADS)
    eng.dma_start(ml[:, :, 0:HD], a["state_mlstm_C"][0, 0, d].rearrange("h p e -> p h e")).then_inc(loaded, 16)
    eng.dma_start(ml[:, :, HD:AUG], a["state_mlstm_n"][0, 0, d].rearrange("h (p o) -> p h o", o=1),
                  allow_slow_non_contiguous=True).then_inc(loaded, 16)


def store_states(eng, out, state, d, stored):
    eng.dma_start(out["ret"][0, 0, d].rearrange("h p e -> p h e"),
                  state[:, 0:W].rearrange("p (h e) -> p h e", h=HEADS)).then_inc(stored, 16)
    ml = state[:, W:STATE].rearrange("p (h e) -> p h e", h=HEADS)
    eng.dma_start(out["C"][0, 0, d].rearrange("h p e -> p h e"), ml[:, :, 0:HD]).then_inc(stored, 16)
    eng.dma_start(out["n"][0, 0, d].rearrange("h (p o) -> p h o", o=1), ml[:, :, HD:AUG],
                  allow_slow_non_contiguous=True).then_inc(stored, 16)


def update_states(dve, old, new, kv_ret, kv_ml, cdec, mdec, done):
    for h in range(HEADS):
        dve.scalar_tensor_tensor(out=new[:, h * HD:(h + 1) * HD], in0=old[:, h * HD:(h + 1) * HD],
                                 scalar=cdec[:, h:h + 1], in1=kv_ret[:, h * HD:(h + 1) * HD], op0=ALU.mult, op1=ALU.add)
        at = slice(W + h * AUG, W + (h + 1) * AUG)
        last = dve.scalar_tensor_tensor(out=new[:, at], in0=old[:, at], scalar=mdec(h),
                                        in1=kv_ml(h), op0=ALU.mult, op1=ALU.add)
    last.then_inc(done, 1)


def backward_scan(nc, a, s, keep, out):
    ident = keep["ident"]
    with ExitStack() as ctx:
        m = Scope(nc, ctx, "bwd")
        convw = m.sb("convw", [P, 3, 2 * W])
        kv = m.sb("kv", [P, 2, 2, W])
        v1 = m.sb("v1", [P, 2, HEADS, AUG])
        xs = m.sb("xs", [P, 2, 3, 2 * W])
        werow = m.sb("werow", [HEADS, 2, P])
        mdec = m.sb("mdec", [P, 2, HEADS])
        sig = m.sb("sig", [P, 2, 2 * W])
        qk = m.sb("qk", [P, 2, 2 * W])
        kret = m.sb("kret", [P, 2, W])
        kml = m.sb("kml", [P, 2, W])
        state = m.sb("state", [P, 2, STATE])
        kvr_ps = m.ps("kvr", [P, 2, BLK])
        kvm_ps = m.ps("kvm", [P, 4, BLK])
        we_ps = m.ps("we", [P, 2, BLK])
        conv_loaded, ones_ready = m.sem("conv_loaded"), m.sem("ones_ready")
        loaded = [m.sem(f"loaded{j}") for j in range(2)]
        LOADS = 7
        side_taps, mid_tap, tap_sum, conv_sum = m.sem("side_taps"), m.sem("mid_tap"), m.sem("tap_sum"), m.sem("conv_sum")
        sig_ready, q_ready, k_ready = m.sem("sig_ready"), m.sem("q_ready"), m.sem("k_ready")
        kret_ready, we_ready, kml_ready = m.sem("kret_ready"), m.sem("we_ready"), m.sem("kml_ready")
        kv_done, updated = m.sem("kv_done"), m.sem("updated")
        zeroed, cached, ctx_stored = m.sem("zeroed"), m.sem("cached"), m.sem("ctx_stored")
        saved = [m.sem(f"saved{j}") for j in range(2)]
        qk_stored = [m.sem(f"qk_stored{j}") for j in range(2)]
        block = ctx.enter_context(nc.Block())

        def chunk(r, seq):
            return r * -1 + (TILES + CTX_TILES - 1 if seq else CTX_TILES - 1)

        def kvm(j, h):
            return kvm_ps[:, 2 * j + h // 2, (h % 2) * AUG:(h % 2 + 1) * AUG]

        @block.sync
        def _(sp):
            sp.dma_start(convw[:, :, :].rearrange("p j n -> p (j n)"),
                         a["conv_w"].rearrange("o j n -> o (j n)").to_broadcast([P, 6 * W])).then_inc(conv_loaded, 16)

            def load(pair, j, seq):
                r = 2 * pair + j
                c = chunk(r, seq)
                if seq:
                    sp.wait_ge(updated, r - 1)
                    sp.wait_ge(ctx_stored, 48)
                for i in range(3):
                    sp.dma_start(xs[:, j, i, :], s["mqk"][bass.ds(c * P + 2 * seq + i, P), :]).then_inc(loaded[j], 16)
                sp.dma_start(kv[:, j, :, :].rearrange("p a n -> p (a n)"), s["qkv"][bass.ts(c, P), W:3 * W]
                             ).then_inc(loaded[j], 16)
                sp.dma_start(v1[:, j, :, 0:HD], s["qkv"][bass.ts(c, P), 3 * W:4 * W].rearrange("p (h e) -> p h e", h=HEADS)
                             ).then_inc(loaded[j], 16)
                sp.dma_start(werow[:, j, :], s["rows"][WE * ROWS + 4:WE * ROWS + 8, bass.ts(c, P)]).then_inc(loaded[j], 16)
                sp.dma_start(mdec[:, j, :], s["mdec"][bass.ds(c, 1), :].to_broadcast([P, HEADS])).then_inc(loaded[j], 16)

            for j in range(2):
                load(0, j, 0)
            sp.wait_ge(updated, CTX_TILES)
            store_states(sp, out, state[:, 0, :], 1, ctx_stored)
            sp.wait_ge(ctx_stored, 48)
            sp.wait_ge(saved[0], 16)
            load_states(sp, a, state[:, 0, :], 1, cached)
            with sp.Fori(1, PAIRS) as pair:
                for j in range(2):
                    load(pair, j, 1)

        @block.scalar
        def _(act):
            def silu(pair, j, seq):
                r = 2 * pair + j
                act.wait_ge(conv_sum, r + 1)
                if seq:
                    act.wait_ge(q_ready, r - 1)
                act.activation(sig[:, j, :], xs[:, j, 1, :], ACT.Sigmoid).then_inc(sig_ready, 1)

            over_tiles(act, silu)

        @block.tensor
        def _(pe):
            def accumulate(pair, j, seq):
                r = 2 * pair + j
                pe.wait_ge(loaded[j], 16 * LOADS * (pair + 1))
                if seq:
                    pe.wait_ge(updated, r - 1)
                pe.wait_ge(kret_ready, r + 1)
                for h in range(HEADS):
                    pe.matmul(kvr_ps[:, j, h * HD:(h + 1) * HD], kret[:, j, h * HD:(h + 1) * HD],
                              kv[:, j, 1, h * HD:(h + 1) * HD], start=True, stop=True)
                pe.transpose(we_ps[:, j, 0:HEADS], werow[:, j, :], ident[0:HEADS, 0:HEADS]).then_inc(we_ready, 1)
                pe.wait_ge(kml_ready, r + 1)
                pe.wait_ge(ones_ready, 1)
                for h in range(HEADS):
                    last = pe.matmul(kvm(j, h), kml[:, j, h * HD:(h + 1) * HD], v1[:, j, h, :], start=True, stop=True)
                last.then_inc(kv_done, 1)

            over_tiles(pe, accumulate)

        @block.vector
        def _(dve):
            dve.memset(state[:, 0, :], 0.0).then_inc(zeroed, 1)
            dve.wait_ge(zeroed, 1)
            dve.wait_ge(conv_loaded, 16)

            def chunk_step(pair, j, seq):
                r = 2 * pair + j
                dve.wait_ge(loaded[j], 16 * LOADS * (pair + 1))
                dve.tensor_tensor(xs[:, j, 1, :], xs[:, j, 1, :], convw[:, 1, :], ALU.mult).then_inc(mid_tap, 1)
                dve.wait_ge(mid_tap, r + 1)
                dve.wait_ge(side_taps, 2 * r + 1)
                dve.tensor_tensor(xs[:, j, 1, :], xs[:, j, 0, :], xs[:, j, 1, :], ALU.add).then_inc(tap_sum, 1)
                dve.wait_ge(tap_sum, r + 1)
                dve.wait_ge(side_taps, 2 * r + 2)
                dve.tensor_tensor(xs[:, j, 1, :], xs[:, j, 1, :], xs[:, j, 2, :], ALU.add).then_inc(conv_sum, 1)
                dve.wait_ge(sig_ready, r + 1)
                dve.wait_ge(conv_sum, r + 1)
                dve.wait_ge(qk_stored[j], 16 * pair)
                dve.scalar_tensor_tensor(out=qk[:, j, W:2 * W], in0=xs[:, j, 1, W:2 * W], scalar=KSCALE,
                                         in1=sig[:, j, W:2 * W], op0=ALU.mult, op1=ALU.mult).then_inc(k_ready, 1)
                dve.wait_ge(we_ready, r + 1)
                dve.wait_ge(k_ready, r + 1)
                dve.tensor_tensor(kml[:, j, :].rearrange("p (h e) -> p h e", h=HEADS),
                                  qk[:, j, W:2 * W].rearrange("p (h e) -> p h e", h=HEADS),
                                  we_ps[:, j, 0:HEADS].rearrange("p (h o) -> p h o", o=1).to_broadcast([P, HEADS, HD]),
                                  ALU.mult).then_inc(kml_ready, 1)
                dve.tensor_tensor(qk[:, j, 0:W], xs[:, j, 1, 0:W], sig[:, j, 0:W], ALU.mult).then_inc(q_ready, 1)
                dve.wait_ge(kv_done, r + 1)
                if seq:
                    dve.wait_ge(cached, 48)
                    dve.wait_ge(updated, r)
                    dve.wait_ge(saved[1 - j], 16 * (pair + j))
                elif j == 1:
                    dve.wait_ge(updated, 1)
                    dve.wait_ge(saved[0], 16)
                update_states(dve, state[:, j, :], state[:, 1 - j, :], kvr_ps[:, j, :], lambda h: kvm(j, h),
                              keep["cdec"][:, 4:8], lambda h: mdec[:, j, h:h + 1], updated)

            over_tiles(dve, chunk_step)

        @block.gpsimd
        def _(pool):
            for j in range(2):
                last = pool.memset(v1[:, j, :, HD:AUG], 1.0)
            last.then_inc(ones_ready, 1)
            pool.wait_ge(conv_loaded, 16)

            def taps(pair, j, seq):
                r = 2 * pair + j
                pool.wait_ge(loaded[j], 16 * LOADS * (pair + 1))
                pool.tensor_tensor(xs[:, j, 0, :], xs[:, j, 0, :], convw[:, 0, :], ALU.mult).then_inc(side_taps, 1)
                pool.tensor_tensor(xs[:, j, 2, :], xs[:, j, 2, :], convw[:, 2, :], ALU.mult).then_inc(side_taps, 1)
                pool.tensor_tensor(kret[:, j, :].rearrange("p (h e) -> p h e", h=HEADS),
                                   kv[:, j, 0, :].rearrange("p (h e) -> p h e", h=HEADS),
                                   keep["kdec"][:, 4:8].rearrange("p (h o) -> p h o", o=1).to_broadcast([P, HEADS, HD]),
                                   ALU.mult).then_inc(kret_ready, 1)
                if seq:
                    pool.wait_ge(updated, r)
                    pool.wait_ge(cached, 48)
                else:
                    pool.wait_ge(zeroed, 1)
                    pool.wait_ge(updated, r)
                pool.dma_start(s["bst"][bass.ds(chunk(r, seq), 1), :, :].rearrange("c p n -> (c p) n"), state[:, j, :]
                               ).then_inc(saved[j], 16)
                pool.wait_ge(q_ready, r + 1)
                pool.wait_ge(conv_loaded, 16)
                pool.dma_start(s["mqk2"][bass.ts(chunk(r, seq), P), :], qk[:, j, :]).then_inc(qk_stored[j], 16)

            over_tiles(pool, taps)
            for j in range(2):
                pool.wait_ge(saved[j], 16 * PAIRS)
                pool.wait_ge(qk_stored[j], 16 * PAIRS)


def forward_scan(nc, a, s, keep, out):
    ident = keep["ident"]
    with ExitStack() as ctx:
        m = Scope(nc, ctx, "fwd")
        far = m.sb("far", [P, 2, P])
        qkv = m.sb("qkv", [P, 2, 3, W])
        v1 = m.sb("v1", [P, 2, HEADS, AUG])
        qk = m.sb("qk", [P, 2, 2 * W])
        gate = m.sb("gate", [P, 2, D])
        rows = m.sb("rows", [3 * ROWS, 2, P])
        wide = m.sb("wide", [P, 2, 2, ROWS, P])
        bst = m.sb("bst", [P, 2, STATE])
        state = m.sb("state", [P, 2, STATE])
        qT = m.sb("qT", [P, 2, HEADS, P])
        kT = m.sb("kT", [P, 2, HEADS, P])
        qd = m.sb("qd", [P, 2, 2, HEADS, P])
        cols = m.sb("cols", [P, 3, ROWS])
        wts = m.sb("wts", [P, 2, HEADS, P])
        aret = m.sb("aret", [P, HEADS, P])
        aml = m.sb("aml", [P, 2, HEADS, P])
        kret = m.sb("kret", [P, W])
        kml = m.sb("kml", [P, W])
        den = m.sb("den", [P, 8])
        den2 = m.sb("den2", [P, 8])
        o = m.sb("o", [P, 2 * HEADS, HD])
        hb = m.sb("hb", [P, HEADS, HD])
        mean = m.sb("mean", [P, 8])
        var = m.sb("var", [P, 8])
        rstd = m.sb("rstd", [P, 8])
        power = m.sb("power", [P, 8])
        y = m.sb("y", [P, 2, D])
        big = m.ps("big", [P, 4, BLK])
        sc = m.ps("sc", [P, 2, BLK])
        ret_ps = m.ps("ret", [P, BLK])
        misc = m.ps("misc", [P, BLK])
        COLS = slice(0, 3 * ROWS)
        KV3 = slice(3 * ROWS, 3 * ROWS + AUG)

        far_loaded, ones_ready = m.sem("far_loaded"), m.sem("ones_ready")
        loaded = [m.sem(f"loaded{j}") for j in range(2)]
        gate_loaded = [m.sem(f"gate_loaded{j}") for j in range(2)]
        LOADS = 7
        transposed, cols_T = m.sem("transposed"), m.sem("cols_T")
        cols_ready, plain_ready, decayed_ready = m.sem("cols_ready"), m.sem("plain_ready"), m.sem("decayed_ready")
        scores, masked, wts_ready = m.sem("scores"), m.sem("masked"), m.sem("wts_ready")
        aret_ready, aml_ready = m.sem("aret_ready"), m.sem("aml_ready")
        kret_ready, kml_ready = m.sem("kret_ready"), m.sem("kml_ready")
        ret_mixed = m.sem("ret_mixed")
        mixed, kv_done, updated = m.sem("mixed"), m.sem("kv_done"), m.sem("updated")
        oret_ready, den_step, h_part = m.sem("oret_ready"), m.sem("den_step"), m.sem("h_part")
        o_ready, norm_step, centred = m.sem("o_ready"), m.sem("norm_step"), m.sem("centred")
        squared, normed, y_ready = m.sem("squared"), m.sem("normed"), m.sem("y_ready")
        y_stored = [m.sem(f"y_stored{j}") for j in range(2)]
        zeroed, cached, ctx_stored = m.sem("zeroed"), m.sem("cached"), m.sem("ctx_stored")
        power_ready = m.sem("power_ready")
        block = ctx.enter_context(nc.Block())

        def retq(d, h):
            return qd[:, 0, d, h, :]

        def mlq(d, h):
            return qd[:, 1, d, h, :]

        def kvm(h):
            return sc[:, 1, h * AUG:(h + 1) * AUG] if h < 3 else misc[:, KV3]

        def num(d, h):
            return big[:, 2 * d + h // 2, (h % 2) * AUG:(h % 2 + 1) * AUG]

        def head_sum(d):
            return big[:, 2 * d:2 * d + 2, 0:2 * AUG].rearrange("p b (g e) -> p b g e", g=2)[:, :, :, 0:HD]

        @block.sync
        def _(sp):
            sp.dma_start(far[:, :, :], a["far"]).then_inc(far_loaded, 16)

            def load(pair, j, seq):
                c = 2 * pair + j
                if seq:
                    sp.wait_ge(updated, c - 1)
                r = bass.ts(c, P)
                inc = (loaded[j], 16)
                sp.dma_start(rows[:, j, :], s["rows"][0:3 * ROWS, r]).then_inc(*inc)
                sp.dma_start(qkv[:, j, :, :].rearrange("p a n -> p (a n)"), s["qkv"][r, 0:3 * W]).then_inc(*inc)
                sp.dma_start(qk[:, j, :], s["mqk2"][r, :]).then_inc(*inc)
                for kind in (MX, WI):
                    sp.dma_start(wide[:, j, kind - MX, :, :], s["rows"][kind * ROWS:(kind + 1) * ROWS, r]
                                 .rearrange("(o k) t -> o k t", o=1).to_broadcast([P, ROWS, P])).then_inc(*inc)
                sp.dma_start(v1[:, j, :, 0:HD], s["qkv"][r, 3 * W:4 * W].rearrange("p (h e) -> p h e", h=HEADS)).then_inc(*inc)
                sp.dma_start(bst[:, j, :], s["bst"][bass.ds(c, 1), :, :].rearrange("c p n -> (c p) n")).then_inc(*inc)
                if seq:
                    sp.wait_ge(y_ready, c - 1)
                sp.dma_start(gate[:, j, :], s["gate"][r, :]).then_inc(gate_loaded[j], 16)

            for j in range(2):
                load(0, j, 0)
            sp.wait_ge(updated, CTX_TILES)
            store_states(sp, out, state[:, 0, :], 0, ctx_stored)
            sp.wait_ge(ctx_stored, 48)
            load_states(sp, a, state[:, 0, :], 0, cached)
            with sp.Fori(1, PAIRS) as pair:
                for j in range(2):
                    load(pair, j, 1)

        @block.scalar
        def _(act):
            def plain(c, pair, j):
                act.wait_ge(scores, 2 * c)
                for i in range(2):
                    act.wait_ge(transposed, 2 * c + i + 1)
                    act.activation(qT[:, i, :, :], big[:, 2 * i, :].rearrange("p (h t) -> p h t", h=HEADS), ACT.Copy)
                    act.activation(kT[:, i, :, :], big[:, 2 * i + 1, :].rearrange("p (h t) -> p h t", h=HEADS), ACT.Copy
                                   ).then_inc(plain_ready, 1)

            def weigh(c, pair, j):
                act.wait_ge(masked, c + 1)
                act.wait_ge(cols_ready, c + 1)
                act.wait_ge(aml_ready, c)
                for d in range(2):
                    for h in range(HEADS):
                        n = HEADS * d + h
                        last = act.activation(wts[:, d, h, :], wide[:, j, 0, n, :], ACT.Exp, bias=cols[:, U, n:n + 1], scale=-1.0)
                last.then_inc(wts_ready, 1)

            def square(c, pair, j):
                act.wait_ge(centred, c + 1)
                act.wait_ge(y_stored[j], 16 * pair)
                act.activation(y[:, j, :], o[:, :, :].rearrange("p h e -> p (h e)"), ACT.Square).then_inc(squared, 1)

            def take_ret(c, pair, j):
                act.wait_ge(ret_mixed, c + 1)
                act.wait_ge(normed, c)
                act.activation(o[:, 0:HEADS, :], ret_ps[:, :].rearrange("p (h e) -> p h e", h=HEADS), ACT.Copy
                               ).then_inc(oret_ready, 1)

            over_steps(act, [(0, plain), (0, weigh), (1, square), (0, take_ret)])

        @block.tensor
        def _(pe):
            def chunk_step(c, pair, j):
                pe.wait_ge(loaded[j], 16 * LOADS * (pair + 1))
                pe.wait_ge(h_part, c)
                srcs = (qkv[:, j, 0, :], qkv[:, j, 1, :], qk[:, j, 0:W], qk[:, j, W:2 * W])
                for i, src in enumerate(srcs):
                    if i == 2:
                        pe.wait_ge(updated, c)
                    for h in range(HEADS):
                        last = pe.transpose(big[:, i, h * P:(h + 1) * P], src[:, h * HD:(h + 1) * HD], ident[:, :])
                    if i % 2:
                        last.then_inc(transposed, 1)
                    if i == 2:
                        pe.transpose(misc[:, COLS], rows[:, j, :], ident[0:3 * ROWS, 0:3 * ROWS]).then_inc(cols_T, 1)
                for i in range(2):
                    pe.wait_ge(plain_ready, 2 * c + i + 1)
                    for h in range(HEADS):
                        last = pe.matmul(sc[:, i, h * P:(h + 1) * P], kT[:, i, h, :], qT[:, i, h, :], start=True, stop=True)
                    last.then_inc(scores, 1)
                pe.wait_ge(aret_ready, c + 1)
                pe.wait_ge(decayed_ready, 2 * c + 1)
                if reuses(c):
                    pe.wait_ge(cached, 48)
                pe.wait_ge(oret_ready, c)
                for h in range(HEADS):
                    at = slice(h * HD, (h + 1) * HD)
                    pe.matmul(ret_ps[:, at], aret[:, h, :], qkv[:, j, 2, at], start=True, stop=False)
                    pe.matmul(ret_ps[:, at], retq(0, h), state[:, j, at], start=False, stop=False)
                    last = pe.matmul(ret_ps[:, at], retq(1, h), bst[:, j, at], start=False, stop=True)
                last.then_inc(ret_mixed, 1)
                pe.wait_ge(decayed_ready, 2 * c + 2)
                pe.wait_ge(aml_ready, c + 1)
                pe.wait_ge(ones_ready, 1)
                for d in range(2):
                    for h in range(HEADS):
                        at = slice(W + h * AUG, W + (h + 1) * AUG)
                        pe.matmul(num(d, h), aml[:, d, h, :], v1[:, j, h, :], start=True, stop=False)
                        last = pe.matmul(num(d, h), mlq(d, h), (state if d == 0 else bst)[:, j, at],
                                         start=False, stop=True)
                last.then_inc(mixed, 1)
                pe.wait_ge(kret_ready, c + 1)
                pe.wait_ge(kml_ready, c + 1)
                for h in range(HEADS):
                    at = slice(h * HD, (h + 1) * HD)
                    pe.matmul(sc[:, 0, at], kret[:, at], qkv[:, j, 2, at], start=True, stop=True)
                for h in range(HEADS):
                    last = pe.matmul(kvm(h), kml[:, h * HD:(h + 1) * HD], v1[:, j, h, :], start=True, stop=True)
                last.then_inc(kv_done, 1)

            over_steps(pe, [(0, chunk_step)])

        @block.vector
        def _(dve):
            dve.memset(state[:, 0, :], 0.0).then_inc(zeroed, 1)
            dve.wait_ge(zeroed, 1)

            def weigh(c, pair, j):
                dve.wait_ge(loaded[j], 16 * LOADS * (pair + 1))
                dve.wait_ge(cols_T, c + 1)
                dve.wait_ge(kml_ready, c)
                dve.wait_ge(wts_ready, c)
                dve.tensor_copy(cols[:, :, :].rearrange("p k r -> p (k r)"), misc[:, COLS]).then_inc(cols_ready, 1)
                dve.wait_ge(mixed, c)
                dve.wait_ge(plain_ready, 2 * c + 1)
                q = big[:, 0, :].rearrange("p (h t) -> p h t", h=HEADS)
                for d in range(2):
                    last = dve.tensor_tensor(qd[:, 0, d, :, :], q, keep["qdec"][:, d, :, :], ALU.mult)
                last.then_inc(decayed_ready, 1)
                dve.wait_ge(scores, 2 * c + 1)
                dve.tensor_tensor(aret[:, :, :], sc[:, 0, :].rearrange("p (h t) -> p h t", h=HEADS), keep["mret"][:, :, :],
                                  ALU.mult).then_inc(aret_ready, 1)
                dve.wait_ge(plain_ready, 2 * c + 2)
                q = big[:, 2, :].rearrange("p (h t) -> p h t", h=HEADS)
                for d in range(2):
                    last = dve.tensor_tensor(qd[:, 1, d, :, :], q, wide[:, j, 1, 4 * d:4 * d + 4, :], ALU.mult)
                last.then_inc(decayed_ready, 1)
                dve.wait_ge(scores, 2 * c + 2)
                dve.wait_ge(wts_ready, c + 1)
                for d in range(2):
                    last = dve.tensor_tensor(aml[:, d, :, :], sc[:, 1, :].rearrange("p (h t) -> p h t", h=HEADS),
                                             wts[:, d, :, :], ALU.mult)
                last.then_inc(aml_ready, 1)

            def combine(c, pair, j):
                dve.wait_ge(mixed, c + 1)
                dv = big[:, :, 0:2 * AUG].rearrange("p b (g e) -> p b g e", g=2)[:, :, :, HD]
                dve.tensor_copy(den[:, :].rearrange("p (b g) -> p b g", g=2), dv).then_inc(den_step, 1)
                dve.wait_ge(den_step, 4 * c + 1)
                dve.scalar_tensor_tensor(out=den2[:, :], in0=den[:, :], scalar=-1.0, in1=den[:, :], op0=ALU.mult, op1=ALU.max
                                         ).then_inc(den_step, 1)
                dve.wait_ge(den_step, 4 * c + 2)
                dve.tensor_tensor(den[:, :], den2[:, :], cols[:, EN, :], ALU.max).then_inc(den_step, 1)
                dve.wait_ge(den_step, 4 * c + 3)
                dve.reciprocal(den2[:, :], den[:, :]).then_inc(den_step, 1)
                dve.wait_ge(den_step, 4 * c + 4)
                dve.wait_ge(o_ready, c)
                dve.wait_ge(normed, c)
                for d, dst in ((0, o[:, HEADS:2 * HEADS, :]), (1, hb[:, :, :])):
                    last = dve.tensor_tensor(dst.rearrange("p (b g) e -> p b g e", g=2), head_sum(d),
                                             den2[:, 4 * d:4 * d + 4].rearrange("p (b g o) -> p b g o", g=2, o=1)
                                             .to_broadcast([P, 2, 2, HD]), ALU.mult)
                last.then_inc(h_part, 1)

            def update(c, pair, j):
                dve.wait_ge(kv_done, c + 1)
                dve.wait_ge(updated, c)
                update_states(dve, state[:, j, :], state[:, 1 - j, :], sc[:, 0, :], kvm, keep["cdec"][:, 0:4],
                              lambda h: wide[:, j, 1, h, P - 1:P], updated)

            def centre(c, pair, j):
                dve.wait_ge(oret_ready, c + 1)
                dve.wait_ge(o_ready, c + 1)
                dve.tensor_reduce(mean[:, :], o[:, :, :], AX_X, ALU.add).then_inc(norm_step, 1)
                dve.wait_ge(norm_step, 5 * c + 1)
                dve.tensor_scalar(mean[:, :], mean[:, :], 1.0 / HD, None, ALU.mult).then_inc(norm_step, 1)
                dve.wait_ge(norm_step, 5 * c + 2)
                wide_mean = mean[:, :].rearrange("p (h o) -> p h o", o=1).to_broadcast([P, 2 * HEADS, HD])
                dve.tensor_tensor(o[:, :, :], o[:, :, :], wide_mean, ALU.subtract).then_inc(centred, 1)

            def normalise(c, pair, j):
                dve.wait_ge(squared, c + 1)
                dve.tensor_reduce(var[:, :], y[:, j, :].rearrange("p (h e) -> p h e", e=HD), AX_X, ALU.add).then_inc(norm_step, 1)
                dve.wait_ge(norm_step, 5 * c + 3)
                dve.tensor_scalar(var[:, :], var[:, :], 1.0 / HD, EPS, ALU.mult, ALU.add).then_inc(norm_step, 1)
                dve.wait_ge(norm_step, 5 * c + 5)
                wide_std = rstd[:, :].rearrange("p (h o) -> p h o", o=1).to_broadcast([P, 2 * HEADS, HD])
                dve.tensor_tensor(y[:, j, :].rearrange("p (h e) -> p h e", e=HD), o[:, :, :], wide_std, ALU.mult).then_inc(normed, 1)

            over_steps(dve, [(1, update), (1, centre), (0, weigh), (1, normalise), (0, combine)])

        @block.gpsimd
        def _(pool):
            for j in range(2):
                last = pool.memset(v1[:, j, :, HD:AUG], 1.0)
            last.then_inc(ones_ready, 1)
            pool.memset(power[:, :], -0.5).then_inc(power_ready, 1)
            pool.wait_ge(power_ready, 1)
            pool.wait_ge(far_loaded, 16)

            def add(c, pair, j):
                pool.wait_ge(h_part, c + 1)
                pool.tensor_tensor(o[:, HEADS:2 * HEADS, :], o[:, HEADS:2 * HEADS, :], hb[:, :, :], ALU.add).then_inc(o_ready, 1)

            def mask(c, pair, j):
                pool.wait_ge(loaded[j], 16 * LOADS * (pair + 1))
                row = wide[:, j, 0, :, :].rearrange("p (d h) t -> p d h t", d=2)
                reach = far[:, :, :].rearrange("p d (o t) -> p d o t", o=1).to_broadcast([P, 2, HEADS, P])
                pool.tensor_tensor(row, row, reach, ALU.add).then_inc(masked, 1)

            def keys(c, pair, j):
                pool.wait_ge(loaded[j], 16 * LOADS * (pair + 1))
                pool.wait_ge(kv_done, c)
                pool.tensor_tensor(kret[:, :].rearrange("p (h e) -> p h e", h=HEADS),
                                   qkv[:, j, 1, :].rearrange("p (h e) -> p h e", h=HEADS),
                                   keep["kdec"][:, 0:4].rearrange("p (h o) -> p h o", o=1).to_broadcast([P, HEADS, HD]),
                                   ALU.mult).then_inc(kret_ready, 1)
                pool.wait_ge(cols_ready, c + 1)
                pool.tensor_tensor(kml[:, :].rearrange("p (h e) -> p h e", h=HEADS),
                                   qk[:, j, W:2 * W].rearrange("p (h e) -> p h e", h=HEADS),
                                   cols[:, WE, 0:4].rearrange("p (h o) -> p h o", o=1).to_broadcast([P, HEADS, HD]),
                                   ALU.mult).then_inc(kml_ready, 1)

            def finish(c, pair, j):
                pool.wait_ge(norm_step, 5 * c + 4)
                pool.tensor_tensor(rstd[:, :], var[:, :], power[:, :], ALU.pow).then_inc(norm_step, 1)
                pool.wait_ge(normed, c + 1)
                pool.wait_ge(gate_loaded[j], 16 * (pair + 1))
                pool.tensor_tensor(y[:, j, :], y[:, j, :], gate[:, j, :], ALU.mult).then_inc(y_ready, 1)
                pool.wait_ge(y_ready, c + 1)
                pool.dma_start(s["y"][bass.ts(c, P), :], y[:, j, :]).then_inc(y_stored[j], 16)

            over_steps(pool, [(1, add), (0, mask), (0, keys), (1, finish)])
            for j in range(2):
                pool.wait_ge(y_stored[j], 16 * PAIRS)


def output(nc, a, s, keep):
    ident = keep["ident"]
    with ExitStack() as ctx:
        m = Scope(nc, ctx, "out")
        w = m.sb("w", [P, 2, KT, D], F32R)
        raw = m.sb("raw", [P, KT, BLK])
        y = m.sb("y", [P, 2, D])
        x = m.sb("x", [P, 2, D])
        yT = m.sb("yT", [P, 2, 2, KT, P], F32R)
        x1 = m.sb("x1", [P, 2, D])
        h = m.sb("h", [P, 2, D])
        hT = m.sb("hT", [P, 2, 2, KT, P], F32R)
        g1 = m.sb("g1", [P, 2, D])
        shift = m.sb("shift", [P, 2, D])
        scale = m.sb("scale", [P, 2, D])
        gain = m.sb("gain", [P, D])
        junk = m.sb("junk", [P, D])
        ssq = m.sb("ssq", [P, 2])
        rstd = m.sb("rstd", [P, 2])
        mean = m.sb("mean", [P, 2])
        power = m.sb("power", [P, 1])
        yT_ps = m.ps("yT_ps", [P, KT, P])
        hT_ps = m.ps("hT_ps", [P, KT, P])
        acc = m.ps("acc", [P, 2, 2, BLK])
        w_hi, w_lo, yT_lo, hT_lo = m.sem("w_hi"), m.sem("w_lo"), m.sem("yT_lo"), m.sem("hT_lo")
        w_loaded, mod_loaded, scale_ready = m.sem("w_loaded"), m.sem("mod_loaded"), m.sem("scale_ready")
        y_loaded = [m.sem(f"y_loaded{j}") for j in range(2)]
        x_loaded = [m.sem(f"x_loaded{j}") for j in range(2)]
        y_T, yT_ready, product_done = m.sem("y_T"), m.sem("yT_ready"), m.sem("product_done")
        gated, x1_ready, ssq_ready = m.sem("gated"), m.sem("x1_ready"), m.sem("ssq_ready")
        rstd_step, scaled, h_ready = m.sem("rstd_step"), m.sem("scaled"), m.sem("h_ready")
        h_T, hT_ready = m.sem("h_T"), m.sem("hT_ready")
        x1_stored = [m.sem(f"x1_stored{j}") for j in range(2)]
        hT_stored = [m.sem(f"hT_stored{j}") for j in range(2)]
        power_ready = m.sem("power_ready")
        block = ctx.enter_context(nc.Block())

        @block.sync
        def _(sp):
            def load_y(t, pair, j):
                if reuses(t):
                    sp.wait_ge(y_T, t - 1)
                sp.dma_start(y[:, j, :], s["y"][bass.ts(t, P), :]).then_inc(y_loaded[j], 16)

            def load_x(t, pair, j):
                if reuses(t):
                    sp.wait_ge(x1_ready, t - 1)
                src = a["x_sample"][0, bass.ts(t - CTX_TILES, P), :] if seq_of(t) else a["x_prompt"][0, bass.ts(t, P), :]
                sp.dma_start(x[:, j, :], src).then_inc(x_loaded[j], 16)

            w_out = a["w_out"][0].rearrange("(k p) n -> p k n", p=P)
            for n in range(2):
                sp.wait_ge(w_lo, n)
                sp.dma_start(raw[:, :, :], w_out[:, :, n * BLK:(n + 1) * BLK]).then_inc(w_loaded, 16)
                if n == 0:
                    for seq in range(2):
                        for dst, at in ((g1, 2), (shift, 3), (scale, 4)):
                            sp.dma_start(dst[:, seq, :], s["mod"][seq:seq + 1, at * D:(at + 1) * D].to_broadcast([P, D])
                                         ).then_inc(mod_loaded, 16)
                    sp.dma_start(gain[:, :], a["norm2_g"].to_broadcast([P, D])).then_inc(mod_loaded, 16)
            over_steps(sp, [(0, load_y), (1, load_x)])

        @block.scalar
        def _(act):
            def split_y(t, pair, j):
                act.wait_ge(y_T, t + 1)
                if reuses(t):
                    act.wait_ge(product_done, t - 1)
                act.activation(yT[:, j, 0, :, :], yT_ps[:, :, :], ACT.Copy).then_inc(yT_ready, 1)

            def split_h(t, pair, j):
                act.wait_ge(h_T, t + 1)
                act.wait_ge(hT_stored[j], 32 * pair)
                act.activation(hT[:, j, 0, :, :], hT_ps[:, :, :], ACT.Copy).then_inc(hT_ready, 1)

            def square(t, pair, j):
                act.wait_ge(x1_ready, t + 1)
                act.wait_ge(ssq_ready, t)
                if reuses(t):
                    act.wait_ge(rstd_step, 2 * (t - 1))
                act.activation(junk[:, :], x1[:, j, :], ACT.Square, accum_out=ssq[:, j:j + 1]).then_inc(ssq_ready, 1)

            for n in range(2):
                act.wait_ge(w_loaded, 16 * (n + 1))
                act.activation(w[:, 0, :, n * BLK:(n + 1) * BLK], raw[:, :, :], ACT.Copy).then_inc(w_hi, 1)
            over_steps(act, [(0, split_y), (2, split_h), (1, square)])

        @block.tensor
        def _(pe):
            def transpose_y(t, pair, j):
                pe.wait_ge(y_loaded[j], 16 * (pair + 1))
                pe.wait_ge(yT_lo, t)
                for k in range(KT):
                    last = pe.transpose(yT_ps[:, k, :], y[:, j, k * P:(k + 1) * P], ident[:, :])
                last.then_inc(y_T, 1)

            def multiply(t, pair, j):
                pe.wait_ge(w_lo, 2)
                pe.wait_ge(yT_lo, t + 1)
                if reuses(t):
                    pe.wait_ge(gated, t - 1)
                for n in range(2):
                    last = product(pe, acc[:, j, n, :], KT, lambda part, k: yT[:, j, part, k, :],
                                   lambda part, k: w[:, part, k, n * BLK:(n + 1) * BLK])
                last.then_inc(product_done, 1)

            def transpose_h(t, pair, j):
                pe.wait_ge(h_ready, t + 1)
                pe.wait_ge(hT_lo, t)
                for k in range(KT):
                    last = pe.transpose(hT_ps[:, k, :], h[:, j, k * P:(k + 1) * P], ident[:, :])
                last.then_inc(h_T, 1)

            over_steps(pe, [(0, transpose_y), (1, multiply), (2, transpose_h)])

        @block.vector
        def _(dve):
            for n in range(2):
                dve.wait_ge(w_hi, n + 1)
                at = slice(n * BLK, (n + 1) * BLK)
                dve.tensor_tensor(w[:, 1, :, at], raw[:, :, :], w[:, 0, :, at].bitcast(F32), ALU.subtract).then_inc(w_lo, 1)
            dve.wait_ge(mod_loaded, 7 * 16)
            for seq in range(2):
                dve.scalar_tensor_tensor(out=scale[:, seq, :], in0=scale[:, seq, :], scalar=1.0, in1=gain[:, :],
                                         op0=ALU.add, op1=ALU.mult).then_inc(scale_ready, 1)
            dve.wait_ge(scale_ready, 2)

            def split_y(t, pair, j):
                dve.wait_ge(yT_ready, t + 1)
                dve.tensor_tensor(yT[:, j, 1, :, :], yT_ps[:, :, :], yT[:, j, 0, :, :].bitcast(F32), ALU.subtract
                                  ).then_inc(yT_lo, 1)

            def split_h(t, pair, j):
                dve.wait_ge(hT_ready, t + 1)
                dve.tensor_tensor(hT[:, j, 1, :, :], hT_ps[:, :, :], hT[:, j, 0, :, :].bitcast(F32), ALU.subtract
                                  ).then_inc(hT_lo, 1)

            def residual(t, pair, j):
                dve.wait_ge(product_done, t + 1)
                dve.wait_ge(x1_stored[j], 16 * pair)
                if reuses(t):
                    dve.wait_ge(h_ready, t - 1)
                dve.tensor_tensor(x1[:, j, :], acc[:, j, :, :].rearrange("p n c -> p (n c)"), g1[:, seq_of(t), :], ALU.mult
                                  ).then_inc(gated, 1)
                dve.wait_ge(gated, t + 1)
                dve.wait_ge(x_loaded[j], 16 * (pair + 1))
                dve.tensor_tensor(x1[:, j, :], x1[:, j, :], x[:, j, :], ALU.add).then_inc(x1_ready, 1)

            def normalise(t, pair, j):
                dve.wait_ge(ssq_ready, t + 1)
                dve.tensor_scalar(mean[:, j:j + 1], ssq[:, j:j + 1], 1.0 / D, EPS, ALU.mult, ALU.add).then_inc(rstd_step, 1)
                dve.wait_ge(rstd_step, 2 * t + 2)
                if reuses(t):
                    dve.wait_ge(h_T, t - 1)
                dve.scalar_tensor_tensor(out=h[:, j, :], in0=x1[:, j, :], scalar=rstd[:, j:j + 1], in1=scale[:, seq_of(t), :],
                                         op0=ALU.mult, op1=ALU.mult).then_inc(scaled, 1)
                dve.wait_ge(scaled, t + 1)
                dve.tensor_tensor(h[:, j, :], h[:, j, :], shift[:, seq_of(t), :], ALU.add).then_inc(h_ready, 1)

            over_steps(dve, [(0, split_y), (1, residual), (2, split_h), (1, normalise)])

        @block.gpsimd
        def _(pool):
            pool.memset(power[:, :], -0.5).then_inc(power_ready, 1)
            pool.wait_ge(power_ready, 1)

            def store_x1(t, pair, j):
                pool.wait_ge(x1_ready, t + 1)
                pool.dma_start(s["x1"][bass.ts(t, P), :], x1[:, j, :]).then_inc(x1_stored[j], 16)

            def store_h(t, pair, j):
                pool.wait_ge(hT_lo, t + 1)
                for part in range(2):
                    pool.dma_start(s["h2T"][:, part, :, bass.ts(t, P)], hT[:, j, part, :, :].bitcast(F32)).then_inc(hT_stored[j], 16)

            def root(t, pair, j):
                pool.wait_ge(rstd_step, 2 * t + 1)
                pool.tensor_tensor(rstd[:, j:j + 1], mean[:, j:j + 1], power[:, 0:1], ALU.pow).then_inc(rstd_step, 1)

            over_steps(pool, [(1, store_x1), (1, root), (2, store_h)])
            for j in range(2):
                pool.wait_ge(x1_stored[j], 16 * PAIRS)
                pool.wait_ge(hT_stored[j], 32 * PAIRS)


def mlp(nc, a, s, keep, out):
    HALF = TILES // 2
    HT = HALF * P
    BLOCKS = 3
    SIZE = HT // BLOCKS
    PB = SIZE // P
    CHUNK_PAIRS = FF_CHUNKS // 2
    with ExitStack() as ctx:
        m = Scope(nc, ctx, "mlp")
        hT = m.sb("hT", [P, 2, KT, HT], F32R)
        total = m.sb("total", [P, HALF, D])
        raw1 = m.sb("raw1", [P, 2, KT, P])
        raw2 = m.sb("raw2", [P, 2, D])
        w1 = m.sb("w1", [P, 2, 2, KT, P], F32R)
        w2 = m.sb("w2", [P, 2, 2, D], F32R)
        rel = m.sb("rel", [P, 2, SIZE])
        sq = m.sb("sq", [P, 2, SIZE])
        fT = m.sb("fT", [P, 2, 2, HT], F32R)
        x1 = m.sb("x1", [P, 2, D])
        g2 = m.sb("g2", [P, 2, D])
        gain = m.sb("gain", [P, D])
        ssq = m.sb("ssq", [P, 2])
        mean = m.sb("mean", [P, 2])
        rstd = m.sb("rstd", [P, 2])
        power = m.sb("power", [P, 1])
        up = m.ps("up", [P, BLOCKS, BLK])
        down = m.ps("down", [P, 4, BLK])
        hT_loaded = [m.sem(f"hT_loaded{i}") for i in range(BLOCKS)]
        w_loaded = [m.sem(f"w_loaded{j}") for j in range(2)]
        w_hi, w_lo = m.sem("w_hi"), m.sem("w_lo")
        up_done, relu_done, sq_ready, f_hi, f_lo = (m.sem(n) for n in ("up_done", "relu_done", "sq_ready", "f_hi", "f_lo"))
        down_done, added = m.sem("down_done"), m.sem("added")
        g2_loaded, gain_loaded, power_ready = m.sem("g2_loaded"), m.sem("gain_loaded"), m.sem("power_ready")
        gated, x2_ready, ssq_ready = m.sem("gated"), m.sem("x2_ready"), m.sem("ssq_ready")
        mean_ready, rstd_ready, y_ready = m.sem("mean_ready"), m.sem("rstd_ready"), m.sem("y_ready")
        x1_loaded = [m.sem(f"x1_loaded{j}") for j in range(2)]
        y_stored = [m.sem(f"y_stored{t}") for t in range(HALF)]
        w_ff1 = a["w_ff1"][0].rearrange("(k p) f -> p k f", p=P)
        w_ff2 = a["w_ff2"][0]
        block = ctx.enter_context(nc.Block())

        def down_bank(j, t, n):
            return (2 * HALF * j + 2 * t + n) % 4

        def over_chunks(engine, half, body):
            lead = half * CHUNK_PAIRS
            for j in range(2):
                body(lead, j, half)
            with engine.Fori(lead + 1, lead + CHUNK_PAIRS) as pair:
                for j in range(2):
                    body(pair, j, half)

        @block.sync
        def _(sp):
            def load_w(pair, j, half):
                f = 2 * pair + j
                at = f - half * FF_CHUNKS
                if not (isinstance(pair, int) and pair == 0):
                    sp.wait_ge(w_lo, 2 * (f - 1))
                sp.dma_start(raw1[:, j, :, :], w_ff1[:, :, bass.ts(at, P)]).then_inc(w_loaded[j], 16)
                sp.dma_start(raw2[:, j, :], w_ff2[bass.ts(at, P), :]).then_inc(w_loaded[j], 16)

            def load_x1(t):
                if t >= 2:
                    sp.wait_ge(ssq_ready, t - 1)
                sp.dma_start(x1[:, t % 2, :], s["x1"][t * P:(t + 1) * P, :]).then_inc(x1_loaded[t % 2], 16)

            sp.dma_start(gain[:, :], a["final_g"].rearrange("(o n) -> o n", o=1).to_broadcast([P, D])).then_inc(gain_loaded, 16)
            for seq in range(2):
                sp.dma_start(g2[:, seq, :], s["mod"][seq:seq + 1, 5 * D:6 * D].to_broadcast([P, D])).then_inc(g2_loaded, 16)
            for half in range(2):
                lead = half * CHUNK_PAIRS
                if half:
                    sp.wait_ge(up_done, BLOCKS * FF_CHUNKS)
                for i in range(BLOCKS):
                    for part in range(2):
                        sp.dma_start(hT[:, part, :, i * SIZE:(i + 1) * SIZE].bitcast(F32),
                                     s["h2T"][:, part, :, half * HT + i * SIZE:half * HT + (i + 1) * SIZE]
                                     ).then_inc(hT_loaded[i], 16)
                    if i == 0:
                        load_w(lead, 0, half)
                load_w(lead, 1, half)
                for i in range(2):
                    load_x1(half * HALF + i)
                with sp.Fori(lead + 1, lead + CHUNK_PAIRS) as pair:
                    for j in range(2):
                        load_w(pair, j, half)
                for t in range(half * HALF, (half + 1) * HALF):
                    if t + 2 < (half + 1) * HALF:
                        load_x1(t + 2)

        @block.scalar
        def _(act):
            def activate(pair, j, half):
                f = 2 * pair + j
                act.wait_ge(w_loaded[j], 32 * (pair + 1))
                if not (isinstance(pair, int) and f < 2):
                    act.wait_ge(up_done, BLOCKS * (f - 1))
                act.activation(w1[:, j, 0, :, :], raw1[:, j, :, :], ACT.Copy).then_inc(w_hi, 1)
                if not (isinstance(pair, int) and f < 2):
                    act.wait_ge(down_done, 2 * HALF * (f - 1))
                act.activation(w2[:, j, 0, :], raw2[:, j, :], ACT.Copy).then_inc(w_hi, 1)
                for i in range(BLOCKS):
                    q = BLOCKS * f + i
                    b = (BLOCKS * j + i) % 2
                    ahead = not (isinstance(pair, int) and q < 2)
                    act.wait_ge(up_done, q + 1)
                    if ahead:
                        act.wait_ge(f_hi, q - 1)
                    act.activation(rel[:, b, :], up[:, i, 0:SIZE], ACT.Relu).then_inc(relu_done, 1)
                    if ahead:
                        act.wait_ge(f_lo, q - 1)
                    act.wait_ge(relu_done, q + 1)
                    act.activation(sq[:, b, :], rel[:, b, :], ACT.Square).then_inc(sq_ready, 1)
                    if i == 0 and not (isinstance(pair, int) and f < 2):
                        act.wait_ge(down_done, 2 * HALF * (f - 1))
                    act.activation(fT[:, j, 0, i * SIZE:(i + 1) * SIZE], rel[:, b, :], ACT.Square).then_inc(f_hi, 1)

            for half in range(2):
                over_chunks(act, half, activate)
                for t in range(half * HALF, (half + 1) * HALF):
                    act.wait_ge(x2_ready, t + 1)
                    if t:
                        act.wait_ge(ssq_ready, t)
                    if t >= 2:
                        act.wait_ge(mean_ready, t - 1)
                    act.activation(x1[:, t % 2, :], total[:, t % HALF, :], ACT.Square, accum_out=ssq[:, t % 2:t % 2 + 1]
                                   ).then_inc(ssq_ready, 1)

        @block.tensor
        def _(pe):
            def multiply(pair, j, half):
                f = 2 * pair + j
                pe.wait_ge(w_lo, 2 * f + 1)
                for i in range(BLOCKS):
                    if isinstance(pair, int) and j == 0:
                        pe.wait_ge(hT_loaded[i], 32 * (half + 1))
                    if not (isinstance(pair, int) and f == 0):
                        pe.wait_ge(relu_done, BLOCKS * (f - 1) + i + 1)
                    last = product(pe, up[:, i, 0:SIZE], KT, lambda part, k: w1[:, j, part, k, :],
                                   lambda part, k: hT[:, part, k, i * SIZE:(i + 1) * SIZE])
                    last.then_inc(up_done, 1)
                pe.wait_ge(w_lo, 2 * f + 2)
                for t in range(HALF):
                    if t % PB == 0:
                        pe.wait_ge(f_lo, BLOCKS * f + t // PB + 1)
                    for n in range(2):
                        q = 2 * HALF * f + 2 * t + n
                        if not (isinstance(pair, int) and q < 4):
                            pe.wait_ge(added, q - 3)
                        last = product(pe, down[:, down_bank(j, t, n), :], 1, lambda part, k: fT[:, j, part, t * P:(t + 1) * P],
                                       lambda part, k: w2[:, j, part, n * BLK:(n + 1) * BLK])
                        last.then_inc(down_done, 1)

            for half in range(2):
                over_chunks(pe, half, multiply)

        @block.vector
        def _(dve):
            def add(pair, j, half):
                f = 2 * pair + j
                first = isinstance(pair, int) and pair == half * CHUNK_PAIRS and j == 0
                for i in range(BLOCKS):
                    q = BLOCKS * f + i
                    b = (BLOCKS * j + i) % 2
                    dve.wait_ge(f_hi, q + 1)
                    at = slice(i * SIZE, (i + 1) * SIZE)
                    dve.tensor_tensor(fT[:, j, 1, at], sq[:, b, :], fT[:, j, 0, at].bitcast(F32), ALU.subtract).then_inc(f_lo, 1)
                for t in range(HALF):
                    for n in range(2):
                        q = 2 * HALF * f + 2 * t + n
                        dst = total[:, t, n * BLK:(n + 1) * BLK]
                        dve.wait_ge(down_done, q + 1)
                        if first:
                            if half and n == 0:
                                dve.wait_ge(y_stored[t], 16)
                            dve.tensor_copy(dst, down[:, down_bank(j, t, n), :]).then_inc(added, 1)
                        else:
                            dve.wait_ge(added, q - 2 * HALF + 1)
                            dve.tensor_tensor(dst, dst, down[:, down_bank(j, t, n), :], ALU.add).then_inc(added, 1)

            def finish(t):
                row = total[:, t % HALF, :]
                dve.wait_ge(gated, t + 1)
                dve.wait_ge(x1_loaded[t % 2], 16 * (t // 2 + 1))
                dve.tensor_tensor(row, row, x1[:, t % 2, :], ALU.add).then_inc(x2_ready, 1)

            def scale(t):
                j = t % 2
                row = total[:, t % HALF, :]
                dve.wait_ge(ssq_ready, t + 1)
                dve.tensor_scalar(mean[:, j:j + 1], ssq[:, j:j + 1], 1.0 / D, EPS, ALU.mult, ALU.add).then_inc(mean_ready, 1)
                dve.wait_ge(rstd_ready, t + 1)
                dve.wait_ge(x2_ready, t + 1)
                dve.scalar_tensor_tensor(out=row, in0=row, scalar=rstd[:, j:j + 1], in1=gain[:, :],
                                         op0=ALU.mult, op1=ALU.mult).then_inc(y_ready, 1)

            dve.wait_ge(gain_loaded, 16)
            for half in range(2):
                over_chunks(dve, half, add)
                first, end = half * HALF, (half + 1) * HALF
                finish(first)
                for t in range(first, end):
                    if t + 1 < end:
                        finish(t + 1)
                    scale(t)

        @block.gpsimd
        def _(pool):
            def split_w(pair, j, half):
                f = 2 * pair + j
                for i, (raw, parts) in enumerate(((raw1[:, j, :, :].rearrange("p k n -> p (k n)"),
                                                   w1[:, j, :, :, :].rearrange("p c k n -> p c (k n)")),
                                                  (raw2[:, j, :], w2[:, j, :, :]))):
                    pool.wait_ge(w_hi, 2 * f + i + 1)
                    pool.tensor_tensor(parts[:, 1, :], raw, parts[:, 0, :].bitcast(F32), ALU.subtract).then_inc(w_lo, 1)

            pool.memset(power[:, :], -0.5).then_inc(power_ready, 1)
            pool.wait_ge(power_ready, 1)
            for half in range(2):
                over_chunks(pool, half, split_w)
                first, end = half * HALF, (half + 1) * HALF

                def gate(t):
                    row = total[:, t % HALF, :]
                    pool.wait_ge(added, 2 * HALF * (FF_CHUNKS * (half + 1) - 1) + 2 * (t - first) + 2)
                    pool.tensor_tensor(row, row, g2[:, int(t >= CTX_TILES), :], ALU.mult).then_inc(gated, 1)

                pool.wait_ge(g2_loaded, 32)
                gate(first)
                for t in range(first, end):
                    j = t % 2
                    if t + 1 < end:
                        gate(t + 1)
                    pool.wait_ge(mean_ready, t + 1)
                    pool.tensor_tensor(rstd[:, j:j + 1], mean[:, j:j + 1], power[:, 0:1], ALU.pow).then_inc(rstd_ready, 1)
                    pool.wait_ge(y_ready, t + 1)
                    dst = out["y_p"][0, t * P:(t + 1) * P, :] if t < CTX_TILES else \
                        out["y_s"][0, (t - CTX_TILES) * P:(t - CTX_TILES + 1) * P, :]
                    pool.dma_start(dst, total[:, t - first, :]).then_inc(y_stored[t - first], 16)
            for t in range(HALF):
                pool.wait_ge(y_stored[t], 32)


_INS = ["x_prompt", "x_sample", "state_ret", "state_mlstm_C", "state_mlstm_n", "state_mlstm_m", "c", "c_ctx", "w_ada",
        "b_ada", "norm1_g", "norm2_g", "w_in", "conv_w", "ret_decay_logit", "mlstm_gate_bias", "ret_gn_g", "mlstm_gn_g",
        "w_out", "w_ff1", "w_ff2", "final_g"]
_OUTS = [("y_p", (1, 256, 1024)), ("y_s", (1, 2048, 1024)), ("ret", (1, 1, 2, 4, 128, 128)), ("C", (1, 1, 2, 4, 128, 128)),
         ("n", (1, 1, 2, 4, 128)), ("m", (1, 1, 2, 4))]


def shape_constants():
    import numpy as np
    i = np.arange(128, dtype=np.float32)
    s, t = i[:, None], i[None, :]
    zero = np.zeros((128, 128), np.float32)
    shapes = np.stack([np.maximum(t - s, 0), np.maximum(s - t, 0), (t >= s).astype(np.float32),
                       (t <= s).astype(np.float32), zero + t + 1, zero + 128 - t], 1).astype(np.float32)
    far = np.stack([np.where(t >= s, 0, 1e30), np.where(t <= s, 0, 1e30)], 1).astype(np.float32)
    rows = np.arange(2048, dtype=np.float32) // 64
    grid_cols = np.arange(2048, dtype=np.float32) % 64
    inv = (10000.0 ** (-np.arange(32, dtype=np.float64) / 32)).astype(np.float32)
    ang = np.concatenate([rows[:, None] * inv, grid_cols[:, None] * inv], -1).astype(np.float64)
    rope = np.stack([np.cos(ang), np.sin(ang)], 1).astype(np.float32)
    return {"ident": np.eye(128, dtype=np.float32), "shapes": shapes, "far": far,
            "cols": np.stack([127 - i, i], 1).astype(np.float32), "rope": rope}


def kernel(**inputs):
    import numpy as np
    import concourse.bacc as bacc
    from concourse import mybir as mb
    from concourse.bass_utils import run_bass_kernel_spmd as run

    nc = bacc.Bacc("TRN2", target_bir_lowering=False, num_devices=1)
    arrays, args = {}, {}
    given = {name: np.ascontiguousarray(inputs[name]) for name in _INS}
    for name, value in {**given, **shape_constants()}.items():
        arrays[f"in_{name}"] = value
        args[name] = nc.dram_tensor(f"in_{name}", value.shape, mb.dt.from_np(value.dtype), kind="ExternalInput").ap()
    outs = {name: nc.dram_tensor(f"out_{name}", shape, mb.dt.float32, kind="ExternalOutput").ap() for name, shape in _OUTS}
    build(nc, args, outs)
    r = run(nc, [arrays], core_ids=[0])
    return tuple(r.results[0][f"out_{name}"] for name, _ in _OUTS)
```

```python
from contextlib import ExitStack

import concourse.bass as bass
from concourse import mybir

ALU = mybir.AluOpType
ACT = mybir.ActivationFunctionType
F32 = mybir.dt.float32
F32R = mybir.dt.float32r
AX_X = mybir.AxisListType.X

P = 128
D = 1024
KT = D // P
HEADS = 4
HD = 128
W = HEADS * HD
AUG = HD + 1
CTX = 256
LAT = 2048
CTX_TILES = CTX // P
TILES = (CTX + LAT) // P
PAIRS = TILES // 2
TOKENS = CTX + LAT
FF = 4 * D
FF_CHUNKS = FF // P
BLK = 512
MOD = 6 * D
EPS = 1e-6
KSCALE = HD ** -0.5
STATE = W + HEADS * AUG
U, EN, WE, MX, WI = range(5)
ROWS = 8
FAR = 1e30


def over_steps(engine, stages):
    def step(t, pair, j):
        for lag, stage in stages:
            if isinstance(t, int):
                if 0 <= t - lag < TILES:
                    stage(t - lag, (t - lag) // 2, (t - lag) % 2)
            else:
                stage(t - lag, pair - (lag - j + 1) // 2, (j - lag) % 2)

    for t in range(4):
        step(t, None, None)
    with engine.Fori(2, PAIRS) as pair:
        for j in range(2):
            step(2 * pair + j, pair, j)
    for t in range(TILES, TILES + 2):
        step(t, None, None)


def seq_of(t):
    return 0 if isinstance(t, int) and t < CTX_TILES else 1


def reuses(t):
    return not isinstance(t, int) or t >= 2


def build(nc, a, out):
    with ExitStack() as ctx:
        def dram(name, shape):
            return nc.dram_tensor(name, shape, F32).ap()

        s = {
            "mod": dram("mod_rows", [2, MOD]),
            "qkv": dram("qkv_rows", [TOKENS, 4 * W]),
            "mqk": dram("mqk_rows", [TOKENS + 4, 2 * W]),
            "mqk2": dram("conv_rows", [TOKENS, 2 * W]),
            "gate": dram("gate_rows_out", [TOKENS, D]),
            "rows": dram("scalar_rows", [5 * ROWS, TOKENS]),
            "mdec": dram("backward_decays", [TILES, HEADS]),
            "bst": dram("backward_states", [TILES, P, STATE]),
            "y": dram("mixed_rows", [TOKENS, D]),
            "x1": dram("residual_rows", [TOKENS, D]),
            "h2T": dram("mlp_in", [P, 2, KT, TOKENS]),
        }
        ident = ctx.enter_context(nc.sbuf_tensor("ident", [P, P], F32))
        with ExitStack() as c2:
            def sb(name, shape):
                return c2.enter_context(nc.sbuf_tensor(name, shape, F32))

            keep = {
                "ident": ident,
                "grows": sb("grows", [P, TOKENS]),
                "mret": sb("mret", [P, HEADS, P]),
                "qdec": sb("qdec", [P, 2, HEADS, P]),
                "kdec": sb("kdec", [P, 8]),
                "cdec": sb("cdec", [P, 8]),
                "cond": sb("silu_cond", [P, 2, KT]),
            }
            modulation(nc, a, s, keep)
            projection(nc, a, s, keep)
            gate_rows(nc, a, s, keep, out)
            backward_scan(nc, a, s, keep, out)
            forward_scan(nc, a, s, keep, out)
        keep = {"ident": ident}
        output(nc, a, s, keep)
        mlp(nc, a, s, keep, out)


class Scope:

    def __init__(self, nc, ctx, name):
        self.nc, self.ctx, self.name, self.sems = nc, ctx, name, []
        ctx.callback(self.close)

    def sb(self, name, shape, dtype=F32):
        return self.ctx.enter_context(self.nc.sbuf_tensor(f"{self.name}_{name}", shape, dtype))

    def ps(self, name, shape):
        return self.ctx.enter_context(self.nc.psum_tensor(f"{self.name}_{name}", shape, F32))

    def sem(self, name):
        self.sems.append(self.nc.alloc_semaphore(name=f"{self.name}_{name}"))
        return self.sems[-1]

    def close(self):
        self.nc.clear_and_free_semaphores(self.sems)
        self.nc.all_engine_barrier()


def product(pe, acc, n, left, right):
    for k in range(n):
        pe.matmul(acc, left(1, k), right(0, k), start=(k == 0), stop=False)
        pe.matmul(acc, left(0, k), right(1, k), start=False, stop=False)
        last = pe.matmul(acc, left(0, k), right(0, k), start=False, stop=(k == n - 1))
    return last


def modulation(nc, a, s, keep):
    NB = 2 * D // BLK
    with ExitStack() as ctx:
        m = Scope(nc, ctx, "mod")
        cond = m.sb("cond", [P, 2, KT])
        sig = m.sb("sig", [P, 2, KT])
        act_c = keep["cond"]
        w = m.sb("w", [P, NB, KT, BLK])
        bias = m.sb("bias", [2, NB, BLK])
        row = m.sb("row", [2, 2, BLK])
        acc = m.ps("acc", [P, 2, BLK])
        cond_loaded, sig_done, silu_done = m.sem("cond_loaded"), m.sem("sig_done"), m.sem("silu_done")
        w_loaded = [m.sem(f"w_loaded{j}") for j in range(NB)]
        product, row_ready = m.sem("product"), m.sem("row_ready")
        row_stored = [m.sem(f"row_stored{j}") for j in range(2)]
        ident_loaded = m.sem("ident_loaded")
        w_ada = a["w_ada"][0].rearrange("(p k) n -> p k n", k=KT)
        block = ctx.enter_context(nc.Block())

        @block.sync
        def _(sp):
            sp.dma_start(cond[:, 0, :], a["c_ctx"].rearrange("(p k) -> p k", k=KT)).then_inc(cond_loaded, 16)
            sp.dma_start(cond[:, 1, :], a["c"][0].rearrange("(p k) -> p k", k=KT)).then_inc(cond_loaded, 16)
            sp.dma_start(keep["ident"][:, :], a["ident"]).then_inc(ident_loaded, 16)

            for n in range(NB):
                sp.dma_start(w[:, n, :, :], w_ada[:, :, bass.ts(n, BLK)]).then_inc(w_loaded[n], 16)
                sp.dma_start(bias[:, n, :], a["b_ada"][0:1, bass.ts(n, BLK)].to_broadcast([2, BLK])
                             ).then_inc(w_loaded[n], 16)
            sp.wait_ge(ident_loaded, 16)

        @block.scalar
        def _(act):
            act.wait_ge(cond_loaded, 32)
            act.activation(sig[:, :, :], cond[:, :, :], ACT.Sigmoid).then_inc(sig_done, 1)

        @block.tensor
        def _(pe):
            pe.wait_ge(silu_done, 1)
            for n in range(NB):
                pe.wait_ge(w_loaded[n], 32)
                if n >= 2:
                    pe.wait_ge(row_ready, n - 1)
                for k in range(KT):
                    last = pe.matmul(acc[0:2, n % 2, :], act_c[:, :, k], w[:, n, k, :], start=(k == 0), stop=(k == KT - 1))
                last.then_inc(product, 1)

        @block.vector
        def _(dve):
            dve.wait_ge(sig_done, 1)
            dve.tensor_tensor(act_c[:, :, :], cond[:, :, :], sig[:, :, :], ALU.mult).then_inc(silu_done, 1)
            for n in range(NB):
                dve.wait_ge(product, n + 1)
                if n >= 2:
                    dve.wait_ge(row_stored[n % 2], 16 * (n // 2))
                dve.tensor_tensor(row[:, n % 2, :], acc[0:2, n % 2, :], bias[:, n, :], ALU.add).then_inc(row_ready, 1)

        @block.gpsimd
        def _(pool):
            for n in range(NB):
                pool.wait_ge(row_ready, n + 1)
                pool.dma_start(s["mod"][:, bass.ts(n, BLK)], row[:, n % 2, :]).then_inc(row_stored[n % 2], 16)
            for j in range(2):
                pool.wait_ge(row_stored[j], 16 * NB // 2)


def load_modulation(sp, s, a, shift, scale, shift_at, scale_at, seq, loaded):
    sp.dma_start(shift[:, :], s["mod"][seq:seq + 1, shift_at * D:(shift_at + 1) * D].to_broadcast([P, D])
                 ).then_inc(loaded, 16)
    sp.dma_start(scale[:, :], s["mod"][seq:seq + 1, scale_at * D:(scale_at + 1) * D].to_broadcast([P, D])
                 ).then_inc(loaded, 16)


def projection(nc, a, s, keep):
    ident = keep["ident"]
    HALF = TILES // 2
    TRIPLES = HALF // 3
    RV, RQ, RK, MQ, MK, RG, MO, MV = range(8)
    COLUMN = {RQ: 0, RK: 1, RV: 2, RG: 3, MQ: 4, MK: 5, MV: 6, MO: 7}
    BLOCKS = range(8)
    ON_DVE = [RQ, RK, RG, MO]
    PIECES = 4
    PK = KT // PIECES
    with ExitStack() as ctx:
        m = Scope(nc, ctx, "proj")
        hT = m.sb("hT", [P, 2, HALF, KT, P], F32R)
        w = m.sb("w", [P, 2, 2, KT, BLK], F32R)
        raw = m.sb("raw", [P, 2, PK, BLK])
        wg16 = m.sb("wg16", [P, KT, 16])
        wg = m.sb("wg", [P, 2, KT, P], F32R)
        gbias = m.sb("gbias", [P, 1])
        x = m.sb("x", [P, 2, D])
        stage = m.sb("stage", [P, 3, BLK])
        pre = m.sb("pre", [P, 3, BLK])
        gnorm = m.sb("gnorm", [P, D])
        shift = m.sb("shift", [P, D])
        scale = m.sb("scale", [P, D])
        rope = m.sb("rope", [P, HALF, 2, HD // 2])
        turn = m.sb("turn", [P, 2, HEADS, HD // 2])
        ssq = m.sb("ssq", [P, 2])
        mean = m.sb("mean", [P, 2])
        rstd = m.sb("rstd", [P, 2])
        power = m.sb("power", [P, 1])
        acc = m.ps("acc", [P, 3, BLK])
        tps = m.ps("tps", [P, KT, P])
        gps = m.ps("gps", [P, BLK])
        junk = m.ps("junk", [P, D])

        wg_loaded, gb_loaded = m.sem("wg_loaded"), m.sem("gb_loaded")
        gb_zero, wg_zero, wg_hi, wg_ready = m.sem("gb_zero"), m.sem("wg_zero"), m.sem("wg_hi"), m.sem("wg_ready")
        first_loaded = [m.sem(f"first_loaded{i}") for i in range(2)]
        raw_loaded = [m.sem(f"raw_loaded{i}") for i in range(2)]
        w_hi, w_lo = m.sem("w_hi"), m.sem("w_lo")
        mod_loaded, gnorm_loaded, rope_loaded = m.sem("mod_loaded"), m.sem("gnorm_loaded"), m.sem("rope_loaded")
        scale_ready, power_ready = m.sem("scale_ready"), m.sem("power_ready")
        x_loaded = [m.sem(f"x_loaded{j}") for j in range(2)]
        ssq_ready, mean_ready, rstd_ready = m.sem("ssq_ready"), m.sem("mean_ready"), m.sem("rstd_ready")
        scaled, h_ready = m.sem("scaled"), m.sem("h_ready")
        transposed, hT_hi, hT_lo = m.sem("transposed"), m.sem("hT_hi"), m.sem("hT_lo")
        done, gate_done, grow_ready = m.sem("done"), m.sem("gate_done"), m.sem("grow_ready")
        acc_read, turned, part_done, gated = m.sem("acc_read"), m.sem("turned"), m.sem("part_done"), m.sem("gated")
        staged = m.sem("staged")
        stored = [m.sem(f"stored{i}") for i in range(3)]
        zero_stored = m.sem("zero_stored")
        w_in = a["w_in"][0].rearrange("(k p) n -> p k n", p=P)
        block = ctx.enter_context(nc.Block())

        def nth(half, b, t):
            return half * (len(BLOCKS) - 1) * HALF + HALF * b + t

        def nth_staged(half, b, t):
            return half * (len(ON_DVE) - 1) * HALF + HALF * ON_DVE.index(b) + t

        def slot_uses(half, b, triple):
            return half * (len(BLOCKS) - 1) * TRIPLES + TRIPLES * b + triple

        def over_triples(engine, half, body):
            if half == 0:
                for i in range(3):
                    body(i, i, 0)
            with engine.Fori(TRIPLES * half + (1 - half), TRIPLES * (half + 1)) as triple:
                for i in range(3):
                    body(3 * triple + i, i, triple)

        @block.sync
        def _(sp):
            def load_x(t):
                if t >= 2:
                    sp.wait_ge(transposed, t - 1)
                src = a["x_prompt"][0, t * P:(t + 1) * P, :] if t < CTX_TILES else \
                    a["x_sample"][0, (t - CTX_TILES) * P:(t - CTX_TILES + 1) * P, :]
                sp.dma_start(x[:, t % 2, :], src).then_inc(x_loaded[t % 2], 16)

            def load_mod(seq):
                if seq:
                    sp.wait_ge(h_ready, CTX_TILES)
                load_modulation(sp, s, a, shift, scale, 0, 1, seq, mod_loaded)

            def store(half, b, t, i):
                q = nth(half, b, t)
                if b in ON_DVE:
                    sp.wait_ge(staged, nth_staged(half, b, t) + 1)
                else:
                    sp.wait_ge(acc_read, q + 1)
                rows = bass.ts(t, P)
                if b in (RQ, RK, RV):
                    dst = s["qkv"][rows, COLUMN[b] * W:(COLUMN[b] + 1) * W]
                elif b == MV:
                    dst = s["qkv"][rows, 3 * W:4 * W]
                elif b in (RG, MO):
                    dst = s["gate"][rows, (b == MO) * W:((b == MO) + 1) * W]
                else:
                    context = isinstance(t, int) and t < CTX_TILES
                    dst = s["mqk"][bass.ds(t * P + (1 if context else 3), P), (b - MQ) * W:(b - MQ + 1) * W]
                sp.dma_start(dst, stage[:, i, :]).then_inc(stored[i], 16)

            def load_first_w(c):
                if c >= 2:
                    sp.wait_ge(w_lo, c - 1)
                col = COLUMN[RV] * BLK
                sp.dma_start(raw[:, c % 2, :, :], w_in[:, PK * c:PK * (c + 1), col:col + BLK]).then_inc(first_loaded[c % 2], 16)

            load_x(0)
            for c in range(2):
                load_first_w(c)
            load_mod(0)
            sp.dma_start(gnorm[:, :], a["norm1_g"].to_broadcast([P, D])).then_inc(gnorm_loaded, 16)
            load_x(1)
            for c in range(2, PIECES):
                load_first_w(c)
            sp.dma_start(wg16[:, :, :], w_in[:, :, len(BLOCKS) * BLK:len(BLOCKS) * BLK + 16]).then_inc(wg_loaded, 16)
            sp.dma_start(rope[:, CTX_TILES:HALF, :, :], a["rope"][0:(HALF - CTX_TILES) * P].rearrange("(t p) a e -> p t a e", p=P)
                         ).then_inc(rope_loaded, 16)
            sp.wait_ge(gb_zero, 2)
            for d in range(2):
                for f in range(2):
                    at = 64 * f + 32 * d
                    sp.dma_start(gbias[at:at + 4, :],
                                 a["mlstm_gate_bias"][0, d, f, :].rearrange("(h o) -> h o", o=1)).then_inc(gb_loaded, 16)
            zero = hT[0:4, 1, HALF - 1, :, :].bitcast(F32).rearrange("p k n -> p (k n)")
            sp.dma_start(s["mqk"][0:1, :], zero[0:1, :]).then_inc(zero_stored, 16)
            sp.dma_start(s["mqk"][CTX + 1:CTX + 3, :], zero[1:3, :]).then_inc(zero_stored, 16)
            sp.dma_start(s["mqk"][TOKENS + 3:TOKENS + 4, :], zero[3:4, :]).then_inc(zero_stored, 16)
            for half in range(2):
                for t in range(half * HALF, (half + 1) * HALF):
                    if t == CTX_TILES:
                        load_mod(1)
                    if t not in (0, 1, HALF, HALF + 1):
                        load_x(t)
                    if t - half * HALF >= 3:
                        store(half, RV, t - 3, t % 3)
                for t in range((half + 1) * HALF - 3, (half + 1) * HALF):
                    store(half, RV, t, t % 3)
                if half == 0:
                    sp.wait_ge(scale_ready, 2)
                    sp.dma_start(gnorm[:, 0:W], a["ret_gn_g"].to_broadcast([P, W])).then_inc(gnorm_loaded, 16)
                    sp.dma_start(gnorm[:, W:D], a["mlstm_gn_g"].to_broadcast([P, W])).then_inc(gnorm_loaded, 16)
                else:
                    sp.wait_ge(staged, nth_staged(0, RK, HALF - 1) + 1)
                    sp.dma_start(rope[:, :, :, :], a["rope"][(HALF - CTX_TILES) * P:].rearrange("(t p) a e -> p t a e", p=P)
                                 ).then_inc(rope_loaded, 16)
                for b in BLOCKS[1:]:
                    if half == 0 and b == BLOCKS[-1]:
                        load_x(HALF)
                        load_x(HALF + 1)
                    over_triples(sp, half, lambda t, i, triple: store(half, b, t, i))
            sp.wait_ge(zero_stored, 48)
            for i in range(3):
                sp.wait_ge(stored[i], 16 * TILES * len(BLOCKS) // 3)

        @block.scalar
        def _(act):
            def square(t):
                act.wait_ge(x_loaded[t % 2], 16 * (t // 2 + 1))
                if t:
                    act.wait_ge(ssq_ready, t)
                if t >= 2:
                    act.wait_ge(mean_ready, t - 1)
                act.activation(junk[:, :], x[:, t % 2, :], ACT.Square, accum_out=ssq[:, t % 2:t % 2 + 1]).then_inc(ssq_ready, 1)

            def evacuate(half, b, t, i, triple):
                q = nth(half, b, t)
                act.wait_ge(done, q + 1)
                if b in ON_DVE:
                    z = nth_staged(half, b, t)
                    if not (isinstance(z, int) and z < 3):
                        act.wait_ge(staged, z - 2)
                    if b == RG:
                        act.wait_ge(stored[i], 16 * slot_uses(half, b, triple))
                        act.activation(stage[:, i, :], acc[:, i, :], ACT.Copy)
                    f = ACT.Copy if b in (RQ, RK) else ACT.Sigmoid
                    act.activation(pre[:, i, :], acc[:, i, :], f, scale=KSCALE if b == RK else 1.0).then_inc(acc_read, 1)
                else:
                    act.wait_ge(stored[i], 16 * slot_uses(half, b, triple))
                    act.activation(stage[:, i, :], acc[:, i, :], ACT.Copy).then_inc(acc_read, 1)

            def gate_rows_out(half):
                act.wait_ge(gb_loaded, 64)
                for g in range(TRIPLES):
                    n = half * TRIPLES + g
                    act.wait_ge(gate_done, n + 1)
                    act.activation(keep["grows"][:, n * 3 * P:(n + 1) * 3 * P], gps[:, 0:3 * P], ACT.Identity,
                                   bias=gbias[:, 0:1]).then_inc(grow_ready, 1)

            for half in range(2):
                first, end = half * HALF, (half + 1) * HALF
                if half == 0:
                    square(first)
                    for c in range(PIECES):
                        act.wait_ge(first_loaded[c % 2], 16 * (c // 2 + 1))
                        act.activation(w[:, 0, 0, PK * c:PK * (c + 1), :], raw[:, c % 2, :, :], ACT.Copy).then_inc(w_hi, 1)
                for t in range(first, end):
                    if t + 1 < end:
                        square(t + 1)
                    act.wait_ge(transposed, t + 1)
                    if half:
                        act.wait_ge(done, nth(0, MV, t - HALF) + 1)
                    act.activation(hT[:, 0, t - first, :, :], tps[:, :, :], ACT.Copy).then_inc(hT_hi, 1)
                    if t > first:
                        evacuate(half, RV, t - 1, (t - 1) % 3, (t - 1) // 3)
                evacuate(half, RV, end - 1, (end - 1) % 3, (end - 1) // 3)
                for b in BLOCKS[1:]:
                    if half == 0 and b == BLOCKS[-1]:
                        square(HALF)
                    over_triples(act, half, lambda t, i, triple: evacuate(half, b, t, i, triple))
                    if b == RQ:
                        gate_rows_out(half)

        @block.tensor
        def _(pe):
            def transpose(t):
                pe.wait_ge(h_ready, t + 1)
                if t:
                    pe.wait_ge(hT_lo, t)
                for k in range(KT):
                    last = pe.transpose(tps[:, k, :], x[:, t % 2, k * P:(k + 1) * P], ident[:, :])
                last.then_inc(transposed, 1)

            def multiply(half, b, t, j):
                q = nth(half, b, t)
                if half or b is not RV or t >= 3:
                    pe.wait_ge(acc_read, q - 2)
                last = product(pe, acc[:, t % 3, :], KT, lambda part, k: hT[:, part, t % HALF, k, :],
                               lambda part, k: w[:, j, part, k, :])
                last.then_inc(done, 1)

            for half in range(2):
                tiles = range(half * HALF, (half + 1) * HALF)
                transpose(tiles[0])
                for t in tiles:
                    if t + 1 in tiles:
                        transpose(t + 1)
                    pe.wait_ge(hT_lo, t + 1)
                    if t == tiles[0]:
                        pe.wait_ge(w_lo, PIECES * (half * len(BLOCKS) + 1))
                    multiply(half, 0, t, 0)
                pe.wait_ge(w_lo, PIECES * (half * len(BLOCKS) + 2))
                for t in tiles:
                    multiply(half, 1, t, 1)
                pe.wait_ge(wg_ready, 1)
                for g in range(TRIPLES):
                    n = half * TRIPLES + g
                    if n:
                        pe.wait_ge(grow_ready, n)
                    last = product(pe, gps[:, 0:3 * P].rearrange("p (t c) -> p t c", t=3), KT, lambda part, k: wg[:, part, k, :],
                                   lambda part, k: hT[:, part, 3 * g:3 * g + 3, k, :])
                    last.then_inc(gate_done, 1)
                with pe.Fori(1, len(BLOCKS) // 2) as pair:
                    for j in range(2):
                        pe.wait_ge(w_lo, PIECES * (half * len(BLOCKS) + 2 * pair + j + 1))
                        for t in tiles:
                            multiply(half, 2 * pair + j, t, j)

        @block.vector
        def _(dve):
            dve.memset(wg[:, :, :, :].bitcast(F32), 0.0).then_inc(wg_zero, 1)
            dve.wait_ge(wg_zero, 1)
            dve.wait_ge(wg_loaded, 16)
            for d in range(2):
                for f in range(2):
                    at, src = 64 * f + 32 * d, wg16[:, :, 8 * d + 4 * f:8 * d + 4 * f + 4]
                    dve.tensor_copy(wg[:, 0, :, at:at + 4], src).then_inc(wg_hi, 1)
                    dve.wait_ge(wg_hi, 2 * d + f + 1)
                    last = dve.tensor_tensor(wg[:, 1, :, at:at + 4], src, wg[:, 0, :, at:at + 4].bitcast(F32), ALU.subtract)
            last.then_inc(wg_ready, 1)

            def normalise(t):
                j = t % 2
                seq = int(t >= CTX_TILES)
                if t in (0, CTX_TILES):
                    dve.wait_ge(mod_loaded, 32 * (seq + 1))
                    dve.wait_ge(gnorm_loaded, 16)
                    dve.scalar_tensor_tensor(out=scale[:, :], in0=scale[:, :], scalar=1.0, in1=gnorm[:, :],
                                             op0=ALU.add, op1=ALU.mult).then_inc(scale_ready, 1)
                    dve.wait_ge(scale_ready, seq + 1)
                dve.wait_ge(ssq_ready, t + 1)
                dve.tensor_scalar(mean[:, j:j + 1], ssq[:, j:j + 1], 1.0 / D, EPS, ALU.mult, ALU.add).then_inc(mean_ready, 1)
                dve.wait_ge(rstd_ready, t + 1)
                dve.scalar_tensor_tensor(out=x[:, j, :], in0=x[:, j, :], scalar=rstd[:, j:j + 1], in1=scale[:, :],
                                         op0=ALU.mult, op1=ALU.mult).then_inc(scaled, 1)
                dve.wait_ge(scaled, t + 1)
                dve.tensor_tensor(x[:, j, :], x[:, j, :], shift[:, :], ALU.add).then_inc(h_ready, 1)

            def finish(half, b, t, i, triple):
                q, z = nth(half, b, t), nth_staged(half, b, t)
                dve.wait_ge(acc_read, q + 1)
                if b != RG:
                    dve.wait_ge(stored[i], 16 * slot_uses(half, b, triple))
                if b in (RQ, RK) and isinstance(t, int) and t < CTX_TILES:
                    dve.tensor_copy(stage[:, i, :], pre[:, i, :]).then_inc(staged, 1)
                elif b in (RQ, RK):
                    v = pre[:, i, :].rearrange("p (h b e) -> p h b e", h=HEADS, b=2)
                    o = stage[:, i, :].rearrange("p (h b e) -> p h b e", h=HEADS, b=2)
                    row = rope[:, bass.ds(t - half * HALF, 1), :, :].rearrange("p o a e -> p (o a) e")
                    cos = row[:, 0:1, :].to_broadcast([P, HEADS, HD // 2])
                    sin = row[:, 1:2, :].to_broadcast([P, HEADS, HD // 2])
                    latents = HALF - CTX_TILES
                    r = (b == RK) * latents + (t - CTX_TILES) if half == 0 else 2 * latents + (b == RK) * HALF + (t - HALF)
                    dve.wait_ge(staged, z)
                    for side in range(2):
                        one, two = (cos, sin) if side == 0 else (sin, cos)
                        dve.tensor_tensor(turn[:, 0, :, :], v[:, :, 0, :], one, ALU.mult)
                        dve.tensor_tensor(turn[:, 1, :, :], v[:, :, 1, :], two, ALU.mult).then_inc(turned, 1)
                        dve.wait_ge(turned, r * 2 + side + 1)
                        last = dve.tensor_tensor(o[:, :, side, :], turn[:, 0, :, :], turn[:, 1, :, :],
                                                 ALU.subtract if side == 0 else ALU.add)
                        if side == 0:
                            last.then_inc(part_done, 1)
                            dve.wait_ge(part_done, r + 1)
                        else:
                            last.then_inc(staged, 1)
                elif b == RG:
                    dve.tensor_tensor(stage[:, i, :], stage[:, i, :], pre[:, i, :], ALU.mult).then_inc(gated, 1)
                    dve.wait_ge(gated, t + 1)
                    dve.tensor_tensor(stage[:, i, :], stage[:, i, :], gnorm[:, 0:W], ALU.mult).then_inc(staged, 1)
                else:
                    dve.tensor_tensor(stage[:, i, :], pre[:, i, :], gnorm[:, W:D], ALU.mult).then_inc(staged, 1)

            for half in range(2):
                first, end = half * HALF, (half + 1) * HALF
                if half == 0:
                    normalise(first)
                for t in range(first, end):
                    if t + 1 < end:
                        normalise(t + 1)
                    dve.wait_ge(hT_hi, t + 1)
                    if t == HALF - 1:
                        dve.wait_ge(zero_stored, 48)
                    dve.tensor_tensor(hT[:, 1, t - first, :, :], tps[:, :, :], hT[:, 0, t - first, :, :].bitcast(F32),
                                      ALU.subtract).then_inc(hT_lo, 1)
                dve.wait_ge(rope_loaded, 16 * (half + 1))
                for b in ON_DVE:
                    if half == 0 and b == RG:
                        dve.wait_ge(gnorm_loaded, 48)
                    over_triples(dve, half, lambda t, i, triple: finish(half, b, t, i, triple))
                if half == 0:
                    normalise(HALF)

        @block.gpsimd
        def _(pool):
            pool.memset(power[:, :], -0.5).then_inc(power_ready, 1)
            pool.memset(gbias[:, :], 0.0).then_inc(gb_zero, 1)
            pool.memset(hT[0:4, 1, HALF - 1, :, :].bitcast(F32), 0.0).then_inc(gb_zero, 1)
            pool.wait_ge(power_ready, 1)

            def weights(half, b, between=()):
                g = half * len(BLOCKS) + b
                if g >= 2:
                    pool.wait_ge(done, HALF * (g - 1))
                col = COLUMN[b] * BLK
                for c in range(PIECES):
                    n = PIECES * g + c
                    if n >= 2:
                        pool.wait_ge(w_lo, n - 1)
                    pool.dma_start(raw[:, c % 2, :, :], w_in[:, PK * c:PK * (c + 1), col:col + BLK]).then_inc(raw_loaded[c % 2], 16)
                    if c:
                        split(g, c - 1)
                    if c < len(between):
                        root(between[c])
                split(g, PIECES - 1)

            def split(g, c):
                n = PIECES * g + c
                k = slice(PK * c, PK * (c + 1))
                if g:
                    pool.wait_ge(raw_loaded[c % 2], 16 * ((n - PIECES) // 2 + 1))
                    pool.tensor_copy(w[:, g % 2, 0, k, :], raw[:, c % 2, :, :]).then_inc(w_hi, 1)
                pool.wait_ge(w_hi, n + 1)
                pool.tensor_tensor(w[:, g % 2, 1, k, :], raw[:, c % 2, :, :], w[:, g % 2, 0, k, :].bitcast(F32), ALU.subtract
                                   ).then_inc(w_lo, 1)

            def root(t):
                j = t % 2
                pool.wait_ge(mean_ready, t + 1)
                pool.tensor_tensor(rstd[:, j:j + 1], mean[:, j:j + 1], power[:, 0:1], ALU.pow).then_inc(rstd_ready, 1)

            for c in range(PIECES):
                split(0, c)
                if c % 2:
                    root(c // 2)
            for half in range(2):
                tiles = range(half * HALF, (half + 1) * HALF)
                between = tiles[2 - half:][:PIECES]
                weights(half, 1, between)
                for t in range(between[-1] + 1, tiles[-1] + 1):
                    root(t)
                for b in BLOCKS[2:]:
                    weights(half, b)
                if half == 0:
                    root(HALF)
                    weights(1, 0)


def gate_rows(nc, a, s, keep, out):
    DONE = 2 * D // BLK
    NB = MOD // BLK - DONE
    RING = 2
    G = 64
    grows = keep["grows"]
    with ExitStack() as ctx:
        m = Scope(nc, ctx, "gates")
        absf = m.sb("absf", [G, TOKENS])
        logf = m.sb("logf", [G, TILES, P])
        logi = m.sb("logi", [G, TILES, P])
        ping = m.sb("ping", [G, TILES, P])
        pong = m.sb("pong", [G, TILES, P])
        cum_b = m.sb("cum_b", [G, TILES, P])
        u = m.sb("u", [G, TILES, P])
        final = m.sb("final", [G, 4, TILES, P])
        ends = m.sb("ends", [G, 2, TILES])
        m_in = m.sb("m_in", [G, TILES + 1])
        m_ctx = m.sb("m_ctx", [G, 1])
        m_chunk = m.sb("m_chunk", [G, TILES])
        logit = m.sb("logit", [P, 8])
        decay_abs = m.sb("decay_abs", [P, 8])
        decay_min = m.sb("decay_min", [P, 8])
        shapes = m.sb("shapes", [P, 6, P])
        cols = m.sb("cols", [P, 2])
        tables = m.sb("tables", [P, 2, HEADS, P])
        w = m.sb("mod_w", [P, RING, KT, BLK])
        bias = m.sb("mod_bias", [2, RING, BLK])
        row = m.sb("mod_row", [2, 2, BLK])
        mod_row = m.sb("mod_sum", [2, 2, BLK])
        acc = m.ps("mod_acc", [P, 2, BLK])
        w_loaded = [m.sem(f"w_loaded{j}") for j in range(RING)]
        product_done, row_copied, row_ready = m.sem("product_done"), m.sem("row_copied"), m.sem("row_ready")
        row_stored = [m.sem(f"row_stored{j}") for j in range(2)]
        w_ada = a["w_ada"][0].rearrange("(p k) n -> p k n", k=KT)
        loaded, m_zero, m_loaded = m.sem("loaded"), m.sem("m_zero"), m.sem("m_loaded")
        act_step, dve_step = m.sem("act_step"), m.sem("dve_step")
        stored = m.sem("stored")
        block = ctx.enter_context(nc.Block())
        F0, B0 = slice(0, 32), slice(32, 64)
        DV_LG = 2
        DV_LOGF = 5
        DV_CUM = DV_LOGF + 2 * 7
        DV_U = DV_CUM + 2
        DV_MAX = DV_U + 2 * 7
        DV_MPREV = DV_MAX + 4 + TILES + 2
        DV_FINAL = DV_MPREV + 4

        def over_blocks(engine, body):
            for j in range(RING):
                body(j, 0, j)
            with engine.Fori(1, NB // RING) as ring:
                for j in range(RING):
                    body(RING * ring + j, ring, j)

        @block.sync
        def _(sp):
            sp.dma_start(logit[:, :], a["ret_decay_logit"].rearrange("o d h -> o (d h)").to_broadcast([P, 8])
                         ).then_inc(loaded, 16)
            sp.dma_start(shapes[:, :, :], a["shapes"]).then_inc(loaded, 16)
            sp.dma_start(cols[:, :], a["cols"]).then_inc(loaded, 16)
            sp.wait_ge(m_zero, 1)
            for d in range(2):
                sp.dma_start(m_in[32 * d:32 * d + 4, CTX_TILES:CTX_TILES + 1],
                             a["state_mlstm_m"][0, 0, d, :].rearrange("(h o) -> h o", o=1)).then_inc(m_loaded, 16)

            def load_w(n, ring, j):
                if not isinstance(ring, int):
                    sp.wait_ge(row_ready, n - RING + 1)
                sp.dma_start(w[:, j, :, :], w_ada[:, :, bass.ts(n + DONE, BLK)]).then_inc(w_loaded[j], 16)
                sp.dma_start(bias[:, j, :], a["b_ada"][0:1, bass.ts(n + DONE, BLK)].to_broadcast([2, BLK])
                             ).then_inc(w_loaded[j], 16)

            over_blocks(sp, load_w)
            for i, (kind, src) in enumerate(((U, ping), (EN, pong), (WE, cum_b), (MX, logi), (WI, logf))):
                sp.wait_ge(dve_step, DV_FINAL + 3 + i + 1)
                for d in range(2):
                    at = kind * ROWS + 4 * d
                    sp.dma_start(s["rows"][at:at + 4, :], src[32 * d:32 * d + 4, :, :].rearrange("p c t -> p (c t)")
                                 ).then_inc(stored, 16)
            for d in range(2):
                sp.dma_start(out["m"][0, 0, d, :].rearrange("(h o) -> h o", o=1), m_ctx[32 * d:32 * d + 4, :]
                             ).then_inc(stored, 16)
            sp.dma_start(s["mdec"].rearrange("c (h o) -> h c o", o=1), logf[32:36, :, 0:1], allow_slow_non_contiguous=True
                         ).then_inc(stored, 16)
            sp.wait_ge(stored, 13 * 16)

        @block.scalar
        def _(act):
            fr = grows[64:128, :]
            act.activation(absf[:, :], fr, ACT.Abs).then_inc(act_step, 1)
            act.wait_ge(loaded, 48)
            act.activation(decay_abs[:, :], logit[:, :], ACT.Abs).then_inc(act_step, 1)
            act.wait_ge(act_step, 2)
            act.activation(decay_abs[:, :], decay_abs[:, :], ACT.Exp, scale=-1.0).then_inc(act_step, 1)
            act.activation(absf[:, :], absf[:, :], ACT.Exp, scale=-1.0).then_inc(act_step, 1)
            act.wait_ge(act_step, 4)
            act.activation(decay_abs[:, :], decay_abs[:, :], ACT.Ln, bias=1.0).then_inc(act_step, 1)
            act.activation(absf[:, :], absf[:, :], ACT.Ln, bias=1.0).then_inc(act_step, 1)
            lg = decay_min
            act.wait_ge(dve_step, DV_LG)
            for d in range(2):
                for h in range(HEADS):
                    g = lg[:, 4 * d + h:4 * d + h + 1]
                    act.activation(tables[:, d, h, :], shapes[:, d, :], ACT.Exp, scale=g).then_inc(act_step, 1)
                    act.activation(keep["qdec"][:, d, h, :], shapes[:, 4 + d, :], ACT.Exp, scale=g).then_inc(act_step, 1)
                    act.activation(keep["kdec"][:, 4 * d + h:4 * d + h + 1], cols[:, d:d + 1], ACT.Exp, scale=g
                                   ).then_inc(act_step, 1)
            act.activation(keep["cdec"][:, :], lg[:, :], ACT.Exp, scale=float(P)).then_inc(act_step, 1)

            def copy_row(n, ring, j):
                act.wait_ge(product_done, n + 1)
                if reuses(n):
                    act.wait_ge(row_ready, n - 1)
                act.activation(row[:, j % 2, :], acc[0:2, j % 2, :], ACT.Copy).then_inc(row_copied, 1)

            over_blocks(act, copy_row)
            act.wait_ge(dve_step, DV_FINAL)
            act.activation(final[:, 3, :, :], final[:, 3, :, :], ACT.Exp).then_inc(act_step, 1)
            act.activation(final[:, 1, :, :], final[:, 1, :, :], ACT.Exp, scale=-1.0).then_inc(act_step, 1)
            act.activation(final[:, 2, :, :], final[:, 2, :, :], ACT.Exp).then_inc(act_step, 1)

        @block.tensor
        def _(pe):
            def multiply(n, ring, j):
                pe.wait_ge(w_loaded[j], 32 * (ring + 1))
                if reuses(n):
                    pe.wait_ge(row_copied, n - 1)
                for k in range(KT):
                    last = pe.matmul(acc[0:2, j % 2, :], keep["cond"][:, :, k], w[:, j, k, :], start=(k == 0), stop=(k == KT - 1))
                last.then_inc(product_done, 1)

            over_blocks(pe, multiply)

        @block.vector
        def _(dve):
            n = [0]

            def step(ins):
                ins.then_inc(dve_step, 1)
                n[0] += 1
                dve.wait_ge(dve_step, n[0])

            dve.wait_ge(act_step, 6)
            step(dve.tensor_scalar(decay_min[:, :], logit[:, :], 0.0, None, ALU.min))
            step(dve.tensor_tensor(decay_min[:, :], decay_min[:, :], decay_abs[:, :], ALU.subtract))
            assert n[0] == DV_LG
            fview = grows[64:128, :].rearrange("p (c t) -> p c t", t=P)
            iview = grows[0:64, :].rearrange("p (c t) -> p c t", t=P)
            lview = absf[:, :].rearrange("p (c t) -> p c t", t=P)
            step(dve.tensor_scalar(ping[:, :, :], fview, 0.0, None, ALU.min))
            step(dve.tensor_tensor(logf[F0, :, :], ping[F0, :, :], lview[F0, :, :], ALU.subtract))
            step(dve.tensor_tensor(logf[B0, :, ::-1], ping[B0, :, :], lview[B0, :, :], ALU.subtract))
            assert n[0] == DV_LOGF

            def scan(src, bufs, dst, op):
                cur = src
                for k in range(7):
                    reach = 1 << k
                    nxt = dst if k == 6 else bufs[k % 2]
                    step(dve.tensor_copy(nxt[:, :, 0:reach], cur[:, :, 0:reach]))
                    step(dve.tensor_tensor(nxt[:, :, reach:P], cur[:, :, reach:P], cur[:, :, 0:P - reach], op))
                    cur = nxt

            scan(logf, (ping, pong), cum_b, ALU.add)
            assert n[0] == DV_CUM
            dve.tensor_copy(logi[F0, :, :], iview[F0, :, :])
            step(dve.tensor_copy(logi[B0, :, ::-1], iview[B0, :, :]))
            step(dve.tensor_tensor(u[:, :, :], logi[:, :, :], cum_b[:, :, :], ALU.subtract))
            assert n[0] == DV_U
            top = final[:, 0, :, :]
            scan(u, (ping, pong), logf, ALU.max)
            assert n[0] == DV_MAX
            for e, src in enumerate((cum_b, logf)):
                step(dve.tensor_copy(ends[F0, e, :], src[F0, :, P - 1]))
                dve.tensor_copy(ends[B0, e, 0:CTX_TILES], src[B0, CTX_TILES - 1::-1, P - 1])
                step(dve.tensor_copy(ends[B0, e, CTX_TILES:TILES], src[B0, TILES - 1:CTX_TILES - 1:-1, P - 1]))
            dve.wait_ge(m_loaded, 32)
            for r in range(TILES):
                dst = m_ctx[:, 0:1] if r == CTX_TILES - 1 else m_in[:, r + 1:r + 2]
                step(dve.scalar_tensor_tensor(out=dst, in0=m_in[:, r:r + 1], scalar=ends[:, 1, r:r + 1],
                                              in1=ends[:, 0, r:r + 1], op0=ALU.max, op1=ALU.add))
            dve.tensor_copy(m_chunk[F0, :], m_in[F0, 0:TILES])
            step(dve.tensor_copy(m_chunk[B0, 0:CTX_TILES], m_in[B0, CTX_TILES - 1::-1]))
            step(dve.tensor_copy(m_chunk[B0, CTX_TILES:TILES], m_in[B0, TILES - 1:CTX_TILES - 1:-1]))
            assert n[0] == DV_MPREV
            mc = m_chunk[:, :].rearrange("p (c o) -> p c o", o=1).to_broadcast([G, TILES, P])
            step(dve.tensor_tensor(top, logf[:, :, :], mc, ALU.max))
            step(dve.tensor_tensor(final[:, 3, :, :], mc, top, ALU.subtract))
            step(dve.tensor_tensor(final[:, 1, :, :], cum_b[:, :, :], top, ALU.add))
            step(dve.tensor_tensor(final[:, 2, :, :], u[:, :, :], final[:, 0, :, P - 1:P].to_broadcast([G, TILES, P]),
                                   ALU.subtract))
            assert n[0] == DV_FINAL
            dve.wait_ge(act_step, 31)
            for d in range(2):
                step(dve.tensor_tensor(tables[:, d, :, :], tables[:, d, :, :],
                                       shapes[:, 2 + d:3 + d, :].to_broadcast([P, HEADS, P]), ALU.mult))
            step(dve.tensor_tensor(keep["mret"][:, :, :], tables[:, 0, :, :], tables[:, 1, :, :], ALU.add))
            dve.wait_ge(act_step, 34)
            for src, dst in ((u, ping), (final[:, 1, :, :], pong), (final[:, 2, :, :], cum_b),
                             (final[:, 0, :, :], logi), (final[:, 3, :, :], logf)):
                dve.tensor_copy(dst[F0, :, :], src[F0, :, :])
                step(dve.tensor_copy(dst[B0, :, ::-1], src[B0, :, :]))

        @block.gpsimd
        def _(pool):
            pool.memset(m_in[:, :], 0.0).then_inc(m_zero, 1)

            def add_bias(n, ring, j):
                pool.wait_ge(row_copied, n + 1)
                if reuses(n):
                    pool.wait_ge(row_stored[j % 2], 16 * ring)
                pool.tensor_tensor(mod_row[:, j % 2, :], row[:, j % 2, :], bias[:, j, :], ALU.add).then_inc(row_ready, 1)
                pool.wait_ge(row_ready, n + 1)
                pool.dma_start(s["mod"][:, bass.ts(n + DONE, BLK)], mod_row[:, j % 2, :]).then_inc(row_stored[j % 2], 16)

            over_blocks(pool, add_bias)
            for j in range(2):
                pool.wait_ge(row_stored[j], 16 * NB // 2)


def load_states(eng, a, state, d, loaded):
    eng.dma_start(state[:, 0:W].rearrange("p (h e) -> p h e", h=HEADS),
                  a["state_ret"][0, 0, d].rearrange("h p e -> p h e")).then_inc(loaded, 16)
    ml = state[:, W:STATE].rearrange("p (h e) -> p h e", h=HEADS)
    eng.dma_start(ml[:, :, 0:HD], a["state_mlstm_C"][0, 0, d].rearrange("h p e -> p h e")).then_inc(loaded, 16)
    eng.dma_start(ml[:, :, HD:AUG], a["state_mlstm_n"][0, 0, d].rearrange("h (p o) -> p h o", o=1),
                  allow_slow_non_contiguous=True).then_inc(loaded, 16)


def store_states(eng, out, state, d, stored):
    eng.dma_start(out["ret"][0, 0, d].rearrange("h p e -> p h e"),
                  state[:, 0:W].rearrange("p (h e) -> p h e", h=HEADS)).then_inc(stored, 16)
    ml = state[:, W:STATE].rearrange("p (h e) -> p h e", h=HEADS)
    eng.dma_start(out["C"][0, 0, d].rearrange("h p e -> p h e"), ml[:, :, 0:HD]).then_inc(stored, 16)
    eng.dma_start(out["n"][0, 0, d].rearrange("h (p o) -> p h o", o=1), ml[:, :, HD:AUG],
                  allow_slow_non_contiguous=True).then_inc(stored, 16)


def update_states(dve, old, new, kv_ret, kv_ml, cdec, mdec, done):
    for h in range(HEADS):
        dve.scalar_tensor_tensor(out=new[:, h * HD:(h + 1) * HD], in0=old[:, h * HD:(h + 1) * HD],
                                 scalar=cdec[:, h:h + 1], in1=kv_ret[:, h * HD:(h + 1) * HD], op0=ALU.mult, op1=ALU.add)
        at = slice(W + h * AUG, W + (h + 1) * AUG)
        last = dve.scalar_tensor_tensor(out=new[:, at], in0=old[:, at], scalar=mdec(h),
                                        in1=kv_ml(h), op0=ALU.mult, op1=ALU.add)
    last.then_inc(done, 1)


def backward_scan(nc, a, s, keep, out):
    ident = keep["ident"]
    with ExitStack() as ctx:
        m = Scope(nc, ctx, "bwd")
        convw = m.sb("convw", [P, 3, 2 * W])
        kv = m.sb("kv", [P, 2, 2, W])
        v1 = m.sb("v1", [P, 2, HEADS, AUG])
        xs = m.sb("xs", [P, 2, 3, 2 * W])
        conv_out = m.sb("conv_out", [P, 2, 2 * W])
        werow = m.sb("werow", [HEADS, 2, P])
        mdec = m.sb("mdec", [P, 2, HEADS])
        sig = m.sb("sig", [P, 2, 2 * W])
        qk = m.sb("qk", [P, 2, 2 * W])
        kret = m.sb("kret", [P, 2, W])
        kml = m.sb("kml", [P, 2, W])
        state = m.sb("state", [P, 2, STATE])
        kvr_ps = m.ps("kvr", [P, 2, BLK])
        kvm_ps = m.ps("kvm", [P, 4, BLK])
        we_ps = m.ps("we", [P, 2, BLK])
        conv_loaded, ones_ready = m.sem("conv_loaded"), m.sem("ones_ready")
        loaded = [m.sem(f"loaded{j}") for j in range(2)]
        mdec_loaded = [m.sem(f"mdec_loaded{j}") for j in range(2)]
        LOADS = 6
        side_taps, mid_tap, tap_sum, conv_sum = m.sem("side_taps"), m.sem("mid_tap"), m.sem("tap_sum"), m.sem("conv_sum")
        sig_ready, q_ready, k_ready = m.sem("sig_ready"), m.sem("q_ready"), m.sem("k_ready")
        kret_ready, we_ready, kml_ready = m.sem("kret_ready"), m.sem("we_ready"), m.sem("kml_ready")
        kv_done, updated = m.sem("kv_done"), m.sem("updated")
        zeroed, cached, ctx_stored = m.sem("zeroed"), m.sem("cached"), m.sem("ctx_stored")
        saved = [m.sem(f"saved{j}") for j in range(2)]
        qk_stored = [m.sem(f"qk_stored{j}") for j in range(2)]
        block = ctx.enter_context(nc.Block())

        def chunk(r, seq):
            return r * -1 + (TILES + CTX_TILES - 1 if seq else CTX_TILES - 1)

        def kvm(j, h):
            return kvm_ps[:, 2 * j + h // 2, (h % 2) * AUG:(h % 2 + 1) * AUG]

        @block.sync
        def _(sp):
            sp.dma_start(convw[:, :, :].rearrange("p j n -> p (j n)"),
                         a["conv_w"].rearrange("o j n -> o (j n)").to_broadcast([P, 6 * W])).then_inc(conv_loaded, 16)

            def load(r, pair, j):
                c = chunk(r, seq_of(r))
                if reuses(r):
                    sp.wait_ge(conv_sum, r - 1)
                for i in range(3):
                    sp.dma_start(xs[:, j, i, :], s["mqk"][bass.ds(c * P + 2 * seq_of(r) + i, P), :]).then_inc(loaded[j], 16)
                if reuses(r):
                    sp.wait_ge(kv_done, r - 1)
                sp.dma_start(kv[:, j, :, :].rearrange("p a n -> p (a n)"), s["qkv"][bass.ts(c, P), W:3 * W]
                             ).then_inc(loaded[j], 16)
                sp.dma_start(v1[:, j, :, 0:HD], s["qkv"][bass.ts(c, P), 3 * W:4 * W].rearrange("p (h e) -> p h e", h=HEADS)
                             ).then_inc(loaded[j], 16)
                sp.dma_start(werow[:, j, :], s["rows"][WE * ROWS + 4:WE * ROWS + 8, bass.ts(c, P)]).then_inc(loaded[j], 16)

            for r in range(CTX_TILES + 1):
                load(r, r // 2, r % 2)
            sp.wait_ge(updated, CTX_TILES)
            store_states(sp, out, state[:, 0, :], 1, ctx_stored)
            sp.wait_ge(ctx_stored, 48)
            sp.wait_ge(saved[0], 16)
            load_states(sp, a, state[:, 0, :], 1, cached)
            load(3, 1, 1)
            with sp.Fori(2, PAIRS) as pair:
                for j in range(2):
                    load(2 * pair + j, pair, j)

        @block.scalar
        def _(act):
            def silu(r, pair, j):
                act.wait_ge(conv_sum, r + 1)
                if reuses(r):
                    act.wait_ge(q_ready, r - 1)
                act.activation(sig[:, j, :], conv_out[:, j, :], ACT.Sigmoid).then_inc(sig_ready, 1)

            def load_decay(r, pair, j):
                if reuses(r):
                    act.wait_ge(updated, r - 1)
                act.dma_start(mdec[:, j, :], s["mdec"][bass.ds(chunk(r, seq_of(r)), 1), :].to_broadcast([P, HEADS])
                              ).then_inc(mdec_loaded[j], 16)

            over_steps(act, [(0, load_decay), (0, silu)])

        @block.tensor
        def _(pe):
            def accumulate(r, pair, j):
                pe.wait_ge(loaded[j], 16 * LOADS * (pair + 1))
                if reuses(r):
                    pe.wait_ge(updated, r - 1)
                pe.wait_ge(kret_ready, r + 1)
                for h in range(HEADS):
                    pe.matmul(kvr_ps[:, j, h * HD:(h + 1) * HD], kret[:, j, h * HD:(h + 1) * HD],
                              kv[:, j, 1, h * HD:(h + 1) * HD], start=True, stop=True)
                pe.transpose(we_ps[:, j, 0:HEADS], werow[:, j, :], ident[0:HEADS, 0:HEADS]).then_inc(we_ready, 1)
                pe.wait_ge(kml_ready, r + 1)
                pe.wait_ge(ones_ready, 1)
                for h in range(HEADS):
                    last = pe.matmul(kvm(j, h), kml[:, j, h * HD:(h + 1) * HD], v1[:, j, h, :], start=True, stop=True)
                last.then_inc(kv_done, 1)

            over_steps(pe, [(0, accumulate)])

        @block.vector
        def _(dve):
            dve.memset(state[:, 0, :], 0.0).then_inc(zeroed, 1)
            dve.wait_ge(zeroed, 1)
            dve.wait_ge(conv_loaded, 16)

            def conv(r, pair, j):
                dve.wait_ge(loaded[j], 16 * LOADS * (pair + 1))
                dve.tensor_tensor(xs[:, j, 1, :], xs[:, j, 1, :], convw[:, 1, :], ALU.mult).then_inc(mid_tap, 1)
                dve.wait_ge(mid_tap, r + 1)
                dve.wait_ge(side_taps, 2 * r + 1)
                dve.tensor_tensor(xs[:, j, 1, :], xs[:, j, 0, :], xs[:, j, 1, :], ALU.add).then_inc(tap_sum, 1)
                dve.wait_ge(tap_sum, r + 1)
                dve.wait_ge(side_taps, 2 * r + 2)
                if reuses(r):
                    dve.wait_ge(q_ready, r - 1)
                dve.tensor_tensor(conv_out[:, j, :], xs[:, j, 1, :], xs[:, j, 2, :], ALU.add).then_inc(conv_sum, 1)
                dve.wait_ge(sig_ready, r + 1)
                dve.wait_ge(conv_sum, r + 1)
                dve.wait_ge(qk_stored[j], 16 * pair)
                dve.scalar_tensor_tensor(out=qk[:, j, W:2 * W], in0=conv_out[:, j, W:2 * W], scalar=KSCALE,
                                         in1=sig[:, j, W:2 * W], op0=ALU.mult, op1=ALU.mult).then_inc(k_ready, 1)
                dve.wait_ge(we_ready, r + 1)
                dve.wait_ge(k_ready, r + 1)
                dve.tensor_tensor(kml[:, j, :].rearrange("p (h e) -> p h e", h=HEADS),
                                  qk[:, j, W:2 * W].rearrange("p (h e) -> p h e", h=HEADS),
                                  we_ps[:, j, 0:HEADS].rearrange("p (h o) -> p h o", o=1).to_broadcast([P, HEADS, HD]),
                                  ALU.mult).then_inc(kml_ready, 1)
                dve.tensor_tensor(qk[:, j, 0:W], conv_out[:, j, 0:W], sig[:, j, 0:W], ALU.mult).then_inc(q_ready, 1)

            def update(r, pair, j):
                dve.wait_ge(kv_done, r + 1)
                dve.wait_ge(mdec_loaded[j], 16 * (pair + 1))
                dve.wait_ge(updated, r)
                if reuses(r):
                    dve.wait_ge(cached, 48)
                if not isinstance(r, int) or r >= 1:
                    dve.wait_ge(saved[1 - j], 16 * (pair + j))
                update_states(dve, state[:, j, :], state[:, 1 - j, :], kvr_ps[:, j, :], lambda h: kvm(j, h),
                              keep["cdec"][:, 4:8], lambda h: mdec[:, j, h:h + 1], updated)

            over_steps(dve, [(0, conv), (1, update)])

        @block.gpsimd
        def _(pool):
            for j in range(2):
                last = pool.memset(v1[:, j, :, HD:AUG], 1.0)
            last.then_inc(ones_ready, 1)
            pool.wait_ge(conv_loaded, 16)

            def taps(r, pair, j):
                pool.wait_ge(loaded[j], 16 * LOADS * (pair + 1))
                pool.tensor_tensor(xs[:, j, 0, :], xs[:, j, 0, :], convw[:, 0, :], ALU.mult).then_inc(side_taps, 1)
                pool.tensor_tensor(xs[:, j, 2, :], xs[:, j, 2, :], convw[:, 2, :], ALU.mult).then_inc(side_taps, 1)
                pool.tensor_tensor(kret[:, j, :].rearrange("p (h e) -> p h e", h=HEADS),
                                   kv[:, j, 0, :].rearrange("p (h e) -> p h e", h=HEADS),
                                   keep["kdec"][:, 4:8].rearrange("p (h o) -> p h o", o=1).to_broadcast([P, HEADS, HD]),
                                   ALU.mult).then_inc(kret_ready, 1)

            def save(r, pair, j):
                seq = seq_of(r)
                pool.wait_ge(zeroed, 1)
                pool.wait_ge(updated, r)
                if seq:
                    pool.wait_ge(cached, 48)
                pool.dma_start(s["bst"][bass.ds(chunk(r, seq), 1), :, :].rearrange("c p n -> (c p) n"), state[:, j, :]
                               ).then_inc(saved[j], 16)
                pool.wait_ge(q_ready, r + 1)
                pool.wait_ge(conv_loaded, 16)
                pool.dma_start(s["mqk2"][bass.ts(chunk(r, seq), P), :], qk[:, j, :]).then_inc(qk_stored[j], 16)

            over_steps(pool, [(0, taps), (1, save)])
            for j in range(2):
                pool.wait_ge(saved[j], 16 * PAIRS)
                pool.wait_ge(qk_stored[j], 16 * PAIRS)


def forward_scan(nc, a, s, keep, out):
    ident = keep["ident"]
    with ExitStack() as ctx:
        m = Scope(nc, ctx, "fwd")
        far = m.sb("far", [P, 2, P])
        qkv = m.sb("qkv", [P, 2, 3, W])
        v1 = m.sb("v1", [P, 2, HEADS, AUG])
        qk = m.sb("qk", [P, 2, 2 * W])
        gate = m.sb("gate", [P, 2, D])
        rows = m.sb("rows", [3 * ROWS, 2, P])
        wide = m.sb("wide", [P, 2, 2, ROWS, P])
        bst = m.sb("bst", [P, 2, STATE])
        state = m.sb("state", [P, 2, STATE])
        qT = m.sb("qT", [P, 2, HEADS, P])
        kT = m.sb("kT", [P, 2, HEADS, P])
        qd = m.sb("qd", [P, 2, 2, HEADS, P])
        cols = m.sb("cols", [P, 3, ROWS])
        wts = m.sb("wts", [P, 2, HEADS, P])
        aret = m.sb("aret", [P, HEADS, P])
        aml = m.sb("aml", [P, 2, HEADS, P])
        kret = m.sb("kret", [P, W])
        kml = m.sb("kml", [P, W])
        den = m.sb("den", [P, 8])
        den2 = m.sb("den2", [P, 8])
        o = m.sb("o", [P, 2, 2 * HEADS, HD])
        hb = m.sb("hb", [P, HEADS, HD])
        mean = m.sb("mean", [P, 8])
        sums = m.sb("sums", [P, 2, 8])
        var = m.sb("var", [P, 8])
        rstd = m.sb("rstd", [P, 8])
        power = m.sb("power", [P, 8])
        y = m.sb("y", [P, 2, D])
        big = m.ps("big", [P, 4, BLK])
        sc = m.ps("sc", [P, 2, BLK])
        ret_ps = m.ps("ret", [P, BLK])
        misc = m.ps("misc", [P, BLK])
        COLS = slice(0, 3 * ROWS)
        KV3 = slice(3 * ROWS, 3 * ROWS + AUG)

        far_loaded, ones_ready = m.sem("far_loaded"), m.sem("ones_ready")
        loaded = [m.sem(f"loaded{j}") for j in range(2)]
        gate_loaded = [m.sem(f"gate_loaded{j}") for j in range(2)]
        LOADS = 7
        transposed, cols_T = m.sem("transposed"), m.sem("cols_T")
        cols_ready, plain_ready, decayed_ready = m.sem("cols_ready"), m.sem("plain_ready"), m.sem("decayed_ready")
        scores, masked, wts_ready = m.sem("scores"), m.sem("masked"), m.sem("wts_ready")
        aret_ready, aml_ready = m.sem("aret_ready"), m.sem("aml_ready")
        kret_ready, kml_ready = m.sem("kret_ready"), m.sem("kml_ready")
        ret_mixed = m.sem("ret_mixed")
        mixed, kv_done, updated = m.sem("mixed"), m.sem("kv_done"), m.sem("updated")
        oret_ready, den_step, h_part = m.sem("oret_ready"), m.sem("den_step"), m.sem("h_part")
        o_ready, mean_step, var_step, centred = (m.sem(n) for n in ("o_ready", "mean_step", "var_step", "centred"))
        squared, normed, y_ready = m.sem("squared"), m.sem("normed"), m.sem("y_ready")
        y_stored = [m.sem(f"y_stored{j}") for j in range(2)]
        zeroed, cached, ctx_stored = m.sem("zeroed"), m.sem("cached"), m.sem("ctx_stored")
        power_ready = m.sem("power_ready")
        block = ctx.enter_context(nc.Block())

        def retq(d, h):
            return qd[:, 0, d, h, :]

        def mlq(d, h):
            return qd[:, 1, d, h, :]

        def kvm(h):
            return sc[:, 1, h * AUG:(h + 1) * AUG] if h < 3 else misc[:, KV3]

        def num(d, h):
            return big[:, 2 * d + h // 2, (h % 2) * AUG:(h % 2 + 1) * AUG]

        def head_sum(d):
            return big[:, 2 * d:2 * d + 2, 0:2 * AUG].rearrange("p b (g e) -> p b g e", g=2)[:, :, :, 0:HD]

        @block.sync
        def _(sp):
            sp.dma_start(far[:, :, :], a["far"]).then_inc(far_loaded, 16)

            def load(pair, j, seq):
                c = 2 * pair + j
                if seq:
                    sp.wait_ge(updated, c - 1)
                r = bass.ts(c, P)
                inc = (loaded[j], 16)
                sp.dma_start(rows[:, j, :], s["rows"][0:3 * ROWS, r]).then_inc(*inc)
                sp.dma_start(qkv[:, j, :, :].rearrange("p a n -> p (a n)"), s["qkv"][r, 0:3 * W]).then_inc(*inc)
                sp.dma_start(qk[:, j, :], s["mqk2"][r, :]).then_inc(*inc)
                for kind in (MX, WI):
                    sp.dma_start(wide[:, j, kind - MX, :, :], s["rows"][kind * ROWS:(kind + 1) * ROWS, r]
                                 .rearrange("(o k) t -> o k t", o=1).to_broadcast([P, ROWS, P])).then_inc(*inc)
                sp.dma_start(v1[:, j, :, 0:HD], s["qkv"][r, 3 * W:4 * W].rearrange("p (h e) -> p h e", h=HEADS)).then_inc(*inc)
                sp.dma_start(bst[:, j, :], s["bst"][bass.ds(c, 1), :, :].rearrange("c p n -> (c p) n")).then_inc(*inc)

            for j in range(2):
                load(0, j, 0)
            sp.wait_ge(updated, CTX_TILES)
            store_states(sp, out, state[:, 0, :], 0, ctx_stored)
            sp.wait_ge(ctx_stored, 48)
            load_states(sp, a, state[:, 0, :], 0, cached)
            with sp.Fori(1, PAIRS) as pair:
                for j in range(2):
                    load(pair, j, 1)

        @block.scalar
        def _(act):
            def plain(c, pair, j):
                act.wait_ge(scores, 2 * c)
                for i in range(2):
                    act.wait_ge(transposed, 2 * c + i + 1)
                    act.activation(qT[:, i, :, :], big[:, 2 * i, :].rearrange("p (h t) -> p h t", h=HEADS), ACT.Copy)
                    act.activation(kT[:, i, :, :], big[:, 2 * i + 1, :].rearrange("p (h t) -> p h t", h=HEADS), ACT.Copy
                                   ).then_inc(plain_ready, 1)

            def weigh(c, pair, j):
                act.wait_ge(masked, c + 1)
                act.wait_ge(cols_ready, c + 1)
                act.wait_ge(aml_ready, c)
                for d in range(2):
                    for h in range(HEADS):
                        n = HEADS * d + h
                        last = act.activation(wts[:, d, h, :], wide[:, j, 0, n, :], ACT.Exp, bias=cols[:, U, n:n + 1], scale=-1.0)
                last.then_inc(wts_ready, 1)

            def square(c, pair, j):
                act.wait_ge(centred, c + 1)
                act.wait_ge(y_stored[j], 16 * pair)
                for h in range(2 * HEADS):
                    last = act.activation(y[:, j, h * HD:(h + 1) * HD], o[:, j, h, :], ACT.Square, accum_out=sums[:, j, h:h + 1])
                last.then_inc(squared, 1)

            def take_ret(c, pair, j):
                act.wait_ge(ret_mixed, c + 1)
                if reuses(c):
                    act.wait_ge(normed, c - 1)
                act.activation(o[:, j, 0:HEADS, :], ret_ps[:, :].rearrange("p (h e) -> p h e", h=HEADS), ACT.Copy
                               ).then_inc(oret_ready, 1)

            def load_gate(c, pair, j):
                if reuses(c):
                    act.wait_ge(y_ready, c - 1)
                act.dma_start(gate[:, j, :], s["gate"][bass.ts(c, P), :]).then_inc(gate_loaded[j], 16)

            over_steps(act, [(0, plain), (0, weigh), (1, load_gate), (1, square), (0, take_ret)])

        @block.tensor
        def _(pe):
            def chunk_step(c, pair, j):
                pe.wait_ge(loaded[j], 16 * LOADS * (pair + 1))
                pe.wait_ge(h_part, c)
                srcs = (qkv[:, j, 0, :], qkv[:, j, 1, :], qk[:, j, 0:W], qk[:, j, W:2 * W])
                for i, src in enumerate(srcs):
                    for h in range(HEADS):
                        last = pe.transpose(big[:, i, h * P:(h + 1) * P], src[:, h * HD:(h + 1) * HD], ident[:, :])
                    if i % 2:
                        last.then_inc(transposed, 1)
                pe.wait_ge(updated, c)
                for i in range(2):
                    pe.wait_ge(plain_ready, 2 * c + i + 1)
                    for h in range(HEADS):
                        last = pe.matmul(sc[:, i, h * P:(h + 1) * P], kT[:, i, h, :], qT[:, i, h, :], start=True, stop=True)
                        if i == 0 and h == 0:
                            pe.transpose(misc[:, COLS], rows[:, j, :], ident[0:3 * ROWS, 0:3 * ROWS]).then_inc(cols_T, 1)
                    last.then_inc(scores, 1)
                pe.wait_ge(aret_ready, c + 1)
                pe.wait_ge(decayed_ready, 2 * c + 1)
                if reuses(c):
                    pe.wait_ge(cached, 48)
                pe.wait_ge(oret_ready, c)
                for h in range(HEADS):
                    at = slice(h * HD, (h + 1) * HD)
                    pe.matmul(ret_ps[:, at], aret[:, h, :], qkv[:, j, 2, at], start=True, stop=False)
                    pe.matmul(ret_ps[:, at], retq(0, h), state[:, j, at], start=False, stop=False)
                    last = pe.matmul(ret_ps[:, at], retq(1, h), bst[:, j, at], start=False, stop=True)
                last.then_inc(ret_mixed, 1)
                pe.wait_ge(decayed_ready, 2 * c + 2)
                pe.wait_ge(aml_ready, c + 1)
                pe.wait_ge(ones_ready, 1)
                for d in range(2):
                    for h in range(HEADS):
                        at = slice(W + h * AUG, W + (h + 1) * AUG)
                        pe.matmul(num(d, h), aml[:, d, h, :], v1[:, j, h, :], start=True, stop=False)
                        last = pe.matmul(num(d, h), mlq(d, h), (state if d == 0 else bst)[:, j, at],
                                         start=False, stop=True)
                last.then_inc(mixed, 1)
                pe.wait_ge(kret_ready, c + 1)
                pe.wait_ge(kml_ready, c + 1)
                for h in range(HEADS):
                    at = slice(h * HD, (h + 1) * HD)
                    pe.matmul(sc[:, 0, at], kret[:, at], qkv[:, j, 2, at], start=True, stop=True)
                for h in range(HEADS):
                    last = pe.matmul(kvm(h), kml[:, h * HD:(h + 1) * HD], v1[:, j, h, :], start=True, stop=True)
                last.then_inc(kv_done, 1)

            over_steps(pe, [(0, chunk_step)])

        @block.vector
        def _(dve):
            dve.memset(state[:, 0, :], 0.0).then_inc(zeroed, 1)
            dve.wait_ge(zeroed, 1)

            def weigh(c, pair, j):
                dve.wait_ge(loaded[j], 16 * LOADS * (pair + 1))
                dve.wait_ge(cols_T, c + 1)
                dve.wait_ge(kml_ready, c)
                dve.wait_ge(wts_ready, c)
                dve.tensor_copy(cols[:, :, :].rearrange("p k r -> p (k r)"), misc[:, COLS]).then_inc(cols_ready, 1)
                dve.wait_ge(mixed, c)
                dve.wait_ge(plain_ready, 2 * c + 1)
                q = big[:, 0, :].rearrange("p (h t) -> p h t", h=HEADS)
                for d in range(2):
                    last = dve.tensor_tensor(qd[:, 0, d, :, :], q, keep["qdec"][:, d, :, :], ALU.mult)
                last.then_inc(decayed_ready, 1)
                dve.wait_ge(scores, 2 * c + 1)
                dve.tensor_tensor(aret[:, :, :], sc[:, 0, :].rearrange("p (h t) -> p h t", h=HEADS), keep["mret"][:, :, :],
                                  ALU.mult).then_inc(aret_ready, 1)
                dve.wait_ge(plain_ready, 2 * c + 2)
                q = big[:, 2, :].rearrange("p (h t) -> p h t", h=HEADS)
                for d in range(2):
                    last = dve.tensor_tensor(qd[:, 1, d, :, :], q, wide[:, j, 1, 4 * d:4 * d + 4, :], ALU.mult)
                last.then_inc(decayed_ready, 1)
                dve.wait_ge(scores, 2 * c + 2)
                dve.wait_ge(wts_ready, c + 1)
                for d in range(2):
                    last = dve.tensor_tensor(aml[:, d, :, :], sc[:, 1, :].rearrange("p (h t) -> p h t", h=HEADS),
                                             wts[:, d, :, :], ALU.mult)
                last.then_inc(aml_ready, 1)

            def combine(c, pair, j):
                dve.wait_ge(mixed, c + 1)
                dv = big[:, :, 0:2 * AUG].rearrange("p b (g e) -> p b g e", g=2)[:, :, :, HD]
                dve.tensor_copy(den[:, :].rearrange("p (b g) -> p b g", g=2), dv).then_inc(den_step, 1)
                dve.wait_ge(den_step, 4 * c + 1)
                dve.scalar_tensor_tensor(out=den2[:, :], in0=den[:, :], scalar=-1.0, in1=den[:, :], op0=ALU.mult, op1=ALU.max
                                         ).then_inc(den_step, 1)
                dve.wait_ge(den_step, 4 * c + 2)
                dve.tensor_tensor(den[:, :], den2[:, :], cols[:, EN, :], ALU.max).then_inc(den_step, 1)
                dve.wait_ge(den_step, 4 * c + 3)
                dve.reciprocal(den2[:, :], den[:, :]).then_inc(den_step, 1)
                dve.wait_ge(den_step, 4 * c + 4)
                dve.wait_ge(o_ready, c)
                if reuses(c):
                    dve.wait_ge(normed, c - 1)
                for d, dst in ((0, o[:, j, HEADS:2 * HEADS, :]), (1, hb[:, :, :])):
                    last = dve.tensor_tensor(dst.rearrange("p (b g) e -> p b g e", g=2), head_sum(d),
                                             den2[:, 4 * d:4 * d + 4].rearrange("p (b g o) -> p b g o", g=2, o=1)
                                             .to_broadcast([P, 2, 2, HD]), ALU.mult)
                last.then_inc(h_part, 1)

            def update(c, pair, j):
                dve.wait_ge(kv_done, c + 1)
                dve.wait_ge(updated, c)
                update_states(dve, state[:, j, :], state[:, 1 - j, :], sc[:, 0, :], kvm, keep["cdec"][:, 0:4],
                              lambda h: wide[:, j, 1, h, P - 1:P], updated)

            def centre(c, pair, j):
                dve.wait_ge(oret_ready, c + 1)
                dve.wait_ge(o_ready, c + 1)
                dve.tensor_reduce(mean[:, :], o[:, j, :, :], AX_X, ALU.add).then_inc(mean_step, 1)
                dve.wait_ge(mean_step, 2 * c + 1)
                dve.tensor_scalar(mean[:, :], mean[:, :], 1.0 / HD, None, ALU.mult).then_inc(mean_step, 1)
                dve.wait_ge(mean_step, 2 * c + 2)
                wide_mean = mean[:, :].rearrange("p (h o) -> p h o", o=1).to_broadcast([P, 2 * HEADS, HD])
                dve.tensor_tensor(o[:, j, :, :], o[:, j, :, :], wide_mean, ALU.subtract).then_inc(centred, 1)

            def variance(c, pair, j):
                dve.wait_ge(squared, c + 1)
                dve.wait_ge(var_step, 2 * c)
                dve.tensor_scalar(var[:, :], sums[:, j, :], 1.0 / HD, EPS, ALU.mult, ALU.add).then_inc(var_step, 1)

            def normalise(c, pair, j):
                dve.wait_ge(var_step, 2 * c + 2)
                wide_std = rstd[:, :].rearrange("p (h o) -> p h o", o=1).to_broadcast([P, 2 * HEADS, HD])
                dve.tensor_tensor(y[:, j, :].rearrange("p (h e) -> p h e", e=HD), o[:, j, :, :], wide_std, ALU.mult
                                  ).then_inc(normed, 1)

            over_steps(dve, [(1, update), (0, weigh), (2, variance), (1, centre), (2, normalise), (0, combine)])

        @block.gpsimd
        def _(pool):
            for j in range(2):
                last = pool.memset(v1[:, j, :, HD:AUG], 1.0)
            last.then_inc(ones_ready, 1)
            pool.memset(power[:, :], -0.5).then_inc(power_ready, 1)
            pool.wait_ge(power_ready, 1)
            pool.wait_ge(far_loaded, 16)

            def add(c, pair, j):
                pool.wait_ge(h_part, c + 1)
                pool.tensor_tensor(o[:, j, HEADS:2 * HEADS, :], o[:, j, HEADS:2 * HEADS, :], hb[:, :, :], ALU.add).then_inc(o_ready, 1)

            def mask(c, pair, j):
                pool.wait_ge(loaded[j], 16 * LOADS * (pair + 1))
                row = wide[:, j, 0, :, :].rearrange("p (d h) t -> p d h t", d=2)
                reach = far[:, :, :].rearrange("p d (o t) -> p d o t", o=1).to_broadcast([P, 2, HEADS, P])
                pool.tensor_tensor(row, row, reach, ALU.add).then_inc(masked, 1)

            def keys(c, pair, j):
                pool.wait_ge(loaded[j], 16 * LOADS * (pair + 1))
                pool.wait_ge(kv_done, c)
                pool.tensor_tensor(kret[:, :].rearrange("p (h e) -> p h e", h=HEADS),
                                   qkv[:, j, 1, :].rearrange("p (h e) -> p h e", h=HEADS),
                                   keep["kdec"][:, 0:4].rearrange("p (h o) -> p h o", o=1).to_broadcast([P, HEADS, HD]),
                                   ALU.mult).then_inc(kret_ready, 1)
                pool.wait_ge(cols_ready, c + 1)
                pool.tensor_tensor(kml[:, :].rearrange("p (h e) -> p h e", h=HEADS),
                                   qk[:, j, W:2 * W].rearrange("p (h e) -> p h e", h=HEADS),
                                   cols[:, WE, 0:4].rearrange("p (h o) -> p h o", o=1).to_broadcast([P, HEADS, HD]),
                                   ALU.mult).then_inc(kml_ready, 1)

            def finish(c, pair, j):
                pool.wait_ge(var_step, 2 * c + 1)
                pool.tensor_tensor(rstd[:, :], var[:, :], power[:, :], ALU.pow).then_inc(var_step, 1)
                pool.wait_ge(normed, c + 1)
                pool.wait_ge(gate_loaded[j], 16 * (pair + 1))
                pool.tensor_tensor(y[:, j, :], y[:, j, :], gate[:, j, :], ALU.mult).then_inc(y_ready, 1)
                pool.wait_ge(y_ready, c + 1)
                pool.dma_start(s["y"][bass.ts(c, P), :], y[:, j, :]).then_inc(y_stored[j], 16)

            over_steps(pool, [(0, mask), (1, add), (0, keys), (2, finish)])
            for j in range(2):
                pool.wait_ge(y_stored[j], 16 * PAIRS)


def output(nc, a, s, keep):
    ident = keep["ident"]
    with ExitStack() as ctx:
        m = Scope(nc, ctx, "out")
        w = m.sb("w", [P, 2, KT, D], F32R)
        raw = m.sb("raw", [P, 2, KT, BLK])
        y = m.sb("y", [P, 2, D])
        x = m.sb("x", [P, 2, D])
        yT = m.sb("yT", [P, 2, 2, KT, P], F32R)
        x1 = m.sb("x1", [P, 2, D])
        h = m.sb("h", [P, 2, D])
        hT = m.sb("hT", [P, 2, 2, KT, P], F32R)
        g1 = m.sb("g1", [P, 2, D])
        shift = m.sb("shift", [P, 2, D])
        scale = m.sb("scale", [P, 2, D])
        gain = m.sb("gain", [P, D])
        junk = m.sb("junk", [P, D])
        ssq = m.sb("ssq", [P, 2])
        rstd = m.sb("rstd", [P, 2])
        mean = m.sb("mean", [P, 2])
        power = m.sb("power", [P, 1])
        yT_ps = m.ps("yT_ps", [P, KT, P])
        hT_ps = m.ps("hT_ps", [P, KT, P])
        acc = m.ps("acc", [P, 2, 2, BLK])
        w_hi, w_lo, yT_lo, hT_lo = m.sem("w_hi"), m.sem("w_lo"), m.sem("yT_lo"), m.sem("hT_lo")
        mod_loaded, scale_ready = m.sem("mod_loaded"), m.sem("scale_ready")
        w_loaded = [m.sem(f"w_loaded{n}") for n in range(2)]
        y_loaded = [m.sem(f"y_loaded{j}") for j in range(2)]
        x_loaded = [m.sem(f"x_loaded{j}") for j in range(2)]
        y_T, yT_ready, product_done = m.sem("y_T"), m.sem("yT_ready"), m.sem("product_done")
        gated, x1_ready, ssq_ready = m.sem("gated"), m.sem("x1_ready"), m.sem("ssq_ready")
        rstd_step, scaled, h_ready = m.sem("rstd_step"), m.sem("scaled"), m.sem("h_ready")
        h_T, hT_ready = m.sem("h_T"), m.sem("hT_ready")
        x1_stored = [m.sem(f"x1_stored{j}") for j in range(2)]
        hT_stored = [m.sem(f"hT_stored{j}") for j in range(2)]
        power_ready = m.sem("power_ready")
        block = ctx.enter_context(nc.Block())

        @block.sync
        def _(sp):
            def load_y(t, pair, j):
                if reuses(t):
                    sp.wait_ge(y_T, t - 1)
                sp.dma_start(y[:, j, :], s["y"][bass.ts(t, P), :]).then_inc(y_loaded[j], 16)

            def load_x(t, pair, j):
                if reuses(t):
                    sp.wait_ge(x1_ready, t - 1)
                src = a["x_sample"][0, bass.ts(t - CTX_TILES, P), :] if seq_of(t) else a["x_prompt"][0, bass.ts(t, P), :]
                sp.dma_start(x[:, j, :], src).then_inc(x_loaded[j], 16)

            w_out = a["w_out"][0].rearrange("(k p) n -> p k n", p=P)
            for n in range(2):
                sp.dma_start(raw[:, n, :, :], w_out[:, :, n * BLK:(n + 1) * BLK]).then_inc(w_loaded[n], 16)
            over_steps(sp, [(0, load_y), (1, load_x)])

        @block.scalar
        def _(act):
            def split_y(t, pair, j):
                act.wait_ge(y_T, t + 1)
                if reuses(t):
                    act.wait_ge(product_done, t - 1)
                act.activation(yT[:, j, 0, :, :], yT_ps[:, :, :], ACT.Copy).then_inc(yT_ready, 1)

            def split_h(t, pair, j):
                act.wait_ge(h_T, t + 1)
                act.wait_ge(hT_stored[j], 32 * pair)
                act.activation(hT[:, j, 0, :, :], hT_ps[:, :, :], ACT.Copy).then_inc(hT_ready, 1)

            def square(t, pair, j):
                act.wait_ge(x1_ready, t + 1)
                act.wait_ge(ssq_ready, t)
                if reuses(t):
                    act.wait_ge(rstd_step, 2 * (t - 1))
                act.activation(junk[:, :], x1[:, j, :], ACT.Square, accum_out=ssq[:, j:j + 1]).then_inc(ssq_ready, 1)

            for seq in range(2):
                for dst, at in ((g1, 2), (shift, 3), (scale, 4)):
                    act.dma_start(dst[:, seq, :], s["mod"][seq:seq + 1, at * D:(at + 1) * D].to_broadcast([P, D])
                                  ).then_inc(mod_loaded, 16)
            act.dma_start(gain[:, :], a["norm2_g"].to_broadcast([P, D])).then_inc(mod_loaded, 16)
            for n in range(2):
                act.wait_ge(w_loaded[n], 16)
                act.activation(w[:, 0, :, n * BLK:(n + 1) * BLK], raw[:, n, :, :], ACT.Copy).then_inc(w_hi, 1)
            over_steps(act, [(0, split_y), (2, split_h), (1, square)])

        @block.tensor
        def _(pe):
            def transpose_y(t, pair, j):
                pe.wait_ge(y_loaded[j], 16 * (pair + 1))
                pe.wait_ge(yT_lo, t)
                for k in range(KT):
                    last = pe.transpose(yT_ps[:, k, :], y[:, j, k * P:(k + 1) * P], ident[:, :])
                last.then_inc(y_T, 1)

            def multiply(t, pair, j):
                pe.wait_ge(yT_lo, t + 1)
                if reuses(t):
                    pe.wait_ge(gated, t - 1)
                for n in range(2):
                    pe.wait_ge(w_lo, n + 1)
                    last = product(pe, acc[:, j, n, :], KT, lambda part, k: yT[:, j, part, k, :],
                                   lambda part, k: w[:, part, k, n * BLK:(n + 1) * BLK])
                last.then_inc(product_done, 1)

            def transpose_h(t, pair, j):
                pe.wait_ge(h_ready, t + 1)
                pe.wait_ge(hT_lo, t)
                for k in range(KT):
                    last = pe.transpose(hT_ps[:, k, :], h[:, j, k * P:(k + 1) * P], ident[:, :])
                last.then_inc(h_T, 1)

            over_steps(pe, [(0, transpose_y), (1, multiply), (2, transpose_h)])

        @block.vector
        def _(dve):
            for n in range(2):
                dve.wait_ge(w_hi, n + 1)
                at = slice(n * BLK, (n + 1) * BLK)
                dve.tensor_tensor(w[:, 1, :, at], raw[:, n, :, :], w[:, 0, :, at].bitcast(F32), ALU.subtract).then_inc(w_lo, 1)
            def gains():
                dve.wait_ge(mod_loaded, 7 * 16)
                for seq in range(2):
                    dve.scalar_tensor_tensor(out=scale[:, seq, :], in0=scale[:, seq, :], scalar=1.0, in1=gain[:, :],
                                             op0=ALU.add, op1=ALU.mult).then_inc(scale_ready, 1)
                dve.wait_ge(scale_ready, 2)

            def split_y(t, pair, j):
                dve.wait_ge(yT_ready, t + 1)
                dve.tensor_tensor(yT[:, j, 1, :, :], yT_ps[:, :, :], yT[:, j, 0, :, :].bitcast(F32), ALU.subtract
                                  ).then_inc(yT_lo, 1)

            def split_h(t, pair, j):
                dve.wait_ge(hT_ready, t + 1)
                dve.tensor_tensor(hT[:, j, 1, :, :], hT_ps[:, :, :], hT[:, j, 0, :, :].bitcast(F32), ALU.subtract
                                  ).then_inc(hT_lo, 1)

            def residual(t, pair, j):
                if isinstance(t, int) and t == 0:
                    gains()
                dve.wait_ge(product_done, t + 1)
                dve.wait_ge(x1_stored[j], 16 * pair)
                if reuses(t):
                    dve.wait_ge(h_ready, t - 1)
                dve.tensor_tensor(x1[:, j, :], acc[:, j, :, :].rearrange("p n c -> p (n c)"), g1[:, seq_of(t), :], ALU.mult
                                  ).then_inc(gated, 1)
                dve.wait_ge(gated, t + 1)
                dve.wait_ge(x_loaded[j], 16 * (pair + 1))
                dve.tensor_tensor(x1[:, j, :], x1[:, j, :], x[:, j, :], ALU.add).then_inc(x1_ready, 1)

            def normalise(t, pair, j):
                dve.wait_ge(ssq_ready, t + 1)
                dve.tensor_scalar(mean[:, j:j + 1], ssq[:, j:j + 1], 1.0 / D, EPS, ALU.mult, ALU.add).then_inc(rstd_step, 1)
                dve.wait_ge(rstd_step, 2 * t + 2)
                if reuses(t):
                    dve.wait_ge(h_T, t - 1)
                dve.scalar_tensor_tensor(out=h[:, j, :], in0=x1[:, j, :], scalar=rstd[:, j:j + 1], in1=scale[:, seq_of(t), :],
                                         op0=ALU.mult, op1=ALU.mult).then_inc(scaled, 1)
                dve.wait_ge(scaled, t + 1)
                dve.tensor_tensor(h[:, j, :], h[:, j, :], shift[:, seq_of(t), :], ALU.add).then_inc(h_ready, 1)

            over_steps(dve, [(0, split_y), (1, residual), (2, split_h), (1, normalise)])

        @block.gpsimd
        def _(pool):
            pool.memset(power[:, :], -0.5).then_inc(power_ready, 1)
            pool.wait_ge(power_ready, 1)

            def store_x1(t, pair, j):
                pool.wait_ge(x1_ready, t + 1)
                pool.dma_start(s["x1"][bass.ts(t, P), :], x1[:, j, :]).then_inc(x1_stored[j], 16)

            def store_h(t, pair, j):
                pool.wait_ge(hT_lo, t + 1)
                for part in range(2):
                    pool.dma_start(s["h2T"][:, part, :, bass.ts(t, P)], hT[:, j, part, :, :].bitcast(F32)).then_inc(hT_stored[j], 16)

            def root(t, pair, j):
                pool.wait_ge(rstd_step, 2 * t + 1)
                pool.tensor_tensor(rstd[:, j:j + 1], mean[:, j:j + 1], power[:, 0:1], ALU.pow).then_inc(rstd_step, 1)

            over_steps(pool, [(1, store_x1), (1, root), (2, store_h)])
            for j in range(2):
                pool.wait_ge(x1_stored[j], 16 * PAIRS)
                pool.wait_ge(hT_stored[j], 32 * PAIRS)


def mlp(nc, a, s, keep, out):
    HALF = TILES // 2
    HT = HALF * P
    BLOCKS = 3
    SIZE = HT // BLOCKS
    PB = SIZE // P
    CHUNK_PAIRS = FF_CHUNKS // 2
    X_RING = 3
    with ExitStack() as ctx:
        m = Scope(nc, ctx, "mlp")
        hT = m.sb("hT", [P, 2, KT, HT], F32R)
        total = m.sb("total", [P, HALF, D])
        raw1 = m.sb("raw1", [P, 2, KT, P])
        raw2 = m.sb("raw2", [P, 2, D])
        w1 = m.sb("w1", [P, 2, 2, KT, P], F32R)
        w2 = m.sb("w2", [P, 2, 2, D], F32R)
        rel = m.sb("rel", [P, 2, SIZE])
        sq = m.sb("sq", [P, 2, SIZE])
        fT = m.sb("fT", [P, 2, 2, HT], F32R)
        x1 = m.sb("x1", [P, X_RING, D])
        g2 = m.sb("g2", [P, 2, D])
        gain = m.sb("gain", [P, D])
        ssq = m.sb("ssq", [P, 2])
        mean = m.sb("mean", [P, 2])
        rstd = m.sb("rstd", [P, 2])
        power = m.sb("power", [P, 1])
        up = m.ps("up", [P, BLOCKS, BLK])
        down = m.ps("down", [P, 4, BLK])
        hT_loaded = [m.sem(f"hT_loaded{i}") for i in range(BLOCKS)]
        w_loaded = [m.sem(f"w_loaded{j}") for j in range(2)]
        w_hi, w_lo = m.sem("w_hi"), m.sem("w_lo")
        up_done, relu_done, sq_ready, f_hi, f_lo = (m.sem(n) for n in ("up_done", "relu_done", "sq_ready", "f_hi", "f_lo"))
        down_done, added = m.sem("down_done"), m.sem("added")
        g2_loaded, gain_loaded, power_ready = m.sem("g2_loaded"), m.sem("gain_loaded"), m.sem("power_ready")
        gated, pool_gated, x2_ready, ssq_ready = m.sem("gated"), m.sem("pool_gated"), m.sem("x2_ready"), m.sem("ssq_ready")
        mean_ready, rstd_ready, y_ready = m.sem("mean_ready"), m.sem("rstd_ready"), m.sem("y_ready")
        x1_loaded = [m.sem(f"x1_loaded{j}") for j in range(X_RING)]
        y_stored = [m.sem(f"y_stored{t}") for t in range(HALF)]
        w_ff1 = a["w_ff1"][0].rearrange("(k p) f -> p k f", p=P)
        w_ff2 = a["w_ff2"][0]
        block = ctx.enter_context(nc.Block())

        def down_bank(j, t, n):
            return (2 * HALF * j + 2 * t + n) % 4

        def over_chunks(engine, half, body):
            lead = half * CHUNK_PAIRS
            for j in range(2):
                body(lead, j, half)
            with engine.Fori(lead + 1, lead + CHUNK_PAIRS) as pair:
                for j in range(2):
                    body(pair, j, half)

        def load_h(engine, half, i):
            for part in range(2):
                engine.dma_start(hT[:, part, :, i * SIZE:(i + 1) * SIZE].bitcast(F32),
                                 s["h2T"][:, part, :, half * HT + i * SIZE:half * HT + (i + 1) * SIZE]
                                 ).then_inc(hT_loaded[i], 16)

        BY_POOL = HALF // 2 + 1

        @block.sync
        def _(sp):
            def load_w(pair, j, half):
                f = 2 * pair + j
                at = f - half * FF_CHUNKS
                if not (isinstance(pair, int) and pair == 0):
                    sp.wait_ge(w_lo, 2 * (f - 1))
                sp.dma_start(raw1[:, j, :, :], w_ff1[:, :, bass.ts(at, P)]).then_inc(w_loaded[j], 16)
                sp.dma_start(raw2[:, j, :], w_ff2[bass.ts(at, P), :]).then_inc(w_loaded[j], 16)

            def load_x1(t):
                if t >= X_RING:
                    sp.wait_ge(ssq_ready, t - X_RING + 1)
                sp.dma_start(x1[:, t % X_RING, :], s["x1"][t * P:(t + 1) * P, :]).then_inc(x1_loaded[t % X_RING], 16)

            for half in range(2):
                lead = half * CHUNK_PAIRS
                if half == 0:
                    load_w(lead, 0, half)
                    for i in range(BLOCKS):
                        load_h(sp, half, i)
                    load_w(lead, 1, half)
                    sp.dma_start(gain[:, :], a["final_g"].rearrange("(o n) -> o n", o=1).to_broadcast([P, D])).then_inc(gain_loaded, 16)
                    for seq in range(2):
                        sp.dma_start(g2[:, seq, :], s["mod"][seq:seq + 1, 5 * D:6 * D].to_broadcast([P, D])).then_inc(g2_loaded, 16)
                    for i in range(X_RING):
                        load_x1(i)
                with sp.Fori(lead + 1, lead + CHUNK_PAIRS) as pair:
                    for j in range(2):
                        load_w(pair, j, half)
                if half == 0:
                    for j in range(2):
                        load_w(lead + CHUNK_PAIRS, j, 1)
                first, end = half * HALF, (half + 1) * HALF
                for t in range(first, end):
                    if t + X_RING < TILES:
                        load_x1(t + X_RING)
                    sp.wait_ge(y_ready, t + 1)
                    dst = out["y_p"][0, t * P:(t + 1) * P, :] if t < CTX_TILES else \
                        out["y_s"][0, (t - CTX_TILES) * P:(t - CTX_TILES + 1) * P, :]
                    sp.dma_start(dst, total[:, t - first, :]).then_inc(y_stored[t - first], 16)
            for t in range(HALF):
                sp.wait_ge(y_stored[t], 32)

        @block.scalar
        def _(act):
            def activate(pair, j, half):
                f = 2 * pair + j
                act.wait_ge(w_loaded[j], 32 * (pair + 1))
                if not (isinstance(pair, int) and f < 2):
                    act.wait_ge(up_done, BLOCKS * (f - 1))
                act.activation(w1[:, j, 0, :, :], raw1[:, j, :, :], ACT.Copy).then_inc(w_hi, 1)
                if not (isinstance(pair, int) and f < 2):
                    act.wait_ge(down_done, 2 * HALF * (f - 1))
                act.activation(w2[:, j, 0, :], raw2[:, j, :], ACT.Copy).then_inc(w_hi, 1)
                for i in range(BLOCKS):
                    q = BLOCKS * f + i
                    b = (BLOCKS * j + i) % 2
                    ahead = not (isinstance(pair, int) and q < 2)
                    act.wait_ge(up_done, q + 1)
                    if ahead:
                        act.wait_ge(f_hi, q - 1)
                    act.activation(rel[:, b, :], up[:, i, 0:SIZE], ACT.Relu).then_inc(relu_done, 1)
                    if ahead:
                        act.wait_ge(f_lo, q - 1)
                    act.wait_ge(relu_done, q + 1)
                    act.activation(sq[:, b, :], rel[:, b, :], ACT.Square).then_inc(sq_ready, 1)
                    if i == 0 and not (isinstance(pair, int) and f < 2):
                        act.wait_ge(down_done, 2 * HALF * (f - 1))
                    act.activation(fT[:, j, 0, i * SIZE:(i + 1) * SIZE], rel[:, b, :], ACT.Square).then_inc(f_hi, 1)

            for half in range(2):
                over_chunks(act, half, activate)
                if half == 0:
                    act.wait_ge(up_done, BLOCKS * FF_CHUNKS)
                    for i in range(BLOCKS):
                        load_h(act, 1, i)
                for t in range(half * HALF, (half + 1) * HALF):
                    act.wait_ge(x2_ready, t + 1)
                    if t:
                        act.wait_ge(ssq_ready, t)
                    if t >= 2:
                        act.wait_ge(mean_ready, t - 1)
                    act.activation(x1[:, t % X_RING, :], total[:, t % HALF, :], ACT.Square, accum_out=ssq[:, t % 2:t % 2 + 1]
                                   ).then_inc(ssq_ready, 1)

        @block.tensor
        def _(pe):
            def multiply(pair, j, half):
                f = 2 * pair + j
                pe.wait_ge(w_lo, 2 * f + 1)
                for i in range(BLOCKS):
                    if isinstance(pair, int) and j == 0:
                        pe.wait_ge(hT_loaded[i], 32 * (half + 1))
                    if not (isinstance(pair, int) and f == 0):
                        pe.wait_ge(relu_done, BLOCKS * (f - 1) + i + 1)
                    last = product(pe, up[:, i, 0:SIZE], KT, lambda part, k: w1[:, j, part, k, :],
                                   lambda part, k: hT[:, part, k, i * SIZE:(i + 1) * SIZE])
                    last.then_inc(up_done, 1)
                pe.wait_ge(w_lo, 2 * f + 2)
                for t in range(HALF):
                    if t % PB == 0:
                        pe.wait_ge(f_lo, BLOCKS * f + t // PB + 1)
                    for n in range(2):
                        q = 2 * HALF * f + 2 * t + n
                        if not (isinstance(pair, int) and q < 4):
                            pe.wait_ge(added, q - 3)
                        last = product(pe, down[:, down_bank(j, t, n), :], 1, lambda part, k: fT[:, j, part, t * P:(t + 1) * P],
                                       lambda part, k: w2[:, j, part, n * BLK:(n + 1) * BLK])
                        last.then_inc(down_done, 1)

            for half in range(2):
                over_chunks(pe, half, multiply)

        @block.vector
        def _(dve):
            def add(pair, j, half):
                f = 2 * pair + j
                first = isinstance(pair, int) and pair == half * CHUNK_PAIRS and j == 0
                for i in range(BLOCKS):
                    q = BLOCKS * f + i
                    b = (BLOCKS * j + i) % 2
                    dve.wait_ge(f_hi, q + 1)
                    at = slice(i * SIZE, (i + 1) * SIZE)
                    dve.tensor_tensor(fT[:, j, 1, at], sq[:, b, :], fT[:, j, 0, at].bitcast(F32), ALU.subtract).then_inc(f_lo, 1)
                for t in range(HALF):
                    for n in range(2):
                        q = 2 * HALF * f + 2 * t + n
                        dst = total[:, t, n * BLK:(n + 1) * BLK]
                        dve.wait_ge(down_done, q + 1)
                        if first:
                            if half and n == 0:
                                dve.wait_ge(y_stored[t], 16)
                            dve.tensor_copy(dst, down[:, down_bank(j, t, n), :]).then_inc(added, 1)
                        else:
                            dve.wait_ge(added, q - 2 * HALF + 1)
                            dve.tensor_tensor(dst, dst, down[:, down_bank(j, t, n), :], ALU.add).then_inc(added, 1)

            def finish(t):
                row = total[:, t % HALF, :]
                half, i = t // HALF, t % HALF
                if i < BY_POOL:
                    dve.wait_ge(pool_gated, BY_POOL * half + i + 1)
                else:
                    dve.wait_ge(added, 2 * HALF * (FF_CHUNKS * (t // HALF + 1) - 1) + 2 * (t % HALF) + 2)
                    dve.tensor_tensor(row, row, g2[:, int(t >= CTX_TILES), :], ALU.mult).then_inc(gated, 1)
                    dve.wait_ge(gated, (HALF - BY_POOL) * half + i - BY_POOL + 1)
                dve.wait_ge(x1_loaded[t % X_RING], 16 * (t // X_RING + 1))
                dve.tensor_tensor(row, row, x1[:, t % X_RING, :], ALU.add).then_inc(x2_ready, 1)

            def average(t):
                j = t % 2
                dve.wait_ge(ssq_ready, t + 1)
                dve.tensor_scalar(mean[:, j:j + 1], ssq[:, j:j + 1], 1.0 / D, EPS, ALU.mult, ALU.add).then_inc(mean_ready, 1)

            def scale(t):
                row = total[:, t % HALF, :]
                dve.wait_ge(rstd_ready, t + 1)
                dve.wait_ge(x2_ready, t + 1)
                dve.scalar_tensor_tensor(out=row, in0=row, scalar=rstd[:, t % 2:t % 2 + 1], in1=gain[:, :],
                                         op0=ALU.mult, op1=ALU.mult).then_inc(y_ready, 1)

            for half in range(2):
                over_chunks(dve, half, add)
                dve.wait_ge(gain_loaded, 16)
                dve.wait_ge(g2_loaded, 32)
                first, end = half * HALF, (half + 1) * HALF
                finish(first)
                for t in range(first, end):
                    average(t)
                    if t + 1 < end:
                        finish(t + 1)
                    scale(t)

        @block.gpsimd
        def _(pool):
            def split_w(pair, j, half):
                f = 2 * pair + j
                for i, (raw, parts) in enumerate(((raw1[:, j, :, :].rearrange("p k n -> p (k n)"),
                                                   w1[:, j, :, :, :].rearrange("p c k n -> p c (k n)")),
                                                  (raw2[:, j, :], w2[:, j, :, :]))):
                    pool.wait_ge(w_hi, 2 * f + i + 1)
                    pool.tensor_tensor(parts[:, 1, :], raw, parts[:, 0, :].bitcast(F32), ALU.subtract).then_inc(w_lo, 1)

            pool.memset(power[:, :], -0.5).then_inc(power_ready, 1)
            pool.wait_ge(power_ready, 1)
            for half in range(2):
                over_chunks(pool, half, split_w)
                first, end = half * HALF, (half + 1) * HALF

                def gate(t):
                    row = total[:, t % HALF, :]
                    pool.wait_ge(added, 2 * HALF * (FF_CHUNKS * (half + 1) - 1) + 2 * (t - first) + 2)
                    pool.tensor_tensor(row, row, g2[:, int(t >= CTX_TILES), :], ALU.mult).then_inc(pool_gated, 1)

                pool.wait_ge(g2_loaded, 32)
                for t in range(first, first + BY_POOL):
                    gate(t)
                for t in range(first, end):
                    j = t % 2
                    pool.wait_ge(mean_ready, t + 1)
                    pool.tensor_tensor(rstd[:, j:j + 1], mean[:, j:j + 1], power[:, 0:1], ALU.pow).then_inc(rstd_ready, 1)


_INS = ["x_prompt", "x_sample", "state_ret", "state_mlstm_C", "state_mlstm_n", "state_mlstm_m", "c", "c_ctx", "w_ada",
        "b_ada", "norm1_g", "norm2_g", "w_in", "conv_w", "ret_decay_logit", "mlstm_gate_bias", "ret_gn_g", "mlstm_gn_g",
        "w_out", "w_ff1", "w_ff2", "final_g"]
_OUTS = [("y_p", (1, 256, 1024)), ("y_s", (1, 2048, 1024)), ("ret", (1, 1, 2, 4, 128, 128)), ("C", (1, 1, 2, 4, 128, 128)),
         ("n", (1, 1, 2, 4, 128)), ("m", (1, 1, 2, 4))]


def shape_constants():
    import numpy as np
    i = np.arange(128, dtype=np.float32)
    s, t = i[:, None], i[None, :]
    zero = np.zeros((128, 128), np.float32)
    shapes = np.stack([np.maximum(t - s, 0), np.maximum(s - t, 0), (t >= s).astype(np.float32),
                       (t <= s).astype(np.float32), zero + t + 1, zero + 128 - t], 1).astype(np.float32)
    far = np.stack([np.where(t >= s, 0, FAR), np.where(t <= s, 0, FAR)], 1).astype(np.float32)
    rows = np.arange(2048, dtype=np.float32) // 64
    grid_cols = np.arange(2048, dtype=np.float32) % 64
    inv = (10000.0 ** (-np.arange(32, dtype=np.float64) / 32)).astype(np.float32)
    ang = np.concatenate([rows[:, None] * inv, grid_cols[:, None] * inv], -1).astype(np.float64)
    rope = np.stack([np.cos(ang), np.sin(ang)], 1).astype(np.float32)
    return {"ident": np.eye(128, dtype=np.float32), "shapes": shapes, "far": far,
            "cols": np.stack([127 - i, i], 1).astype(np.float32), "rope": rope}


def kernel(**inputs):
    import numpy as np
    import concourse.bacc as bacc
    from concourse import mybir as mb
    from concourse.bass_utils import run_bass_kernel_spmd as run

    nc = bacc.Bacc("TRN2", target_bir_lowering=False, num_devices=1)
    arrays, args = {}, {}
    given = {name: np.ascontiguousarray(inputs[name]) for name in _INS}
    for name, value in {**given, **shape_constants()}.items():
        arrays[f"in_{name}"] = value
        args[name] = nc.dram_tensor(f"in_{name}", value.shape, mb.dt.from_np(value.dtype), kind="ExternalInput").ap()
    outs = {name: nc.dram_tensor(f"out_{name}", shape, mb.dt.float32, kind="ExternalOutput").ap() for name, shape in _OUTS}
    build(nc, args, outs)
    r = run(nc, [arrays], core_ids=[0])
    return tuple(r.results[0][f"out_{name}"] for name, _ in _OUTS)
```
